# Optimizing a Trainium2 kernel written in Bass

```python
import jax, jax.numpy as jnp
from jax import lax
import numpy as np
import math
import jax
import jax.numpy as jnp

D_MODEL = 1024
BATCH = 1
SEQ = 512
DEPTH = 1

MIX_A = D_MODEL // 2
MIX_B = D_MODEL - MIX_A
CHUNK = 128
A_GROUPS = 4
A_GROUP_DIM = MIX_A // A_GROUPS
B_HEAD_DIM = 64
B_HEADS = MIX_B // B_HEAD_DIM
LORA_W = 64
LORA_A = 64
LORA_G = 160
RWKV_COLS = 3 * MIX_B + LORA_W + LORA_A + LORA_G
IN_COLS = 2 * MIX_A + RWKV_COLS
FFN_HIDDEN = ((8 * D_MODEL + 3 * 256 - 1) // (3 * 256)) * 256
ALPHA = (2 * DEPTH) ** 0.25
BETA = (8 * DEPTH) ** -0.25
LN_EPS = 1e-5
GN_EPS = 64e-5


def layer_norm(x, g, b, eps=LN_EPS):
    xf = x.astype(jnp.float32)
    mu = jnp.mean(xf, axis=-1, keepdims=True)
    var = jnp.mean(jnp.square(xf - mu), axis=-1, keepdims=True)
    y = (xf - mu) * lax.rsqrt(var + eps)
    return (y * g.astype(jnp.float32) + b.astype(jnp.float32)).astype(x.dtype)

def token_shift(p):
    return jnp.pad(p, ((0, 0), (1, 0), (0, 0)))[:, :-1]

def gmlp_spatial_gating(pu, pv, ln_g, ln_b, w_s, b_s):
    B, S, _ = pu.shape
    nc = S // CHUNK
    u = jax.nn.gelu(pu)
    v = layer_norm(jax.nn.gelu(pv), ln_g, ln_b)
    vc = v.reshape(B, nc, CHUNK, A_GROUPS, A_GROUP_DIM)
    mask = jnp.tril(jnp.ones((CHUNK, CHUNK), dtype=w_s.dtype))
    s = jnp.einsum('gts,bnsgd->bntgd', w_s * mask, vc) + b_s.T[None, None, :, :, None]
    return u * s.reshape(B, S, MIX_A)

def _rwkv7_step(S, inp):
    r, w, k, v, a, b = inp
    sa = jnp.einsum('bhij,bhj->bhi', S, a)
    S = S * w[:, :, None, :] + sa[..., None] * b[:, :, None, :] + v[..., None] * k[:, :, None, :]
    y = jnp.einsum('bhij,bhj->bhi', S, r)
    return S, y

def rwkv7_time_mix(p, mu, w0, w_up, a0, a_up, g_up, k_k, k_a, r_k, lnx_g, lnx_b):
    B, S, _ = p.shape
    p = p + (token_shift(p) - p) * mu
    r, k, v = p[..., :MIX_B], p[..., MIX_B:2 * MIX_B], p[..., 2 * MIX_B:3 * MIX_B]
    o = 3 * MIX_B
    wd = p[..., o:o + LORA_W]
    ad = p[..., o + LORA_W:o + LORA_W + LORA_A]
    gd = p[..., o + LORA_W + LORA_A:]
    f32 = jnp.float32
    wlog = -jax.nn.softplus(-(w0 + jnp.tanh(wd) @ w_up).astype(f32)) - 0.5
    decay = jnp.exp(-jnp.exp(wlog))
    a = jax.nn.sigmoid((a0 + ad @ a_up).astype(f32))
    g = jax.nn.sigmoid(gd) @ g_up
    rf, kf, vf = r.astype(f32), k.astype(f32), v.astype(f32)
    heads = lambda t: t.reshape(B, S, B_HEADS, B_HEAD_DIM)
    kk = heads(kf * k_k.astype(f32))
    kk = kk / jnp.maximum(jnp.sqrt(jnp.sum(kk * kk, axis=-1, keepdims=True)), 1e-12)
    kf = kf * (1.0 + (a - 1.0) * k_a.astype(f32))
    rh, kh, vh, wh, ah = heads(rf), heads(kf), heads(vf), heads(decay), heads(a)
    xs = tuple(jnp.swapaxes(t, 0, 1) for t in (rh, wh, kh, vh, -kk, kk * ah))
    S0 = jnp.zeros((B, B_HEADS, B_HEAD_DIM, B_HEAD_DIM), f32)
    _, y = lax.scan(_rwkv7_step, S0, xs)
    y = jnp.swapaxes(y, 0, 1)
    mu_y = jnp.mean(y, axis=-1, keepdims=True)
    var_y = jnp.mean(jnp.square(y - mu_y), axis=-1, keepdims=True)
    y = ((y - mu_y) * lax.rsqrt(var_y + GN_EPS)).reshape(B, S, MIX_B)
    y = y * lnx_g.astype(f32) + lnx_b.astype(f32)
    bonus = jnp.sum(rh * kh * r_k.astype(f32), axis=-1, keepdims=True) * vh
    y = y + bonus.reshape(B, S, MIX_B)
    return (y * g.astype(f32)).astype(p.dtype)

def first_inputs(seed: int = 0) -> dict:
    key = jax.random.key(seed)
    ks = jax.random.split(key, 32)
    L, D = DEPTH, D_MODEL
    f32 = jnp.float32
    nrm = lambda k, shape, s: jax.random.normal(k, shape, f32) * s
    return {
        "x": nrm(ks[0], (BATCH, SEQ, D), 1.0),
        "c": nrm(ks[1], (BATCH, D), 1.0),
        "emb_ln_g": 1.0 + nrm(ks[2], (D,), 0.05),
        "emb_ln_b": nrm(ks[3], (D,), 0.02),
        "w_ada": nrm(ks[4], (L, D, 6 * D), 0.5 * D ** -0.5),
        "b_ada": nrm(ks[5], (L, 6 * D), 0.02),
        "w_in": nrm(ks[6], (L, D, IN_COLS), D ** -0.5),
        "mu_shift": jax.random.uniform(ks[7], (L, RWKV_COLS), f32),
        "sg_ln_g": 1.0 + nrm(ks[8], (L, MIX_A), 0.05),
        "sg_ln_b": nrm(ks[9], (L, MIX_A), 0.02),
        "w_s": nrm(ks[10], (L, A_GROUPS, CHUNK, CHUNK), CHUNK ** -0.5),
        "b_s": 1.0 + nrm(ks[11], (L, A_GROUPS, CHUNK), 0.1),
        "w0": jax.random.uniform(ks[12], (L, MIX_B), f32, -6.0, 1.0),
        "w_up": nrm(ks[13], (L, LORA_W, MIX_B), LORA_W ** -0.5),
        "a0": nrm(ks[14], (L, MIX_B), 0.1),
        "a_up": nrm(ks[15], (L, LORA_A, MIX_B), LORA_A ** -0.5),
        "g_up": nrm(ks[16], (L, LORA_G, MIX_B), LORA_G ** -0.5),
        "k_k": 0.85 + nrm(ks[17], (L, MIX_B), 0.05),
        "k_a": 1.0 + nrm(ks[18], (L, MIX_B), 0.05),
        "r_k": nrm(ks[19], (L, B_HEADS, B_HEAD_DIM), 0.1),
        "lnx_g": 1.0 + nrm(ks[20], (L, MIX_B), 0.05),
        "lnx_b": nrm(ks[21], (L, MIX_B), 0.02),
        "w_out": nrm(ks[22], (L, D, D), BETA * D ** -0.5),
        "ln1_g": 1.0 + nrm(ks[23], (L, D), 0.05),
        "ln1_b": nrm(ks[24], (L, D), 0.02),
        "w_ffn_in": nrm(ks[25], (L, D, 2 * FFN_HIDDEN), D ** -0.5),
        "w_ffn_out": nrm(ks[26], (L, FFN_HIDDEN, D), BETA * FFN_HIDDEN ** -0.5),
        "ln2_g": 1.0 + nrm(ks[27], (L, D), 0.05),
        "ln2_b": nrm(ks[28], (L, D), 0.02),
    }

def first_block(x, c, emb_ln_g, emb_ln_b, w_ada, b_ada, w_in, mu_shift, sg_ln_g, sg_ln_b, w_s, b_s,
              w0, w_up, a0, a_up, g_up, k_k, k_a, r_k, lnx_g, lnx_b, w_out, ln1_g, ln1_b,
              w_ffn_in, w_ffn_out, ln2_g, ln2_b):
    x = layer_norm(x, emb_ln_g, emb_ln_b)
    cs = jax.nn.silu(c)
    for l in range(DEPTH):
        mod = cs @ w_ada[l] + b_ada[l]
        sh1, sc1, gt1, sh2, sc2, gt2 = [m[:, None, :] for m in jnp.split(mod, 6, axis=-1)]
        h = x * (1.0 + sc1) + sh1
        p = h @ w_in[l]
        y_a = gmlp_spatial_gating(p[..., :MIX_A], p[..., MIX_A:2 * MIX_A],
                                  sg_ln_g[l], sg_ln_b[l], w_s[l], b_s[l])
        y_b = rwkv7_time_mix(p[..., 2 * MIX_A:], mu_shift[l], w0[l], w_up[l], a0[l], a_up[l],
                             g_up[l], k_k[l], k_a[l], r_k[l], lnx_g[l], lnx_b[l])
        mix = jnp.concatenate([y_a, y_b], axis=-1) @ w_out[l]
        x = layer_norm(ALPHA * x + gt1 * mix, ln1_g[l], ln1_b[l])
        h = x * (1.0 + sc2) + sh2
        gu = h @ w_ffn_in[l]
        f = (jax.nn.silu(gu[..., :FFN_HIDDEN]) * gu[..., FFN_HIDDEN:]) @ w_ffn_out[l]
        x = layer_norm(ALPHA * x + gt2 * f, ln2_g[l], ln2_b[l])
    return x


D_MIX = D_MODEL
D_NSA = D_MIX // 2
D_CONV = D_MIX - D_NSA
HEAD_DIM = 64
N_HEADS = D_NSA // HEAD_DIM
N_KV = 2
REP = N_HEADS // N_KV
KV_W = N_KV * HEAD_DIM
N_GATES = 3 * N_HEADS
D_IN = D_NSA + 6 * KV_W + N_GATES + 3 * D_CONV
L_CMP = 32
S_CMP = 16
L_SLC = 64
N_SEL = 16
WINDOW = 512
Q_BLOCK = 128
CMP_HIDDEN = 256
CONV_W = 3
D_FF = 2816
N_BUCKETS = 32
MAX_DIST = 128
RMS_EPS = 1e-6
NEG = -1e30
FORCE_BONUS = 1e4


def rms_norm(x, g):
    xf = x.astype(jnp.float32)
    y = xf * lax.rsqrt(jnp.mean(xf * xf, axis=-1, keepdims=True) + RMS_EPS)
    return (y * g.astype(jnp.float32)).astype(x.dtype)

def causal_dwconv(x, w):
    return lax.conv_general_dilated(
        x, w[:, None, :].astype(x.dtype), window_strides=(1,),
        padding=[(CONV_W - 1, 0)], dimension_numbers=('NWC', 'WIO', 'NWC'),
        feature_group_count=x.shape[-1])

def t5_bucket(dist):
    max_exact = N_BUCKETS // 2
    d = jnp.maximum(dist, 0)
    df = jnp.maximum(d, 1).astype(jnp.float32)
    large = max_exact + (jnp.log(df / max_exact) / math.log(MAX_DIST / max_exact)
                         * (N_BUCKETS - max_exact)).astype(jnp.int32)
    return jnp.where(d < max_exact, d, jnp.minimum(large, N_BUCKETS - 1))

def masked_softmax(logits, mask):
    z = jnp.where(mask, logits.astype(jnp.float32), NEG)
    p = jax.nn.softmax(z, axis=-1)
    return p * jnp.any(mask, axis=-1, keepdims=True)

def compress_kv(kv, pe, w1, w2):
    B, S, G, dh = kv.shape
    n_cmp = (S - L_CMP) // S_CMP + 1
    idx = jnp.arange(n_cmp)[:, None] * S_CMP + jnp.arange(L_CMP)[None, :]
    blk = kv[:, idx] + pe[None, None, :, None, :]
    blk = blk.transpose(0, 3, 1, 2, 4).reshape(B, G, n_cmp, L_CMP * dh)
    return jax.nn.gelu(blk @ w1, approximate=True) @ w2

def nsa_attention(q, k_c, v_c, k_s, v_s, k_w, v_w, gate_logits,
                  pe_k, pe_v, wk1, wk2, wv1, wv2, rel_bias):
    B, S = q.shape[0], q.shape[1]
    n_cmp = (S - L_CMP) // S_CMP + 1
    n_slc = S // L_SLC
    n_sel = min(N_SEL, n_slc)
    nqb = S // Q_BLOCK
    scale = HEAD_DIM ** -0.5
    t = jnp.arange(S)
    tab = rel_bias.reshape(N_KV, REP, N_BUCKETS)
    qg = q.reshape(B, S, N_KV, REP, HEAD_DIM).transpose(0, 2, 3, 1, 4)

    kc = compress_kv(k_c, pe_k, wk1, wk2)
    vc = compress_kv(v_c, pe_v, wv1, wv2)
    c_start = jnp.arange(n_cmp) * S_CMP
    dist_c = t[:, None] - (c_start + L_CMP - 1)[None, :]
    logits_c = (jnp.einsum('bgrsd,bgnd->bgrsn', qg, kc) * scale
                + tab[:, :, t5_bucket(dist_c)])
    p_c = masked_softmax(logits_c, dist_c >= 0)
    o_c = jnp.einsum('bgrsn,bgnd->bgrsd', p_c.astype(vc.dtype), vc)

    s_start = jnp.arange(n_slc) * L_SLC
    overlap = jnp.clip(jnp.minimum(c_start[:, None] + L_CMP, s_start[None, :] + L_SLC)
                       - jnp.maximum(c_start[:, None], s_start[None, :]), 0, None)
    overlap = overlap.astype(jnp.float32) / L_CMP
    imp = jnp.einsum('bgrsn,nj->bgsj', p_c, overlap)
    j = jnp.arange(n_slc)[None, :]
    cur = (t // L_SLC)[:, None]
    forced = (j == 0) | (j == cur) | (j == cur - 1)
    score = jnp.where(j <= cur, imp + jnp.where(forced, FORCE_BONUS, 0.0), NEG)
    top_val, top_idx = lax.top_k(score, n_sel)
    top_ok = top_val > 0.5 * NEG

    k_sb = k_s.reshape(B, n_slc, L_SLC, N_KV, HEAD_DIM).transpose(0, 3, 1, 2, 4)
    v_sb = v_s.reshape(B, n_slc, L_SLC, N_KV, HEAD_DIM).transpose(0, 3, 1, 2, 4)
    k_wp = jnp.pad(k_w, ((0, 0), (WINDOW, 0), (0, 0), (0, 0)))
    v_wp = jnp.pad(v_w, ((0, 0), (WINDOW, 0), (0, 0), (0, 0)))
    bi = jnp.arange(B)[:, None, None, None]
    gi = jnp.arange(N_KV)[None, :, None, None]

    def block_fn(args):
        n, q_b, idx_b, ok_b = args
        t_b = n * Q_BLOCK + jnp.arange(Q_BLOCK)
        ks = k_sb[bi, gi, idx_b].reshape(B, N_KV, Q_BLOCK, n_sel * L_SLC, HEAD_DIM)
        vs = v_sb[bi, gi, idx_b].reshape(B, N_KV, Q_BLOCK, n_sel * L_SLC, HEAD_DIM)
        pos = (idx_b[..., None] * L_SLC + jnp.arange(L_SLC)).reshape(
            B, N_KV, Q_BLOCK, n_sel * L_SLC)
        dist_s = t_b[None, None, :, None] - pos
        m_s = (dist_s >= 0) & jnp.repeat(ok_b, L_SLC, axis=-1)
        bias_s = jnp.moveaxis(tab[gi, :, t5_bucket(dist_s)], -1, 2)
        logits_s = jnp.einsum('bgrqd,bgqkd->bgrqk', q_b, ks) * scale + bias_s
        p_s = masked_softmax(logits_s, m_s[:, :, None])
        o_s = jnp.einsum('bgrqk,bgqkd->bgrqd', p_s.astype(vs.dtype), vs)
        kw = lax.dynamic_slice_in_dim(k_wp, n * Q_BLOCK, Q_BLOCK + WINDOW, axis=1)
        vw = lax.dynamic_slice_in_dim(v_wp, n * Q_BLOCK, Q_BLOCK + WINDOW, axis=1)
        s_w = n * Q_BLOCK - WINDOW + jnp.arange(Q_BLOCK + WINDOW)
        dist_w = t_b[:, None] - s_w[None, :]
        m_w = (dist_w >= 0) & (dist_w < WINDOW) & (s_w[None, :] >= 0)
        logits_w = (jnp.einsum('bgrqd,bkgd->bgrqk', q_b, kw) * scale
                    + tab[:, :, t5_bucket(dist_w)])
        p_w = masked_softmax(logits_w, m_w)
        o_w = jnp.einsum('bgrqk,bkgd->bgrqd', p_w.astype(vw.dtype), vw)
        return o_s, o_w

    q_blocks = jnp.moveaxis(qg.reshape(B, N_KV, REP, nqb, Q_BLOCK, HEAD_DIM), 3, 0)
    idx_blocks = jnp.moveaxis(top_idx.reshape(B, N_KV, nqb, Q_BLOCK, n_sel), 2, 0)
    ok_blocks = jnp.moveaxis(top_ok.reshape(B, N_KV, nqb, Q_BLOCK, n_sel), 2, 0)
    o_s, o_w = lax.map(block_fn, (jnp.arange(nqb), q_blocks, idx_blocks, ok_blocks))
    o_s = jnp.moveaxis(o_s, 0, 3).reshape(B, N_KV, REP, S, HEAD_DIM)
    o_w = jnp.moveaxis(o_w, 0, 3).reshape(B, N_KV, REP, S, HEAD_DIM)

    g = jax.nn.sigmoid(gate_logits.astype(jnp.float32)).reshape(B, S, N_KV, REP, 3)
    g = g.transpose(0, 2, 3, 1, 4).astype(q.dtype)
    o = g[..., 0:1] * o_c + g[..., 1:2] * o_s + g[..., 2:3] * o_w
    return o.transpose(0, 3, 1, 2, 4).reshape(B, S, D_NSA)

def short_conv_mixer(b_gate, c_gate, x_t, conv_w):
    return b_gate * causal_dwconv(c_gate * x_t, conv_w)

def split_points():
    sizes = [D_NSA] + [KV_W] * 6 + [N_GATES, D_CONV, D_CONV]
    pts, acc = [], 0
    for s in sizes:
        acc += s
        pts.append(acc)
    return pts

def second_inputs(seed: int = 0) -> dict:
    key = jax.random.key(seed)
    ks = jax.random.split(key, 20)

    def nrm(k, shape, scale):
        return jax.random.normal(k, shape, jnp.float32) * scale

    return {
        'x': nrm(ks[0], (BATCH, SEQ, D_MODEL), 1.0),
        'norm_mix_pre': 1.0 + nrm(ks[1], (DEPTH, D_MODEL), 0.05),
        'norm_mix_post': 1.0 + nrm(ks[2], (DEPTH, D_MODEL), 0.05),
        'norm_ffn_pre': 1.0 + nrm(ks[3], (DEPTH, D_MODEL), 0.05),
        'norm_ffn_post': 1.0 + nrm(ks[4], (DEPTH, D_MODEL), 0.05),
        'w_in': nrm(ks[5], (DEPTH, D_MODEL, D_IN), D_MODEL ** -0.5),
        'pe_cmp_k': nrm(ks[6], (DEPTH, L_CMP, HEAD_DIM), 0.5),
        'pe_cmp_v': nrm(ks[7], (DEPTH, L_CMP, HEAD_DIM), 0.5),
        'w_cmp_k1': nrm(ks[8], (DEPTH, L_CMP * HEAD_DIM, CMP_HIDDEN), (L_CMP * HEAD_DIM) ** -0.5),
        'w_cmp_k2': nrm(ks[9], (DEPTH, CMP_HIDDEN, HEAD_DIM), CMP_HIDDEN ** -0.5),
        'w_cmp_v1': nrm(ks[10], (DEPTH, L_CMP * HEAD_DIM, CMP_HIDDEN), (L_CMP * HEAD_DIM) ** -0.5),
        'w_cmp_v2': nrm(ks[11], (DEPTH, CMP_HIDDEN, HEAD_DIM), CMP_HIDDEN ** -0.5),
        'rel_bias': nrm(ks[12], (N_HEADS, N_BUCKETS), 0.5),
        'conv_mix_w': nrm(ks[13], (DEPTH, CONV_W, D_CONV), CONV_W ** -0.5),
        'w_out': nrm(ks[14], (DEPTH, D_MIX, D_MODEL), D_MIX ** -0.5),
        'w_ffn_up': nrm(ks[15], (DEPTH, D_MODEL, 2 * D_FF), D_MODEL ** -0.5),
        'ffn_conv_w': nrm(ks[16], (DEPTH, CONV_W, 2 * D_FF), CONV_W ** -0.5),
        'w_ffn_down': nrm(ks[17], (DEPTH, D_FF, D_MODEL), D_FF ** -0.5),
    }

def second_block(x, norm_mix_pre, norm_mix_post, norm_ffn_pre, norm_ffn_post, w_in,
              pe_cmp_k, pe_cmp_v, w_cmp_k1, w_cmp_k2, w_cmp_v1, w_cmp_v2, rel_bias,
              conv_mix_w, w_out, w_ffn_up, ffn_conv_w, w_ffn_down):
    B, S, _ = x.shape
    for l in range(DEPTH):
        h = rms_norm(x, norm_mix_pre[l])
        u = h @ w_in[l]
        q, k_c, v_c, k_s, v_s, k_w, v_w, gl, b_g, c_g, x_t = jnp.split(
            u, split_points(), axis=-1)
        kv = lambda a: a.reshape(B, S, N_KV, HEAD_DIM)
        o_nsa = nsa_attention(q.reshape(B, S, N_HEADS, HEAD_DIM),
                              kv(k_c), kv(v_c), kv(k_s), kv(v_s), kv(k_w), kv(v_w), gl,
                              pe_cmp_k[l], pe_cmp_v[l], w_cmp_k1[l], w_cmp_k2[l],
                              w_cmp_v1[l], w_cmp_v2[l], rel_bias)
        o_conv = short_conv_mixer(b_g, c_g, x_t, conv_mix_w[l])
        y = jnp.concatenate([o_nsa, o_conv], axis=-1) @ w_out[l]
        x = x + rms_norm(y, norm_mix_post[l])
        h = rms_norm(x, norm_ffn_pre[l])
        gu = causal_dwconv(h @ w_ffn_up[l], ffn_conv_w[l])
        g, up = jnp.split(gu, 2, axis=-1)
        y = (jax.nn.gelu(g, approximate=True) * up) @ w_ffn_down[l]
        x = x + rms_norm(y, norm_ffn_post[l])
    return x


def setup_inputs(seed=0):
    out = dict(first_inputs(seed))
    for name, value in second_inputs(seed + 1).items():
        if name != "x":
            out[name + "_2"] = value
    return out


def reference(
    x, c, emb_ln_g, emb_ln_b, w_ada, b_ada, w_in, mu_shift, sg_ln_g, sg_ln_b, w_s, b_s, w0,
    w_up, a0, a_up, g_up, k_k, k_a, r_k, lnx_g, lnx_b, w_out, ln1_g, ln1_b, w_ffn_in, w_ffn_out,
    ln2_g, ln2_b, norm_mix_pre_2, norm_mix_post_2, norm_ffn_pre_2, norm_ffn_post_2, w_in_2,
    pe_cmp_k_2, pe_cmp_v_2, w_cmp_k1_2, w_cmp_k2_2, w_cmp_v1_2, w_cmp_v2_2, rel_bias_2,
    conv_mix_w_2, w_out_2, w_ffn_up_2, ffn_conv_w_2, w_ffn_down_2,
):
    x = first_block(
        x, c, emb_ln_g, emb_ln_b, w_ada, b_ada, w_in, mu_shift, sg_ln_g, sg_ln_b, w_s, b_s, w0,
        w_up, a0, a_up, g_up, k_k, k_a, r_k, lnx_g, lnx_b, w_out, ln1_g, ln1_b, w_ffn_in,
        w_ffn_out, ln2_g, ln2_b,
    )
    return second_block(
        x, norm_mix_pre_2, norm_mix_post_2, norm_ffn_pre_2, norm_ffn_post_2, w_in_2, pe_cmp_k_2,
        pe_cmp_v_2, w_cmp_k1_2, w_cmp_k2_2, w_cmp_v1_2, w_cmp_v2_2, rel_bias_2, conv_mix_w_2,
        w_out_2, w_ffn_up_2, ffn_conv_w_2, w_ffn_down_2,
    )


_drawn_inputs = setup_inputs


def setup_inputs(seed=0):
    import zlib

    import numpy as np

    out = dict(_drawn_inputs(seed))
    spreads = {}
    factors = {'b_ada': 2.867,
     'sg_ln_g': 8.0,
     'sg_ln_b': 38.459,
     'b_s': 4.264,
     'w_up': 7.739,
     'a0': 8.0,
     'k_k': 36.487,
     'k_a': 8.0,
     'lnx_g': 8.0,
     'lnx_b': 40.588,
     'pe_cmp_k_2': 3.769}
    for name, (base, spread) in spreads.items():
        noise = np.random.default_rng([zlib.crc32(name.encode()), seed]).standard_normal(out[name].shape)
        drawn = base * np.exp(spread * noise) if base else spread * noise
        out[name] = jnp.asarray(drawn.astype(out[name].dtype))
    for name, factor in factors.items():
        out[name] = (out[name] * factor).astype(out[name].dtype)
    return out
```

```python
import math

import numpy as np

import concourse.bass as bass
from concourse import mybir

F32 = mybir.dt.float32
F32R = mybir.dt.float32r
ACT = mybir.ActivationFunctionType
ALU = mybir.AluOpType
AX_X = mybir.AxisListType.X

P = 128
SEQ = 512
TT = SEQ // P
DM = 1024
KC = DM // P
MIX = 512
PAIRS = MIX // P
HD = 64
CH = 32
NCH = P // CH
FFN = 2816
FT = FFN // P
ALPHA = 2.0 ** 0.25
LN_EPS, GN_EPS, RMS_EPS = 1e-5, 64e-5, 1e-6
DECAY = math.exp(-0.5)
N_HEADS, N_KV, REP = 8, 2, 4
L_CMP, S_CMP = 32, 16
N_CMP = (SEQ - L_CMP) // S_CMP + 1
CMP_HID = 256
N_BUCKETS, MAX_DIST = 32, 128
NEG = -1e30
GRID = SEQ + P

COLS, N_COLS = {}, 0
for _name, _n in (("c", KC), ("emb_g", KC), ("emb_b", KC), ("mu_l", 1), ("mu_g0", 1), ("mu_g1", 1),
                  ("mu_k", 4), ("mu_v", 4), ("mu_r", 4), ("w0", 4), ("a0", 4), ("k_k", 4), ("k_a", 4),
                  ("r_k", 4), ("lnx_g", 4), ("lnx_b", 4), ("ln1_g", KC), ("ln1_b", KC), ("nmp", KC),
                  ("nfp", KC), ("cmix", 12), ("cffn", 3 * 2 * FT), ("pe_k", L_CMP), ("pe_v", L_CMP),
                  ("has_key", 1), ("b_sh1", KC), ("b_sc1", KC), ("b_sh2", KC), ("b_sc2", KC)):
    COLS[_name] = N_COLS
    N_COLS += _n
N_MU = 15

CONSTS = {"ident": (0, 128), "bd64": (128, 128), "up": (256, 128), "mask_qr": (384, 256),
          "mask_mk": (640, 256), "mask_d": (896, 128), "mask_e": (1024, 128), "chunk_rows": (1152, 4),
          "onehot": (1156, GRID), "future": (1156 + GRID, SEQ)}
N_CONST = 1156 + GRID + SEQ


def shape_constants():
    c = np.zeros((P, N_CONST), np.float32)
    p, f = np.arange(P)[:, None], np.arange(P)[None, :]

    def put(name, v):
        at, n = CONSTS[name]
        c[:, at:at + n] = v

    same = lambda n: (p // n) == (f // n)
    put("ident", p == f)
    put("bd64", same(64))
    put("up", p <= f)
    put("mask_qr", np.concatenate([(p < f) & same(16), (p <= f) & same(CH)], 1))
    put("mask_mk", np.concatenate([(p < f) & same(CH), (p <= f) & same(CH)], 1))
    put("mask_d", (p > f) & same(16))
    put("mask_e", (p > f) & same(CH) & ~same(16))
    put("chunk_rows", (p // CH) == np.arange(NCH)[None, :])
    dist = (SEQ - 1) - np.arange(GRID)
    exact = N_BUCKETS // 2
    d = np.maximum(dist, 0)
    df = np.maximum(d, 1).astype(np.float32)
    scaled = np.log(df / np.float32(exact)) / np.float32(math.log(MAX_DIST / exact))
    large = exact + (scaled * np.float32(N_BUCKETS - exact)).astype(np.int32)
    bucket = np.where(d < exact, d, np.minimum(large, N_BUCKETS - 1))
    c[:N_BUCKETS, CONSTS["onehot"][0]:][:, :GRID] = bucket[None, :] == np.arange(N_BUCKETS)[:, None]
    put("future", np.where(p + 384 - np.arange(SEQ)[None, :] < 0, -NEG, 0.0))
    return c


def weight_units():
    units = [(f"ada0_{k}", "w_ada", k * P, 1, ((0, 2 * DM),)) for k in range(KC)]
    base = 2 * MIX
    lora = base + 3 * MIX
    win = [("lora0", ((lora, 256),)), ("lora1", ((lora + 160, 128),))]
    win += [(f"k{j}", ((base + MIX + 256 * j, 256),)) for j in range(2)]
    win += [(f"r{j}", ((base + 256 * j, 256),)) for j in range(2)]
    win += [(f"v{j}", ((base + 2 * MIX + 256 * j, 256),)) for j in range(2)]
    win += [(f"pu{j}", ((256 * j, 256),)) for j in range(2)]
    win += [(f"pv{j}", ((MIX + 256 * j, 256),)) for j in range(2)]
    ada = [(f"ada1_{k}", "w_ada", k * P, 1, ((3 * DM, 2 * DM),)) for k in range(KC)]
    ada += [(f"ada2_{k}", "w_ada", k * P, 1, ((2 * DM, DM), (5 * DM, DM))) for k in range(KC)]
    for n, (name, ranges) in enumerate(win):
        units.append((name, "w_in", 0, KC, ranges))
        units.append(ada[n])
    units += ada[len(win):]
    units += [(f"out1_{n}", "w_out", 2 * n * P, 2, ((0, DM),)) for n in range(4)]
    for m in range(FT):
        units.append((f"up1_{m}", "w_ffn_in", 0, KC, ((m * P, P), (FFN + m * P, P))))
    for n in range(FT // 2):
        units.append((f"down1_{n}", "w_ffn_out", 2 * n * P, 2, ((0, DM),)))
    kv = MIX
    win2 = [("cmp", ((kv, 256),))] + [(f"q{j}", ((256 * j, 256),)) for j in range(2)]
    win2 += [("slc", ((kv + 256, 256),)), ("win", ((kv + 512, 256),)), ("gates", ((kv + 768, 24),))]
    for part, name in enumerate(("bg", "cg", "xt")):
        win2 += [(f"{name}{j}", ((kv + 792 + part * MIX + 256 * j, 256),)) for j in range(2)]
    units += [(name, "w_in_2", 0, KC, ranges) for name, ranges in win2]
    units += [(f"out2_{n}", "w_out_2", 2 * n * P, 2, ((0, DM),)) for n in range(4)]
    units += [(f"up2_{m}", "w_ffn_up_2", 0, KC, ((m * P, P), (FFN + m * P, P))) for m in range(FT)]
    units += [(f"down2_{n}", "w_ffn_down_2", 2 * n * P, 2, ((0, DM),)) for n in range(FT // 2)]
    return units


UNITS = weight_units()
UNIT_AT = {u[0]: n for n, u in enumerate(UNITS)}
UNIT_SIZE = [u[3] * sum(w for _, w in u[4]) for u in UNITS]
UNIT_START = [sum(UNIT_SIZE[:n]) for n in range(len(UNITS) + 1)]
SPLIT_UNITS = [n for n, u in enumerate(UNITS) if u[1] != "w_ada"]
SPLIT_AT = {n: i for i, n in enumerate(SPLIT_UNITS)}
RAW, SPLIT = 3, 2


class Order:

    def __init__(self, eng, own):
        self.eng, self.own, self.count, self.last = eng, own, {}, None

    def done(self, ins, sem=None):
        sem = self.own if sem is None else sem
        self.count[sem.name] = self.count.get(sem.name, 0) + 1
        ins.then_inc(sem, 1)
        self.last = (sem, self.count[sem.name])

    def settle(self):
        self.eng.wait_ge(*self.last)

    def step(self, ins, sem=None):
        self.done(ins, sem)
        self.settle()


class Banks:

    def __init__(self):
        self.fills = [0] * 8
        self.drains = {"dve": [0] * 8, "act": [0] * 8}
        self.of = {}
        self.turn = 0

    def add(self, name, bank=None, dve=0, act=0, unit=None):
        if bank is None:
            bank = 4 + self.turn % 4
            self.turn += 1
        before = {e: self.drains[e][bank] for e in self.drains}
        if unit is None:
            self.fills[bank] += 1
        self.drains["dve"][bank] += dve
        self.drains["act"][bank] += act
        after = {e: self.drains[e][bank] for e in self.drains}
        self.of[name] = (bank, self.fills[bank] if unit is None else SPLIT_AT[UNIT_AT[unit]] + 1, before, after,
                         unit is not None)


def plan_banks():
    b = Banks()
    turn = [0]

    def dense(name, drains):
        pair = 2 * (turn[0] % 2)
        turn[0] += 1
        for j, drain in enumerate(drains):
            b.add((name, j), pair + j, unit=name if j == len(drains) - 1 else None, **drain)

    def dense_rows(name, last_unit, act=0):
        for t in range(TT):
            for j in range(2):
                b.add((name, t, j), 2 * t + j, dve=1, act=act, unit=last_unit if (t, j) == (TT - 1, 1) else None)

    b.add("cols0", dve=1)
    for k in range(KC):
        b.add(("h1", k), dve=1, act=1)
    for name in ("lora0", "lora1", "k0", "k1", "r0", "r1", "v0", "v1"):
        dense(name, drains=[dict(dve=1, act=1)] * (1 if name == "lora1" else 2))
    b.add("cols1", dve=1)
    prep(b, 0)
    for name in ("pu0", "pu1"):
        dense(name, drains=[dict(act=1)] * 2)
    for name in ("pv0", "pv1"):
        dense(name, drains=[dict(act=1)] * 2)
    for g in range(4):
        b.add(("sgu", g), dve=1)
    for p in range(PAIRS):
        if p:
            prep(b, p)
        prep2(b, p)
        for pair_of_tiles in range(2):
            tiles = (2 * pair_of_tiles, 2 * pair_of_tiles + 1)
            for stage, drain in CHUNK_STAGES:
                for t in tiles:
                    b.add((stage, p, t), **drain)
            for t in tiles:
                b.add(("y", p, t), dve=1)
                for c in range(NCH):
                    b.add(("state", p, t, c), dve=1)
        b.add(("mean", p), dve=1)
        b.add(("var", p), dve=1)
    for j in range(4):
        b.add(("mod_rows", j), j, act=1)
    dense_rows("mix1", "out1_3")
    for k in range(KC):
        b.add(("h2", k), dve=1, act=1)
    for m in range(FT):
        dense(f"up1_{m}", drains=[dict(act=1), dict(dve=1)])
    dense_rows("ff1", f"down1_{FT // 2 - 1}")
    plan_second(b, dense, dense_rows)
    return b.of


def prep(b, p):
    for name, drain in (("z", dict(act=1)), ("a", dict(act=1)), ("kk", dict(dve=1))):
        b.add((name, p), **drain)


def prep2(b, p):
    b.add(("bonus", p), dve=1)
    b.add(("g", p), act=1)


CHUNK_STAGES = (("turn", dict(dve=2, act=2)), ("m1", dict(dve=1)), ("m2", dict(dve=1)), ("n1", dict(dve=2)),
                ("n2", dict(dve=2)), ("mv", dict(act=1)), ("q2", dict(act=2)), ("n4", dict(act=1)),
                ("q4", dict(dve=1, act=1)), ("r2", dict(dve=1, act=1)), ("r3", dict(dve=1)),
                ("z1", dict(dve=1, act=1)), ("z2", dict(dve=1)), ("yl", dict(dve=2, act=2)),
                ("gt", dict(dve=1)), ("hh", dict(dve=1)))


ITEMS = [(br, h, i) for br in ("slc", "win", "cmp") for h in range(N_HEADS) for i in range(TT)]
N_SLOTS = len(ITEMS) + 3
SLOT_UNITS = ("bg0", "bg1", "cg0", "cg1", "xt0", "xt1")
PER_UNIT = -(-N_SLOTS // len(SLOT_UNITS))
FIRST_UNITS = ("cmp", "q0", "q1", "slc", "win", "gates")


def slots_of(n):
    return range(PER_UNIT * n, min(PER_UNIT * (n + 1), N_SLOTS))


def stages_of(slot):
    return [(st, slot - lag) for st, lag in (("scores", 0), ("turn2", 2), ("values", 3))
            if 0 <= slot - lag < len(ITEMS)]


def n_keys(item):
    br, _, i = ITEMS[item]
    return (P // S_CMP) * i + P // S_CMP - 1 if br == "cmp" else P * (i + 1)


def plan_second(b, dense, dense_rows):
    for k in range(KC):
        b.add(("h3", k), dve=1, act=1)
    for j in range(2):
        b.add(("bias", j), act=1)
    for name in FIRST_UNITS:
        dense(name, drains=[dict(act=1)] * (1 if name == "gates" else 2))
        if name in ("q1", "win"):
            kv = "k" if name == "q1" else "v"
            b.add(("hidden", kv), act=1)
            b.add(("compressed", kv), act=1)
    for n, name in enumerate(SLOT_UNITS):
        dense(name, drains=[dict(dve=1) if name[:2] == "xt" else dict(act=1)] * 2)
        for slot in slots_of(n):
            for st, item in stages_of(slot):
                b.add((st, item), **(dict(act=1) if st == "turn2" else dict(dve=1)))
    for k in range(PAIRS):
        b.add(("turn_o", k), act=1, dve=1)
    dense_rows("mix2", "out2_3", act=1)
    for k in range(KC):
        b.add(("h4", k), dve=1, act=1)
    for m in range(FT):
        dense(f"up2_{m}", drains=[dict(act=1, dve=1)] * 2)
    dense_rows("ff2", f"down2_{FT // 2 - 1}", act=1)


def build(nc, src, out):
    bank_of = plan_banks()
    byte = {"at": (nc.sbuf_base + 63) // 64 * 64}
    from contextlib import ExitStack
    ctx = ExitStack()

    def place(name, shape, dt=F32, at=None):
        size = (4 * int(np.prod(shape[1:])) + 31) // 32 * 32
        if at is None:
            at = byte["at"]
            byte["at"] += size
        t = nc.alloc_sbuf_tensor_at(name, list(shape), dt, offset=at)
        return t, at + size

    def sem(name):
        return ctx.enter_context(nc.semaphore(name))

    raw = [place(f"raw{i}", [P, 2048])[0] for i in range(RAW)]
    whi = [place(f"weight_hi{i}", [P, 2048], F32R)[0] for i in range(SPLIT)]
    wlo = [place(f"weight_lo{i}", [P, 2048], F32R)[0] for i in range(SPLIT)]
    act_at = byte["at"]
    act_hi, _ = place("act_hi", [P, KC, SEQ], F32R)
    act_lo, _ = place("act_lo", [P, KC, SEQ], F32R)
    xres, _ = place("xres", [P, TT, DM])
    acc, _ = place("acc", [P, 2 * DM])
    pc, _ = place("params", [P, N_COLS])
    omu, _ = place("one_minus_mu", [P, N_MU])
    oka, _ = place("one_minus_ka", [P, 4])
    affine, _ = place("affine", [P, 4, KC])
    modc, _ = place("mod_columns", [P, 2 * KC])
    ident, _ = place("ident", [P, P])
    bd64, _ = place("bd64", [P, P])
    stats, _ = place("stats", [P, 2, 6])
    mv, _ = place("mean_var", [P, TT, 2])
    rstd, _ = place("rstd", [P, TT])
    ones, _ = place("ones", [P, 1])
    bias4, _ = place("bias4", [4, SEQ])
    byte["small"] = byte["at"]
    byte["at"] += 32
    arena = byte["at"]

    nxt = arena
    def here(name, shape, dt=F32):
        nonlocal nxt
        t, nxt = place(name, shape, dt, nxt)
        return t
    kT, rT, vT = (here(f"{n}T", [P, PAIRS, SEQ]) for n in "krv")
    lora = here("lora", [P, SEQ])
    gd = here("gd", [P, 2, SEQ])
    uT = here("uT", [P, 4, SEQ])
    wup = here("wup", [P, MIX])
    gup = here("gup", [P, 2, MIX])
    chunk_rows = here("chunk_rows", [P, NCH])
    masks = here("masks", [P, 4, P])
    mask_d = here("mask_d", [P, P])
    mask_e = here("mask_e", [P, P])
    restart = here("restart", [P, SEQ])
    state = [here(f"state{i}", [P, P]) for i in range(2)]
    decayed = here("decayed", [P, P])
    pend = here("chunk_decay", [P, SEQ // CH])
    gm_at = nxt
    pv = here("pv", [P, TT, MIX])
    wsT = here("wsT", [P, 4, P])
    bs = here("bs", [P, 4, P])
    sg_g = here("sg_g", [P, MIX])
    sg_b = here("sg_b", [P, MIX])
    gm_end = nxt
    pair_at = nxt
    sig = here("sig", [P, SEQ])
    cs = here("cs", [P, SEQ])
    aa = here("aa", [P, SEQ])
    kk = here("kk", [P, SEQ])
    ep = here("ep", [P, SEQ])
    sq = here("sq", [P, SEQ])
    ar = here("ar", [P, 2, SEQ])
    bt = here("bt", [P, SEQ])
    kt = here("kt", [P, SEQ])
    pair_end = nxt
    row_a, _ = place("row_a", [P, DM], F32, pair_at)
    row_b, _ = place("row_b", [P, DM], F32, pair_at + 4096)
    up, _ = place("up", [P, P], F32, pair_at + 8192)
    assert pair_end <= nc.sbuf_usable_end, (pair_end, nc.sbuf_usable_end)

    sets = []
    nxt = act_at
    gap = act_at + 2 * KC * SEQ * 4
    def chunk(name, shape):
        nonlocal nxt
        size = (4 * int(np.prod(shape[1:])) + 31) // 32 * 32
        if nxt <= gap and nxt + size > gap:
            nxt = gm_at
        t, nxt = place(name, shape, F32, nxt)
        assert nxt <= gap or gm_at < nxt <= gm_end, (name, nxt)
        return t
    for q in range(2):
        d = {}
        for name, shape in (("mm", [P, 2, 4, P]), ("nd", [P, 2, P]), ("ee", [P, 2, P]),
                            ("rq", [P, 2, 2, P]), ("nn", [P, 2, P]), ("rb", [P, 2, P]), ("z0", [P, 256]),
                            ("z1", [P, 256]), ("z", [P, 256]), ("gt", [P, NCH, P]), ("hb", [P, NCH, P]),
                            ("rp", [P, P]), ("yl", [P, P]), ("bx", [P, NCH, P]), ("kx", [P, NCH, P]),
                            ("vz", [P, 256])):
            d[name] = chunk(f"{name}_{q}", shape)
        sets.append(d)

    hid_hi, e1 = place("hid_hi", [P, FT, SEQ], F32R, arena)
    hid_lo, e1 = place("hid_lo", [P, FT, SEQ], F32R, e1)
    assert e1 <= nc.sbuf_usable_end, (e1, nc.sbuf_usable_end)

    nxt = arena
    xn2, _ = place("xn2", [P, TT, DM], F32, nxt)
    w1 = here("w1", [P, L_CMP // 2, CMP_HID])
    qT = here("qT", [P, PAIRS, SEQ])
    kvc = here("kvc", [P, 2, SEQ])
    ksl = here("ksl", [P, 2, SEQ])
    kwn = here("kwn", [P, 2, SEQ])
    vsl = here("vsl", [P, TT, P])
    vwn = here("vwn", [P, TT, P])
    gate = here("gate", [P, TT, 24])
    bgT = here("bgT", [P, 4, SEQ])
    cgT = here("cgT", [P, 4, SEQ])
    strip = here("strip", [P, N_HEADS, SEQ])
    o_at = nxt
    o = here("o", [P, TT, MIX])
    onehot, z = place("onehot", [P, GRID], F32, o_at)
    future, z = place("future", [P, SEQ], F32, z)
    grow, z = place("grow", [N_HEADS, GRID], F32, z)
    assert z <= nxt
    blk = here("blk", [P, L_CMP // 2, 2 * N_CMP])
    w2k = here("w2k", [P, 2, P])
    w2v = here("w2v", [P, 2, HD])
    hc = here("hc", [P, 2, 2 * N_CMP])
    kc2 = here("kc2", [P, 2, N_CMP])
    vc = here("vc", [P, 2, HD])
    relb = here("relb", [P, N_HEADS])
    low = here("low", [P, 3])
    den = here("den", [P, 3])
    weights4 = here("weights4", [P, 4])
    sc4 = here("sc4", [P, SEQ])
    assert nxt <= nc.sbuf_usable_end, nxt
    scores = [acc[:, SEQ * j:SEQ * j + SEQ] for j in range(3)]
    probsT = [acc[:, 3 * SEQ:4 * SEQ], sc4[:]]
    conv_t = w1[:].rearrange("p a b -> p (a b)")[:, 0:SEQ]
    row3, z = place("row3", [P, DM], F32, arena + 4 * TT * DM)
    rms_t, _ = place("rms_t", [P, DM], F32, z)
    row4, z = place("row4", [P, DM], F32, act_at)
    rms_t2, _ = place("rms_t2", [P, DM], F32, z)
    squares, _ = place("squares", [P, 2 * TT], F32, byte["small"])
    scratch = nc.dram_tensor("bias_rows", (N_HEADS, P, GRID), F32, kind="Internal").ap()

    banks = [ctx.enter_context(nc.psum_tensor(f"bank{i}", [P, 512], F32)) for i in range(8)]

    filled = [sem(f"filled{i}") for i in range(8)]
    drained = {"dve": [sem(f"dve_drained{i}") for i in range(8)],
               "act": [sem(f"act_drained{i}") for i in range(8)]}
    raw_landed = [sem(f"raw_landed{i}") for i in range(RAW)]
    hi_ready, lo_ready, unit_used, ada_used = sem("hi_ready"), sem("lo_ready"), sem("unit_used"), sem("ada_used")
    act_step, dve_step, pe_step = sem("act_step"), sem("dve_step"), sem("pe_step")
    load = {n: sem(f"load_{n}") for n in ("x", "params", "consts", "masks", "gmlp", "rows0", "rows1", "rows2",
                                          "bias", "out", "tabs", "w1", "strip0", "strip", "rows3", "rows4")}
    S = {n: sem(n) for n in ("silu_c", "std_x", "xn_ready", "affine1", "h_hi", "h_lo", "shift_ready", "lora_ready",
                             "kk_sq", "cs_ready", "exp_ready", "ss_ready", "root_ready", "prep_ready",
                             "bars_ready", "wst_ready", "pv_ready", "pv_std", "pv_root", "gelu_ready", "acc1", "acc2",
                             "r0_ready", "w_ready", "sets_ready", "state_zero", "y_raw", "y_sq", "var_ready", "yb_ready",
                             "y_hi", "y_lo", "gates_ready", "var1", "root1", "xn2_ready", "affine2", "hid_hi_ready",
                             "hid_ready", "var2", "root2", "x_ready", "ss3", "root3", "xn3_ready", "grow_ready", "strip_ready", "blk_ready", "hc_ready", "low_ready",
                             "exp_done", "gate_ready", "o_ready", "conv_ready", "y2_hi", "y2_lo", "squares_ready",
                             "rms_ready", "rms_root", "conv1_ready", "gelu2", "prod2", "hid2_hi", "hid2_lo", "out_ready", "keys_part", "weight_ready")}

    def job(name):
        return bank_of[name]

    def bank(name):
        return banks[job(name)[0]]

    def claim(pe, name):
        b, _, before, _, _ = job(name)
        for e in ("dve", "act"):
            if before[e]:
                pe.wait_ge(drained[e][b], before[e])

    def full_sem(name):
        b, n, _, _, by_unit = job(name)
        return (unit_used if by_unit else filled[b]), n

    def await_full(eng, name):
        eng.wait_ge(*full_sem(name))

    def await_drained(eng, name, by):
        b, _, _, after, _ = job(name)
        eng.wait_ge(drained[by][b], after[by])

    def drain(name, by):
        return drained[by][job(name)[0]]

    def raw_ready(eng, n):
        eng.wait_ge(raw_landed[n % RAW], 16 * (n // RAW + 1))

    def col(name, j=0):
        return pc[:, COLS[name] + j:COLS[name] + j + 1]

    def tok(t):
        return slice(t * P, (t + 1) * P)

    def const(name):
        at, n = CONSTS[name]
        return src["consts"][:, at:at + n]

    row2_a, a2 = place("row2_a", [P, DM], F32, act_at)
    row2_b, a2 = place("row2_b", [P, DM], F32, a2)
    mixed2, a2 = place("mixed2", [P, DM], F32, a2)
    mixed, _ = place("mixed", [P, DM], F32, arena)

    def second_act(act, a, convert, affine_hi):
        act.wait_ge(S["x_ready"], 1)

        def squares_of_x():
            for t in range(TT):
                a.step(act.activation(xn2[:, t, :], xres[:, t, :], ACT.Square, accum_out=rstd[:, t:t + 1]),
                       S["squares_ready"])

        def root(n):
            act.wait_ge(S["rms_ready"], n)
            a.done(act.activation(rstd[:], rstd[:], ACT.Sqrt), S["rms_root"])

        squares_of_x()
        act.dma_start(relb[0:N_BUCKETS, :], src["rel_bias_t"]).then_inc(load["tabs"], 16)
        act.dma_start(onehot[0:N_BUCKETS, :], const("onehot")[0:N_BUCKETS]).then_inc(load["tabs"], 16)
        act.dma_start(future[:], const("future")).then_inc(load["tabs"], 16)
        act.dma_start(w2k[:], src["w2k"]).then_inc(load["tabs"], 16)
        act.dma_start(w2v[:], src["w2v"]).then_inc(load["tabs"], 16)
        root(1)
        affine_hi("h3", "nmp")
        act.dma_start(w1[:], src["w1"][0]).then_inc(load["w1"], 16)
        for j, n in enumerate((SEQ, GRID - SEQ)):
            await_full(act, ("bias", j))
            a.done(act.activation(grow[:, SEQ * j:SEQ * j + n], bank(("bias", j))[0:N_HEADS, 0:n], ACT.Copy, scale=-1.0),
                   drain(("bias", j), "act"))
        a.settle()
        act.wait_ge(drained["act"][job(("bias", 0))[0]], job(("bias", 0))[3]["act"])
        act.dma_start(scratch, grow[:].unsqueeze(1).to_broadcast([N_HEADS, P, GRID])).then_inc(load["strip0"], 16)
        act.wait_ge(load["strip0"], 16)
        act.dma_start(strip[:], bass.AP(scratch.tensor, P - 1, [[GRID - 1, P], [P * GRID, N_HEADS], [1, SEQ]])).then_inc(load["strip"], 16)

        def compress(kv):
            j = "kv".index(kv)
            await_full(act, ("hidden", kv))
            a.done(act.activation(hc[:].rearrange("p a b -> p (a b)"), bank(("hidden", kv))[:, 0:4 * N_CMP], ACT.Gelu_apprx_tanh),
                   drain(("hidden", kv), "act"))
            if kv == "k":
                act.dma_start(w1[:], src["w1"][1]).then_inc(load["w1"], 16)
            await_full(act, ("compressed", kv))
            b = bank(("compressed", kv))
            if kv == "k":
                a.done(act.activation(kc2[:].rearrange("p a b -> p (a b)"), b[:, 0:2 * N_CMP], ACT.Copy), drain(("compressed", kv), "act"))
            else:
                a.done(act.activation(vc[0:N_CMP].rearrange("p a b -> p (a b)"), b[0:N_CMP, 0:2 * HD], ACT.Copy),
                       drain(("compressed", kv), "act"))

        for name in FIRST_UNITS:
            convert()
            b0 = bank((name, 0))
            if name in ("cmp", "q0", "q1"):
                for j in range(2):
                    await_full(act, (name, j))
                    if name == "cmp":
                        ins = act.activation(kvc[:, j, :], bank((name, j))[:], ACT.Copy)
                    else:
                        ins = act.activation(qT[:, 2 * int(name[1]) + j, :], bank((name, j))[:], ACT.Copy, scale=-(HD ** -0.5))
                    a.done(ins, drain((name, j), "act"))
            elif name in ("slc", "win"):
                keys, values = (ksl, vsl) if name == "slc" else (kwn, vwn)
                await_full(act, (name, 0))
                for g in range(N_KV):
                    for half in range(2):
                        ins = act.activation(keys[HD * half:HD * half + HD, g, :], b0[HD * g:HD * g + HD, :], ACT.Copy)
                        a.done(ins, drain((name, 0), "act") if g == half == 1 else S["keys_part"])
                await_full(act, (name, 1))
                a.done(act.activation(values[:].rearrange("p t d -> p (t d)"), bank((name, 1))[:], ACT.Copy), drain((name, 1), "act"))
            else:
                await_full(act, (name, 0))
                a.done(act.activation(gate[:].rearrange("p t g -> p (t g)"), b0[:, 0:24 * TT], ACT.Sigmoid), drain((name, 0), "act"))
            if name in ("q1", "win"):
                compress("k" if name == "q1" else "v")

        for n, name in enumerate(SLOT_UNITS):
            convert()
            for slot in slots_of(n):
                if 0 <= slot < len(ITEMS):
                    x, w = slot % 3, n_keys(slot)
                    act.wait_ge(S["low_ready"], slot + 1)
                    a.step(act.activation(scores[x][:, 0:w], scores[x][:, 0:w], ACT.Exp, bias=low[:, x:x + 1], scale=-1.0,
                                          accum_out=den[:, x:x + 1]), S["exp_done"])
                if 0 <= slot - 2 < len(ITEMS):
                    item = slot - 2
                    w = n_keys(item)
                    await_full(act, ("turn2", item))
                    if item >= 2:
                        await_full(act, ("values", item - 2))
                    b = bank(("turn2", item))
                    if w < P:
                        ins = act.activation(probsT[item % 2][0:w, 0:P], b[0:w, 0:P], ACT.Copy)
                    else:
                        ins = act.activation(probsT[item % 2][:, 0:w], b[:, 0:w], ACT.Copy)
                    a.done(ins, drain(("turn2", item), "act"))
            if name[:2] != "xt":
                dest = bgT if name[0] == "b" else cgT
                for j in range(2):
                    await_full(act, (name, j))
                    a.done(act.activation(dest[:, 2 * int(name[2]) + j, :], bank((name, j))[:], ACT.Copy), drain((name, j), "act"))

        for k in range(PAIRS):
            await_full(act, ("turn_o", k))
            a.done(act.activation(act_hi[:, k, :], bank(("turn_o", k))[:], ACT.Copy), drain(("turn_o", k), "act"))
        act.wait_ge(S["conv_ready"], 4)
        a.done(act.activation(act_hi[:, 4:8, :], bgT[:], ACT.Copy), S["y2_hi"])
        act.dma_start(row3[:], src["mix_post"].partition_broadcast(P)).then_inc(load["rows3"], 16)

        def squares_of_rows(stage, temp):
            for t in range(TT):
                for j in range(2):
                    await_full(act, (stage, t, j))
                    a.step(act.activation(temp[:, 0:SEQ], bank((stage, t, j))[:], ACT.Square,
                                          accum_out=squares[:, 2 * t + j:2 * t + j + 1]), drain((stage, t, j), "act"))

        for n in range(4):
            convert()
        squares_of_rows("mix2", rms_t)
        root(2)
        act.wait_ge(S["x_ready"], 2)
        squares_of_x()
        root(3)
        affine_hi("h4", "nfp")

        for m in range(FT):
            convert()
            name = f"up2_{m}"
            pair = [acc[:, SEQ * (2 * (m % 2) + j):SEQ * (2 * (m % 2) + j) + SEQ] for j in range(2)]
            for j in range(2):
                await_full(act, (name, j))
                a.done(act.activation(pair[j], bank((name, j))[:], ACT.Copy, scale=col("cffn", 2 * 2 * FT + FT * j + m)),
                       drain((name, j), "act"))
            await_drained(act, (name, 0), "dve")
            a.done(act.activation(pair[0], pair[0], ACT.Gelu_apprx_tanh), S["gelu2"])
            act.wait_ge(S["prod2"], m + 1)
            a.done(act.activation(hid_hi[:, m, :], pair[1], ACT.Copy), S["hid2_hi"])
        for n in range(FT // 2):
            convert()
            if n == 0:
                await_full(act, (f"up2_{FT - 1}", 1))
                act.dma_start(row4[:], src["ffn_post"].partition_broadcast(P)).then_inc(load["rows4"], 16)
        squares_of_rows("ff2", rms_t2)
        root(4)

    def second_dve(dve, d, ts, tt, stt, affine_lo):
        V = dve

        def rms(n):
            ts(rstd[:], rstd[:], 1.0 / DM, RMS_EPS, ALU.mult, ALU.add, sem=S["rms_ready"])
            dve.wait_ge(S["rms_root"], n)
            d.step(V.reciprocal(rstd[:], rstd[:]))

        def scale_x(n):
            dve.wait_ge(S["squares_ready"], TT * (1 if n == 1 else 2))
            rms(n)
            for t in range(TT):
                ts(xn2[:, t, :], xres[:, t, :], rstd[:, t:t + 1], sem=S["xn3_ready"])

        temp4 = acc[:].rearrange("p (a n) -> p a n", a=4)
        scale_x(1)
        affine_lo("h3", "nmp", temp4)
        dve.wait_ge(load["strip"], 16)
        dve.wait_ge(load["tabs"], 80)
        tt(strip[:], strip[:], future[:].unsqueeze(1).to_broadcast([P, N_HEADS, SEQ]), ALU.add)

        def windows(kv):
            j = "kv".index(kv)
            pe_at = COLS["pe_" + kv]
            if j:
                await_full(dve, ("hidden", "k"))
            for g in range(N_KV):
                rows = slice(HD * g, HD * g + HD)
                x = kvc[rows, j, :].rearrange("p (m l o) -> p o l m", l=8, o=2)
                for odd in range(2):
                    for half in range(2):
                        pe_c = pc[rows, pe_at + 16 * half + odd:pe_at + 16 * half + 16:2]
                        tt(blk[HD * odd:HD * odd + HD, 8 * half:8 * half + 8, N_CMP * g:N_CMP * g + N_CMP],
                           x[:, odd, :, half:half + N_CMP], pe_c.unsqueeze(2).to_broadcast([HD, 8, N_CMP]), ALU.add,
                           sem=S["blk_ready"])

        await_drained(dve, ("cmp", 1), "act")
        windows("k")
        windows("v")
        await_drained(dve, ("gates", 0), "act")
        for h in range(N_HEADS):
            ts(gate[:, 0, 3 * h:3 * h + 1], gate[:, 0, 3 * h:3 * h + 1], col("has_key"))

        for n, name in enumerate(SLOT_UNITS):
            for slot in slots_of(n):
                if 0 <= slot < len(ITEMS):
                    br, h, i = ITEMS[slot]
                    x, w = slot % 3, n_keys(slot)
                    at = 384 - P * i
                    bias = strip[:, h, at:at + w] if br != "cmp" else strip[:, h, at + L_CMP - 1:SEQ:S_CMP]
                    await_full(dve, ("scores", slot))
                    if slot >= 3:
                        await_full(dve, ("turn2", slot - 3))
                    d.step(V.tensor_tensor_reduce(out=scores[x][:, 0:w], in0=bank(("scores", slot))[:, 0:w], in1=bias,
                                                  scale=1.0, scalar=3e38, op0=ALU.add, op1=ALU.min,
                                                  accum_out=low[:, x:x + 1]), drain(("scores", slot), "dve"))
                    d.step(V.tensor_copy(low[:, x:x + 1], low[:, x:x + 1]), S["low_ready"])
                if 0 <= slot - 3 < len(ITEMS):
                    item = slot - 3
                    br, h, i = ITEMS[item]
                    part = ("cmp", "slc", "win").index(br)
                    oh = o[:, i, HD * h:HD * h + HD]
                    b = bank(("values", item))[:, 0:HD]
                    await_full(dve, ("values", item))
                    if br == "slc":
                        ts(oh, b, weights4[:, item % 4:item % 4 + 1], sem=drain(("values", item), "dve"))
                    else:
                        stt(oh, b, weights4[:, item % 4:item % 4 + 1], oh, ALU.mult, ALU.add, sem=drain(("values", item), "dve"))
                if 0 <= slot - 1 < len(ITEMS):
                    item = slot - 1
                    br, h, i = ITEMS[item]
                    part = ("cmp", "slc", "win").index(br)
                    dve.wait_ge(S["exp_done"], item + 1)
                    d.step(V.reciprocal(weights4[:, item % 4:item % 4 + 1], den[:, item % 3:item % 3 + 1]))
                    ts(weights4[:, item % 4:item % 4 + 1], weights4[:, item % 4:item % 4 + 1],
                       gate[:, i, 3 * h + part:3 * h + part + 1], sem=S["weight_ready"])
            if name[:2] == "xt":
                for j in range(2):
                    k = 2 * int(name[2]) + j
                    await_full(dve, (name, j))
                    tt(cgT[:, k, :], bank((name, j))[:], cgT[:, k, :], ALU.mult, sem=drain((name, j), "dve"))
                    ts(conv_t, cgT[:, k, :], col("cmix", 8 + k))
                    stt(conv_t[:, 1:], cgT[:, k, 0:SEQ - 1], col("cmix", 4 + k), conv_t[:, 1:], ALU.mult, ALU.add)
                    stt(conv_t[:, 2:], cgT[:, k, 0:SEQ - 2], col("cmix", k), conv_t[:, 2:], ALU.mult, ALU.add)
                    tt(bgT[:, k, :], bgT[:, k, :], conv_t, ALU.mult, sem=S["conv_ready"])
        for k in range(PAIRS):
            await_full(dve, ("turn_o", k))
            await_drained(dve, ("turn_o", k), "act")
            tt(act_lo[:, k, :], bank(("turn_o", k))[:], act_hi[:, k, :].bitcast(F32), ALU.subtract, sem=drain(("turn_o", k), "dve"))
        dve.wait_ge(S["y2_hi"], 1)
        tt(act_lo[:, 4:8, :], bgT[:], act_hi[:, 4:8, :].bitcast(F32), ALU.subtract, sem=S["y2_lo"])

        def add_rms(stage, n, row, temp, sem):
            await_full(dve, (stage, TT - 1, 1))
            await_drained(dve, (stage, TT - 1, 1), "act")
            tt(rstd[:], squares[:].rearrange("p (t j) -> p t j", j=2)[:, :, 0],
               squares[:].rearrange("p (t j) -> p t j", j=2)[:, :, 1], ALU.add)
            rms(n)
            for t in range(TT):
                for j in range(2):
                    h = slice(SEQ * j, SEQ * j + SEQ)
                    await_drained(dve, (stage, t, j), "act")
                    stt(temp[:, h], bank((stage, t, j))[:], rstd[:, t:t + 1], row[:, h], ALU.mult, ALU.mult,
                        sem=drain((stage, t, j), "dve"))
                tt(xres[:, t, :], xres[:, t, :], temp[:], ALU.add, sem if t == TT - 1 else None)

        dve.wait_ge(load["rows3"], 16)
        add_rms("mix2", 2, row3, rms_t, S["x_ready"])
        scale_x(3)
        affine_lo("h4", "nfp", temp4)
        for m in range(FT):
            name = f"up2_{m}"
            pair = [acc[:, SEQ * (2 * (m % 2) + j):SEQ * (2 * (m % 2) + j) + SEQ] for j in range(2)]
            for j in range(2):
                await_full(dve, (name, j))
                await_drained(dve, (name, j), "act")
                c = FT * j + m
                stt(pair[j][:, 1:], bank((name, j))[:, 0:SEQ - 1], col("cffn", 2 * FT + c), pair[j][:, 1:], ALU.mult, ALU.add)
                stt(pair[j][:, 2:], bank((name, j))[:, 0:SEQ - 2], col("cffn", c), pair[j][:, 2:], ALU.mult, ALU.add,
                    sem=drain((name, j), "dve"))
            dve.wait_ge(S["gelu2"], m + 1)
            tt(pair[1], pair[1], pair[0], ALU.mult, sem=S["prod2"])
            dve.wait_ge(S["hid2_hi"], m + 1)
            tt(hid_lo[:, m, :], pair[1], hid_hi[:, m, :].bitcast(F32), ALU.subtract, sem=S["hid2_lo"])
        dve.wait_ge(load["rows4"], 16)
        add_rms("ff2", 4, row4, rms_t2, S["out_ready"])

    def second_pe(pe, three, next_unit, dense_feature, dense_token, dense_rows, turn_x, fill):
        pe.wait_ge(S["xn3_ready"], TT)
        turn_x("h3", xn2)
        pe.wait_ge(load["tabs"], 80)
        for j, n in enumerate((SEQ, GRID - SEQ)):
            claim(pe, ("bias", j))
            fill(("bias", j), pe.matmul(bank(("bias", j))[0:N_HEADS, 0:n], relb[0:N_BUCKETS, :],
                                        onehot[0:N_BUCKETS, SEQ * j:SEQ * j + n], start=True, stop=True))
        pe.wait_ge(S["h_lo"], 3 * KC)

        def compress(kv):
            j = "kv".index(kv)
            pe.wait_ge(load["w1"], 16 * (j + 1))
            pe.wait_ge(S["blk_ready"], 8 * (j + 1))
            claim(pe, ("hidden", kv))
            b = bank(("hidden", kv))
            for half in range(2):
                for l in range(L_CMP // 2):
                    mm = pe.matmul(b[:, 2 * N_CMP * half:2 * N_CMP * half + 2 * N_CMP], w1[:, l, P * half:P * half + P],
                                   blk[:, l, :], start=l == 0, stop=l == L_CMP // 2 - 1)
            fill(("hidden", kv), mm)
            claim(pe, ("compressed", kv))
            await_drained(pe, ("hidden", kv), "act")
            b = bank(("compressed", kv))
            for g in range(1 if kv == "k" else N_KV):
                for half in range(2):
                    if kv == "k":
                        mm = pe.matmul(b[:, 0:2 * N_CMP], w2k[:, half, :], hc[:, half, :], start=half == 0, stop=half == 1)
                    else:
                        mm = pe.matmul(b[0:N_CMP, HD * g:HD * g + HD], hc[:, half, N_CMP * g:N_CMP * g + N_CMP],
                                       w2v[:, half, :], start=half == 0, stop=half == 1)
            fill(("compressed", kv), mm)

        def keys_and_values(name):
            (hi, lo), w = next_unit(name)
            claim(pe, (name, 0))
            for k in range(KC):
                mm = three(bank((name, 0))[:], (hi[:, k, 0:P], lo[:, k, 0:P]), (act_hi[:, k, :], act_lo[:, k, :]),
                           k == 0, k == KC - 1)
            fill((name, 0), mm)
            claim(pe, (name, 1))
            for t in range(TT):
                for k in range(KC):
                    mm = three(bank((name, 1))[:, tok(t)], (act_hi[:, k, tok(t)], act_lo[:, k, tok(t)]),
                               (hi[:, k, P:], lo[:, k, P:]), k == 0, k == KC - 1)
            mm.then_inc(full_sem((name, 1))[0], 1)

        for name in FIRST_UNITS:
            if name in ("slc", "win"):
                keys_and_values(name)
            elif name == "gates":
                dense_token(name, TT)
            else:
                dense_feature(name, 2)
            if name in ("q1", "win"):
                compress("k" if name == "q1" else "v")

        def attention(slot):
            for st, item in stages_of(slot):
                br, h, i = ITEMS[item]
                g, rows, w = h // REP, slice(HD * (h % 2), HD * (h % 2) + HD), n_keys(item)
                b = bank((st, item))
                claim(pe, (st, item))
                if st == "scores":
                    keys = kc2[rows, g, 0:w] if br == "cmp" else (ksl if br == "slc" else kwn)[rows, g, 0:w]
                    mm = pe.matmul(b[:, 0:w], qT[rows, h // 2, tok(i)], keys, start=True, stop=True)
                elif st == "turn2":
                    pe.wait_ge(S["exp_done"], item + 1)
                    x = scores[item % 3]
                    for j in range(-(-w // P)):
                        n = min(P, w - P * j)
                        mm = pe.transpose(b[0:n, tok(j)], x[:, P * j:P * j + n], ident[:])
                else:
                    await_drained(pe, ("turn2", item), "act")
                    for j in range(-(-w // P)):
                        n = min(P, w - P * j)
                        values = vc[0:n, g, :] if br == "cmp" else (vsl if br == "slc" else vwn)[:, j, HD * g:HD * g + HD]
                        mm = pe.matmul(b[:, 0:HD], probsT[item % 2][0:n, tok(j)], values, start=j == 0, stop=j == -(-w // P) - 1)
                fill((st, item), mm)

        await_drained(pe, ("win", 1), "act")
        await_drained(pe, ("compressed", "v"), "act")
        for n, name in enumerate(SLOT_UNITS):
            slots = list(slots_of(n))
            steps = 2 * KC
            dense_feature(name, 2, lambda k: [attention(s) for s in slots[k * len(slots) // steps:(k + 1) * len(slots) // steps]])
        for k in range(PAIRS):
            claim(pe, ("turn_o", k))
            await_drained(pe, ("values", len(ITEMS) - 1), "dve")
            for t in range(TT):
                mm = pe.transpose(bank(("turn_o", k))[:, tok(t)], o[:, t, P * k:P * k + P], ident[:])
            fill(("turn_o", k), mm)
        pe.wait_ge(S["y2_lo"], 1)
        dense_rows("mix2", "out2", 4, act_hi, act_lo, None)
        pe.wait_ge(S["xn3_ready"], 2 * TT)
        turn_x("h4", xn2)
        pe.wait_ge(S["h_lo"], 4 * KC)
        for m in range(FT):
            dense_feature(f"up2_{m}", 2)
        pe.wait_ge(S["hid2_lo"], FT)
        dense_rows("ff2", "down2", FT // 2, hid_hi, hid_lo, None)

    block = ctx.enter_context(nc.Block())
    W_IN1 = ("lora0", "lora1", "k0", "k1", "r0", "r1", "v0", "v1", "pu0", "pu1", "pv0", "pv1")
    CHUNK_TILES = ((0, 1), (2, 3))

    def finish(sp):
        sp.wait_ge(S["out_ready"], 1)
        sp.dma_start(out.rearrange("b (t p) d -> p (b t) d", p=P), xres[:]).then_inc(load["out"], 16)
        sp.wait_ge(load["out"], 16)

    @block.sync
    def _(sp):
        sp.dma_start(xres[:], src["x"].rearrange("b (t p) d -> p (b t) d", p=P)).then_inc(load["x"], 16)
        sp.dma_start(pc[:], src["params"]).then_inc(load["params"], 16)
        at, n = CONSTS["ident"]
        sp.dma_start(ident[:], const("ident")).then_inc(load["consts"], 16)
        sp.dma_start(bd64[:], const("bd64")).then_inc(load["consts"], 16)
        for n in range(len(UNITS)):
            if n >= RAW:
                m = n - RAW
                if m in SPLIT_AT:
                    sp.wait_ge(lo_ready, SPLIT_AT[m] + 1)
                else:
                    sp.wait_ge(ada_used, m - sum(1 for i in SPLIT_UNITS if i < m) + 1)
            sp.dma_start(raw[n % RAW][:, :UNIT_SIZE[n]],
                         src["weights"][:, UNIT_START[n]:UNIT_START[n + 1]]).then_inc(raw_landed[n % RAW], 16)
        finish(sp)

    @block.gpsimd
    def _(pool):
        for i, n in enumerate(SPLIT_UNITS):
            pool.wait_ge(hi_ready, i + 1)
            size = UNIT_SIZE[n]
            pool.tensor_tensor(wlo[i % SPLIT][:, :size], raw[n % RAW][:, :size], whi[i % SPLIT][:, :size],
                               ALU.subtract).then_inc(lo_ready, 1)

    @block.scalar
    def _(act):
        a = Order(act, act_step)
        at = [0]

        def convert():
            i = at[0]
            at[0] += 1
            if i == len(SPLIT_UNITS):
                return
            n = SPLIT_UNITS[i]
            raw_ready(act, n)
            if i >= SPLIT:
                act.wait_ge(unit_used, i - SPLIT + 1)
            a.done(act.activation(whi[i % SPLIT][:, :UNIT_SIZE[n]], raw[n % RAW][:, :UNIT_SIZE[n]], ACT.Copy),
                   hi_ready)

        act.dma_start(up[:], const("up")).then_inc(load["gmlp"], 16)
        act.dma_start(wsT[:], src["w_s_t"]).then_inc(load["gmlp"], 16)
        act.dma_start(bs[:], src["b_s"].partition_broadcast(P)).then_inc(load["gmlp"], 16)
        act.dma_start(sg_g[:], src["sg_ln_g"].partition_broadcast(P)).then_inc(load["gmlp"], 16)
        act.dma_start(sg_b[:], src["sg_ln_b"].partition_broadcast(P)).then_inc(load["gmlp"], 16)
        act.dma_start(row_a[:], src["emb_ln_g"].partition_broadcast(P)).then_inc(load["rows0"], 16)
        act.dma_start(row_b[:], src["emb_ln_b"].partition_broadcast(P)).then_inc(load["rows0"], 16)
        act.dma_start(wup[:], src["lora_up"]).then_inc(load["masks"], 16)
        act.dma_start(gup[:], src["g_up_pad"]).then_inc(load["masks"], 16)
        act.dma_start(masks[:, 0:2, :], const("mask_qr").rearrange("p (a b) -> p a b", a=2)).then_inc(load["masks"], 16)
        act.dma_start(masks[:, 2:4, :], const("mask_mk").rearrange("p (a b) -> p a b", a=2)).then_inc(load["masks"], 16)
        act.dma_start(mask_d[:], const("mask_d")).then_inc(load["masks"], 16)
        act.dma_start(mask_e[:], const("mask_e")).then_inc(load["masks"], 16)
        act.dma_start(chunk_rows[:], const("chunk_rows")).then_inc(load["masks"], 16)
        act.dma_start(bias4[:], src["b_gates"]).then_inc(load["bias"], 16)

        act.wait_ge(load["params"], 16)
        a.done(act.activation(pc[:, COLS["c"]:COLS["c"] + KC], pc[:, COLS["c"]:COLS["c"] + KC], ACT.Silu), S["silu_c"])
        act.wait_ge(S["var1"], 1)
        a.done(act.activation(rstd[:], rstd[:], ACT.Sqrt), S["root1"])

        def affine_hi(stage, part):
            if isinstance(part, str):
                for k in range(KC):
                    await_full(act, (stage, k))
                    a.done(act.activation(act_hi[:, k, :], bank((stage, k))[:], ACT.Copy, scale=col(part, k)),
                           drain((stage, k), "act"))
                return
            act.wait_ge(S["affine1"], part // 2 + 1)
            for k in range(KC):
                await_full(act, (stage, k))
                a.done(act.activation(act_hi[:, k, :], bank((stage, k))[:], ACT.Identity,
                                      bias=affine[:, part + 1, k:k + 1], scale=affine[:, part, k:k + 1]),
                       drain((stage, k), "act"))

        convert()
        affine_hi("h1", 0)

        def unshifted(name, j, dest, mu):
            await_full(act, (name, j))
            a.done(act.activation(dest, bank((name, j))[:], ACT.Copy, scale=omu[:, mu:mu + 1]), drain((name, j), "act"))

        def prep_act(p):
            await_full(act, ("z", p))
            a.done(act.activation(sig[:], bank(("z", p))[:], ACT.Sigmoid, bias=col("w0", p)), drain(("z", p), "act"))
            await_full(act, ("a", p))
            a.done(act.activation(aa[:], bank(("a", p))[:], ACT.Sigmoid, bias=col("a0", p)), drain(("a", p), "act"))

        def prep_act_b(p):
            act.wait_ge(S["ss_ready"], p + 1)
            a.done(act.activation(sq[:], sq[:], ACT.Sqrt), S["root_ready"])
            act.wait_ge(S["cs_ready"], p + 1)
            a.done(act.activation(ep[:], cs[:], ACT.Exp, scale=-DECAY), S["exp_ready"])
            a.step(act.activation(sig[:], sig[:], ACT.Exp, scale=-DECAY), S["exp_ready"])
            a.done(act.activation(cs[:], cs[:], ACT.Exp, scale=DECAY), S["exp_ready"])

        for name in W_IN1:
            if name != W_IN1[-1]:
                convert()
            if name in ("lora0", "lora1"):
                for j in range(2 if name == "lora0" else 1):
                    m = j if name == "lora0" else 2
                    unshifted(name, j, lora[:] if m == 0 else gd[:, m - 1, :], m)
                if name == "lora1":
                    act.wait_ge(S["shift_ready"], 3)
                    a.done(act.activation(lora[0:HD, :], lora[0:HD, :], ACT.Tanh), S["lora_ready"])
                    a.done(act.activation(gd[:], gd[:], ACT.Sigmoid), S["lora_ready"])
            elif name[0] in "krv":
                dest, mu = {"k": (kT, 3), "v": (vT, 7), "r": (rT, 11)}[name[0]]
                for j in range(2):
                    n = 2 * int(name[1]) + j
                    unshifted(name, j, dest[:, n, :], mu + n)
                if name == "v1":
                    prep_act(0)
            elif name[:2] == "pu":
                for j in range(2):
                    await_full(act, (name, j))
                    a.done(act.activation(uT[:, 2 * int(name[2]) + j, :], bank((name, j))[:], ACT.Gelu_apprx_tanh),
                           drain((name, j), "act"))
                if name == "pu0":
                    prep_act_b(0)
            else:
                half = slice(256 * int(name[2]), 256 * int(name[2]) + 256)
                for j in range(2):
                    await_full(act, (name, j))
                    a.done(act.activation(pv[:, 2 * j:2 * j + 2, half], bank((name, j))[:].rearrange("p (t d) -> p t d", t=2),
                                          ACT.Gelu_apprx_tanh), drain((name, j), "act"))
        act.wait_ge(S["pv_std"], 1)
        a.done(act.activation(rstd[:], rstd[:], ACT.Sqrt), S["pv_root"])

        def chunk_act(p, t, stage):
            d = sets[t % 2]
            if stage not in ("turn", "mv", "q2", "n4", "q4", "r2", "z1", "yl"):
                return
            b = bank((stage, p, t))
            await_full(act, (stage, p, t))
            done = lambda ins: a.done(ins, drain((stage, p, t), "act"))
            copy = lambda o, i: done(act.activation(o, i, ACT.Copy))
            if stage == "turn":
                if (p, t) == (0, 0):
                    act.wait_ge(S["sets_ready"], 1)
                copy(d["z0"][:].rearrange("p (a b) -> p a b", b=HD)[:, 0:4:3, :],
                     b[:, 0:P].rearrange("p (a b) -> p a b", b=HD))
                copy(d["vz"][:, HD:HD + P], b[:, 3 * P:4 * P])
            elif stage == "mv":
                copy(d["z0"][:, HD:HD + P], b[:, 0:P])
            elif stage == "q2":
                copy(d["rq"][:, :, 1, :], b[:, 0:256].rearrange("p (h n) -> p h n", h=2))
                copy(d["nn"][:], b[:, 256:512].rearrange("p (h n) -> p h n", h=2))
            elif stage == "n4":
                copy(d["nd"][:], b[:, 0:256].rearrange("p (h n) -> p h n", h=2))
            elif stage == "q4":
                copy(d["rq"][:, :, 1, :], b[:].rearrange("p (h a n) -> p h a n", h=2, a=2)[:, :, 1, :])
            elif stage == "r2":
                copy(d["nn"][:], b[:, 256:512].rearrange("p (h n) -> p h n", h=2))
            elif stage == "z1":
                copy(d["nd"][:], b[:, 0:256].rearrange("p (h n) -> p h n", h=2))
            elif stage == "yl":
                copy(d["yl"][0:HD, :], b[HD:P, 0:P])
                copy(d["yl"][HD:P, :], b[0:HD, P:2 * P])

        for p in range(PAIRS):
            if p:
                prep_act(p)
                prep_act_b(p)
            await_full(act, ("g", p))
            a.done(act.activation(kT[:, p, :], bank(("g", p))[:], ACT.Copy), drain(("g", p), "act"))
            for tiles in CHUNK_TILES:
                for stage, _ in CHUNK_STAGES:
                    for t in tiles:
                        chunk_act(p, t, stage)
            act.wait_ge(S["var_ready"], p + 1)
            a.done(act.activation(sq[:], sq[:], ACT.Sqrt), S["root_ready"])

        act.wait_ge(S["yb_ready"], PAIRS)
        await_full(act, ("state", PAIRS - 1, TT - 1, NCH - 1))
        a.done(act.activation(act_hi[:, 0:4, :], uT[:], ACT.Copy), S["y_hi"])
        a.done(act.activation(act_hi[:, 4:8, :], vT[:], ACT.Copy), S["y_hi"])
        act.dma_start(row_a[:], src["ln1_g"].partition_broadcast(P)).then_inc(load["rows1"], 16)
        act.dma_start(row_b[:], src["ln1_b"].partition_broadcast(P)).then_inc(load["rows1"], 16)
        for j in range(4):
            await_full(act, ("mod_rows", j))
            a.done(act.activation(acc[:, SEQ * j:SEQ * j + SEQ], bank(("mod_rows", j))[:], ACT.Copy), drain(("mod_rows", j), "act"))
        for n in range(5):
            convert()
        act.wait_ge(S["var1"], 2)
        a.done(act.activation(rstd[:], rstd[:], ACT.Sqrt), S["root1"])
        affine_hi("h2", 2)

        def ffn_first(m):
            convert()
            name = f"up1_{m}"
            await_full(act, (name, 0))
            a.done(act.activation(acc[:, 0:SEQ], bank((name, 0))[:], ACT.Silu), drain((name, 0), "act"))
            await_drained(act, (name, 1), "dve")
            a.done(act.activation(hid_hi[:, m, :], acc[:, SEQ:2 * SEQ], ACT.Copy), S["hid_hi_ready"])

        for m in range(FT):
            ffn_first(m)
        for n in range(FT // 2):
            convert()
            if n == 0:
                await_full(act, (f"up1_{FT - 1}", 1))
                act.dma_start(row2_a[:], src["ln2_g"].partition_broadcast(P)).then_inc(load["rows2"], 16)
                act.dma_start(row2_b[:], src["ln2_b"].partition_broadcast(P)).then_inc(load["rows2"], 16)
        act.wait_ge(S["var1"], 3)
        a.done(act.activation(rstd[:], rstd[:], ACT.Sqrt), S["root1"])

        second_act(act, a, convert, affine_hi)

    @block.vector
    def _(dve):
        d = Order(dve, dve_step)
        V = dve
        counts = {"ada": 0}

        def ts(out, in0, s1, s2=None, op0=ALU.mult, op1=None, sem=None):
            d.step(V.tensor_scalar(out, in0, s1, s2, op0, op1) if op1 is not None else
                   V.tensor_scalar(out, in0, s1, None, op0), sem)

        def tt(out, a, b, op, sem=None):
            d.step(V.tensor_tensor(out, a, b, op), sem)

        def stt(out, a, s, b, op0, op1, sem=None):
            d.step(V.scalar_tensor_tensor(out=out, in0=a, scalar=s, in1=b, op0=op0, op1=op1), sem)

        def ada():
            i = counts["ada"]
            counts["ada"] += 1
            n = UNIT_AT[f"ada{i // KC}_{i % KC}"]
            raw_ready(dve, n)
            if i == 0:
                dve.wait_ge(S["silu_c"], 1)
            c = col("c", i % KC)
            r = raw[n % RAW][:]
            if i % KC == 0:
                ts(acc[:], r, c, sem=ada_used)
            else:
                stt(acc[:], r, c, acc[:], ALU.mult, ALU.add, sem=ada_used)

        def layer_stats(t, source):
            d.step(V.bn_stats(stats[:, 0, :], source[:, 0:512]))
            d.step(V.bn_stats(stats[:, 1, :], source[:, 512:1024]))
            d.step(V.bn_aggr(mv[:, t, :], stats[:]))

        def normalise():
            n = counts["norm"] = counts.get("norm", 0) + 1
            ts(rstd[:], mv[:, :, 1], LN_EPS, op0=ALU.add, sem=S["var1"])
            dve.wait_ge(S["root1"], n)
            d.step(V.reciprocal(rstd[:], rstd[:]))
            for t in range(TT):
                ts(xres[:, t, :], xres[:, t, :], mv[:, t, 0:1], rstd[:, t:t + 1], ALU.subtract, ALU.mult,
                   sem=S["xn_ready"])

        def affine_rows(g, b, sem=None):
            for t in range(TT):
                tt(xres[:, t, :], xres[:, t, :], g[:], ALU.mult)
                tt(xres[:, t, :], xres[:, t, :], b[:], ALU.add, sem if t == TT - 1 else None)

        def affine_lo(stage, part, temp):
            for k in range(KC):
                full = temp[:, k % 2, :]
                await_full(dve, (stage, k))
                await_drained(dve, (stage, k), "act")
                if isinstance(part, str):
                    ts(full, bank((stage, k))[:], col(part, k), sem=drain((stage, k), "dve"))
                    tt(act_lo[:, k, :], full, act_hi[:, k, :].bitcast(F32), ALU.subtract, sem=S["h_lo"])
                    continue
                ts(full, bank((stage, k))[:], affine[:, part, k:k + 1], affine[:, part + 1, k:k + 1],
                   ALU.mult, ALU.add, sem=drain((stage, k), "dve"))
                tt(act_lo[:, k, :], full, act_hi[:, k, :].bitcast(F32), ALU.subtract, sem=S["h_lo"])

        def mod_columns(jobname, part, g, b, sh, sc):
            await_full(dve, jobname)
            tt(modc[:], bank(jobname)[:, 0:2 * KC], pc[:, COLS[sh]:COLS[sh] + 2 * KC], ALU.add, sem=drain(jobname, "dve"))
            ts(modc[:, KC:], modc[:, KC:], 1.0, op0=ALU.add)
            tt(affine[:, part, :], pc[:, COLS[g]:COLS[g] + KC], modc[:, KC:], ALU.mult)
            tt(affine[:, part + 1, :], pc[:, COLS[b]:COLS[b] + KC], modc[:, KC:], ALU.mult)
            tt(affine[:, part + 1, :], affine[:, part + 1, :], modc[:, 0:KC], ALU.add, sem=S["affine1"])

        d.step(V.memset(ones[:], 1.0))
        d.step(V.memset(restart[:], 1.0))
        d.step(V.memset(restart[:].rearrange("p (c t) -> p c t", t=CH)[:, :, 0:1], 0.0))
        dve.wait_ge(load["params"], 16)
        ts(omu[:], pc[:, COLS["mu_l"]:COLS["mu_l"] + N_MU], -1.0, 1.0, ALU.mult, ALU.add)
        ts(oka[:], pc[:, COLS["k_a"]:COLS["k_a"] + 4], -1.0, 1.0, ALU.mult, ALU.add)
        dve.wait_ge(load["x"], 16)
        for t in range(TT):
            layer_stats(t, xres[:, t, :])
        normalise()
        for i in range(KC):
            ada()
        mod_columns("cols0", 0, "emb_g", "emb_b", "b_sh1", "b_sc1")
        affine_lo("h1", 0, ar)
        dve.wait_ge(load["rows0"], 32)
        affine_rows(row_a, row_b)

        def shifted(name, j, dest, mu, sem=None):
            await_drained(dve, (name, j), "act")
            stt(dest[:, 1:SEQ], bank((name, j))[:, 0:SEQ - 1], pc[:, COLS["mu_l"] + mu:COLS["mu_l"] + mu + 1],
                dest[:, 1:SEQ], ALU.mult, ALU.add, sem=drain((name, j), "dve"))

        def prep_dve(p):
            ts(kk[:], kT[:, p, :], col("k_k", p))
            tt(sq[:], kk[:], kk[:], ALU.mult, sem=S["kk_sq"])
            await_drained(dve, ("z", p), "act")
            d.step(V.tensor_tensor_scan(cs[:], restart[:], sig[:], 0.0, ALU.mult, ALU.add))
            tt(sig[:], cs[:], sig[:], ALU.subtract, sem=S["cs_ready"])
            await_full(dve, ("kk", p))
            ts(sq[:], bank(("kk", p))[:], 1e-24, op0=ALU.max, sem=drain(("kk", p), "dve"))
            d.step(V.tensor_copy(sq[:, 0:1], sq[:, 0:1]), S["ss_ready"])

        def prep_dve_b(p):
            dve.wait_ge(S["root_ready"], 2 * p + 1)
            d.step(V.reciprocal(sq[:], sq[:]))
            tt(kk[:], kk[:], sq[:], ALU.mult)
            dve.wait_ge(S["exp_ready"], 3 * p + 3)
            stt(ar[:, 0, :], kk[:], -1.0, sig[:], ALU.mult, ALU.mult)
            tt(ar[:, 1, :], rT[:, p, :], ep[:], ALU.mult)
            d.step(V.tensor_copy(pend[:], ep[:, CH - 1:SEQ:CH]))
            await_drained(dve, ("a", p), "act")
            ts(ep[:], aa[:], col("k_a", p), oka[:, p:p + 1], ALU.mult, ALU.add)
            tt(kT[:, p, :], kT[:, p, :], ep[:], ALU.mult)
            tt(aa[:], kk[:], aa[:], ALU.mult)
            tt(bt[:], aa[:], cs[:], ALU.mult)
            tt(kt[:], kT[:, p, :], cs[:], ALU.mult)
            stt(rT[:, p, :], rT[:, p, :], col("r_k", p), kT[:, p, :], ALU.mult, ALU.mult, sem=S["prep_ready"])
            ends = pend[:].unsqueeze(2).to_broadcast([P, SEQ // CH, CH])
            tt(sig[:].rearrange("p (c t) -> p c t", t=CH), bt[:].rearrange("p (c t) -> p c t", t=CH), ends, ALU.mult)
            tt(cs[:].rearrange("p (c t) -> p c t", t=CH), kt[:].rearrange("p (c t) -> p c t", t=CH), ends, ALU.mult,
               sem=S["bars_ready"])

        for n, name in enumerate(W_IN1):
            if name in ("lora0", "lora1"):
                for j in range(2 if name == "lora0" else 1):
                    m = j if name == "lora0" else 2
                    shifted(name, j, lora[:] if m == 0 else gd[:, m - 1, :], m)
                    d.step(V.tensor_copy(stats[:, 0, 0:1], stats[:, 0, 0:1]), S["shift_ready"])
            elif name[0] in "krv":
                dest, mu = {"k": (kT, 3), "v": (vT, 7), "r": (rT, 11)}[name[0]]
                for j in range(2):
                    m = 2 * int(name[1]) + j
                    shifted(name, j, dest[:, m, :], mu + m)
            ada()
            if n == KC - 1:
                d.step(V.tensor_copy(stats[:, 0, 0:1], stats[:, 0, 0:1]), S["acc1"])
                mod_columns("cols1", 2, "ln1_g", "ln1_b", "b_sh2", "b_sc2")
                dve.wait_ge(load["gmlp"], 80)
                tt(wsT[:], wsT[:], up[:].unsqueeze(1).to_broadcast([P, 4, P]), ALU.mult, sem=S["wst_ready"])
                prep_dve(0)
            if name == "pu1":
                prep_dve_b(0)

        for t in range(TT):
            await_drained(dve, ("pv1", t // 2), "act")
            d.step(V.bn_stats(stats[:, 0, :], pv[:, t, :]))
            d.step(V.bn_aggr(mv[:, t, :], stats[:, 0:1, :]))
        ts(rstd[:], mv[:, :, 1], LN_EPS, op0=ALU.add, sem=S["pv_std"])
        dve.wait_ge(S["pv_root"], 1)
        d.step(V.reciprocal(rstd[:], rstd[:]))
        for t in range(TT):
            ts(pv[:, t, :], pv[:, t, :], mv[:, t, 0:1], rstd[:, t:t + 1], ALU.subtract, ALU.mult)
            tt(pv[:, t, :], pv[:, t, :], sg_g[:], ALU.mult)
            tt(pv[:, t, :], pv[:, t, :], sg_b[:], ALU.add, sem=S["pv_ready"])
        for g in range(4):
            await_full(dve, ("sgu", g))
            tt(sg_g[:].rearrange("p (t n) -> p t n", n=P), bank(("sgu", g))[:].rearrange("p (t n) -> p t n", n=P),
               bs[:, g, :].unsqueeze(1).to_broadcast([P, TT, P]), ALU.add, sem=drain(("sgu", g), "dve"))
            tt(uT[:, g, :], uT[:, g, :], sg_g[:], ALU.mult)
        await_full(dve, ("pv1", 1))
        for q in range(2):
            d.step(V.memset(sets[q]["vz"][:], 0.0))
        d.step(V.tensor_copy(stats[:, 0, 0:1], stats[:, 0, 0:1]), S["sets_ready"])

        def heads(ap):
            return ap.rearrange("p (h n) -> p h n", h=2)

        def chunk_dve(p, t, stage):
            s = sets[t % 2]
            name = (stage, p, t)
            if stage in ("mv", "q2", "n4"):
                return
            b = bank(name)
            await_full(dve, name)
            if stage in ("turn", "q4", "r2", "z1", "yl"):
                await_drained(dve, name, "act")
            out_ = drain(name, "dve")
            if stage == "turn":
                rows = chunk_rows[:].unsqueeze(2).to_broadcast([P, NCH, P])
                for key, part in (("bx", 1), ("kx", 2)):
                    tt(s[key][:], b[:, part * P:part * P + P].unsqueeze(1).to_broadcast([P, NCH, P]), rows,
                       ALU.mult, sem=out_)
            elif stage in ("m1", "m2"):
                h = int(stage[1]) - 1
                tt(s["mm"][:, h], b[:].rearrange("p (a n) -> p a n", a=4), masks[:], ALU.mult, sem=out_)
            elif stage in ("n1", "n2"):
                h = int(stage[1]) - 1
                tt(s["nd"][:, h, :], b[:, 0:P], mask_d[:], ALU.mult, sem=out_)
                tt(s["ee"][:, h, :], b[:, 0:P], mask_e[:], ALU.mult, sem=out_)
                if h:
                    tt(s["rq"][:, :, 0, :], s["mm"][:, :, 0, :], ident[:].unsqueeze(1).to_broadcast([P, 2, P]),
                       ALU.add, sem=S["r0_ready"])
            elif stage == "q4":
                tt(s["rb"][:], b[:].rearrange("p (h a n) -> p h a n", h=2, a=2)[:, :, 0, :], s["rq"][:, :, 0, :],
                   ALU.add, sem=out_)
            elif stage == "r2":
                tt(s["rq"][:, :, 0, :], heads(b[:, 0:256]), s["rb"][:], ALU.add, sem=out_)
            elif stage == "r3":
                tt(s["rb"][:], heads(b[:, 0:256]), s["rq"][:, :, 0, :], ALU.add, sem=out_)
            elif stage == "z1":
                d.step(V.tensor_copy(s["z1"][:], b[:, 256:512]), out_)
            elif stage == "z2":
                tt(s["z"][:], b[:, 0:256], s["z1"][:], ALU.add, sem=out_)
                d.step(V.tensor_copy(s["nn"][:, 0, :].rearrange("p (a b) -> p a b", b=HD),
                                     s["z"][:].rearrange("p (a b) -> p a b", b=HD)[:, 0:4:3, :]), S["w_ready"])
            elif stage == "yl":
                tt(s["rp"][0:HD, :], b[0:HD, 0:P], ar[0:HD, 1, tok(t)], ALU.add, sem=out_)
                tt(s["rp"][HD:P, :], b[HD:P, P:2 * P], ar[HD:P, 1, tok(t)], ALU.add, sem=out_)
            elif stage in ("gt", "hh"):
                tt(s["gt" if stage == "gt" else "hb"][:], b[:].rearrange("p (c n) -> p c n", c=NCH),
                   bd64[:].unsqueeze(1).to_broadcast([P, NCH, P]), ALU.mult, sem=out_)

        for p in range(PAIRS):
            if p:
                prep_dve(p)
                prep_dve_b(p)
            if p == 0:
                dve.wait_ge(load["masks"], 16 * 7)
            d.step(V.memset(state[0][:], 0.0), S["state_zero"])
            await_full(dve, ("bonus", p))
            tt(rT[:, p, :], bank(("bonus", p))[:], vT[:, p, :], ALU.mult, sem=drain(("bonus", p), "dve"))
            for tiles in CHUNK_TILES:
                for stage, _ in CHUNK_STAGES:
                    for t in tiles:
                        chunk_dve(p, t, stage)
                for t in tiles:
                    s = sets[t % 2]
                    for c in range(NCH):
                        old, new = state[c % 2], state[(c + 1) % 2]
                        g = t * NCH + c
                        stt(decayed[:], old[:], pend[:, g:g + 1], s["hb"][:, c, :], ALU.mult, ALU.add)
                        if c == NCH - 1:
                            await_full(dve, ("y", p, t))
                            await_drained(dve, ("yl", p, t), "act")
                            tt(kk[:, tok(t)], bank(("y", p, t))[:, 0:P], s["yl"][:], ALU.add, sem=drain(("y", p, t), "dve"))
                        name = ("state", p, t, c)
                        await_full(dve, name)
                        tt(new[:], bank(name)[:, 0:P], decayed[:], ALU.add, sem=drain(name, "dve"))
            d.step(V.tensor_copy(stats[:, 0, 0:1], stats[:, 0, 0:1]), S["y_raw"])
            await_full(dve, ("mean", p))
            stt(kk[:], bank(("mean", p))[:], -1.0 / HD, kk[:], ALU.mult, ALU.add, sem=drain(("mean", p), "dve"))
            tt(sq[:], kk[:], kk[:], ALU.mult, sem=S["y_sq"])
            await_full(dve, ("var", p))
            ts(sq[:], bank(("var", p))[:], 1.0 / HD, GN_EPS, ALU.mult, ALU.add, sem=drain(("var", p), "dve"))
            d.step(V.tensor_copy(stats[:, 0, 0:1], stats[:, 0, 0:1]), S["var_ready"])
            dve.wait_ge(S["root_ready"], 2 * p + 2)
            d.step(V.reciprocal(sq[:], sq[:]))
            tt(kk[:], kk[:], sq[:], ALU.mult)
            ts(kk[:], kk[:], col("lnx_g", p), col("lnx_b", p), ALU.mult, ALU.add)
            tt(kk[:], kk[:], rT[:, p, :], ALU.add)
            await_drained(dve, ("g", p), "act")
            tt(vT[:, p, :], kk[:], kT[:, p, :], ALU.mult, sem=S["yb_ready"])
            ada()
        d.step(V.tensor_copy(stats[:, 0, 0:1], stats[:, 0, 0:1]), S["acc2"])
        await_full(dve, ("state", PAIRS - 1, TT - 1, NCH - 1))
        for half, part in enumerate((uT, vT)):
            dve.wait_ge(S["y_hi"], half + 1)
            tt(act_lo[:, 4 * half:4 * half + 4, :], part[:], act_hi[:, 4 * half:4 * half + 4, :].bitcast(F32),
               ALU.subtract, sem=S["y_lo"])

        def residual(stage, gate, temp):
            for t in range(TT):
                for j in range(2):
                    h = slice(SEQ * j, SEQ * j + SEQ)
                    await_full(dve, (stage, t, j))
                    tt(temp[:, h], bank((stage, t, j))[:], gate[:, h], ALU.mult, sem=drain((stage, t, j), "dve"))
                stt(xres[:, t, :], xres[:, t, :], ALPHA, temp[:], ALU.mult, ALU.add)
                layer_stats(t, xres[:, t, :])
            normalise()

        await_drained(dve, ("mod_rows", 3), "act")
        residual("mix1", acc[:, 0:DM], mixed)
        affine_lo("h2", 2, ar)
        dve.wait_ge(load["rows1"], 32)
        affine_rows(row_a, row_b)
        for m in range(FT):
            name = f"up1_{m}"
            await_full(dve, (name, 1))
            await_drained(dve, (name, 0), "act")
            tt(acc[:, SEQ:2 * SEQ], bank((name, 1))[:], acc[:, 0:SEQ], ALU.mult, sem=drain((name, 1), "dve"))
            dve.wait_ge(S["hid_hi_ready"], m + 1)
            tt(hid_lo[:, m, :], acc[:, SEQ:2 * SEQ], hid_hi[:, m, :].bitcast(F32), ALU.subtract, sem=S["hid_ready"])
        residual("ff1", acc[:, DM:2 * DM], mixed2)
        dve.wait_ge(load["rows2"], 32)
        affine_rows(row2_a, row2_b, S["x_ready"])
        second_dve(dve, d, ts, tt, stt, affine_lo)

    @block.tensor
    def _(pe):
        used = [0]

        def three(o, l, r, first, last):
            pe.matmul(o, l[0], r[0], start=first, stop=False)
            pe.matmul(o, l[0], r[1], start=False, stop=False)
            return pe.matmul(o, l[1], r[0], start=False, stop=last)

        def next_unit(name):
            i = used[0]
            used[0] += 1
            n = SPLIT_UNITS[i]
            assert UNITS[n][0] == name, (UNITS[n][0], name)
            pe.wait_ge(lo_ready, i + 1)
            kc = UNITS[n][3]
            w = UNIT_SIZE[n] // kc
            return [x[i % SPLIT][:, :kc * w].rearrange("p (k n) -> p k n", k=kc) for x in (whi, wlo)], w

        def dense_feature(name, blocks, beside=None):
            (hi, lo), w = next_unit(name)
            for j in range(blocks):
                claim(pe, (name, j))
                for k in range(KC):
                    if beside is not None:
                        beside(j * KC + k)
                    c = slice(P * j, P * j + P)
                    mm = three(bank((name, j))[:], (hi[:, k, c], lo[:, k, c]), (act_hi[:, k, :], act_lo[:, k, :]),
                               k == 0, k == KC - 1)
                mm.then_inc(full_sem((name, j))[0], 1)

        def dense_token(name, per_bank):
            (hi, lo), w = next_unit(name)
            for j in range(TT // per_bank):
                claim(pe, (name, j))
                for i in range(per_bank):
                    t = per_bank * j + i
                    for k in range(KC):
                        mm = three(bank((name, j))[:, i * w:i * w + w], (act_hi[:, k, tok(t)], act_lo[:, k, tok(t)]),
                                   (hi[:, k, :], lo[:, k, :]), k == 0, k == KC - 1)
                mm.then_inc(full_sem((name, j))[0], 1)

        def dense_rows(stage, unit, n_units, hi_in, lo_in, ready):
            for n in range(n_units):
                (hi, lo), w = next_unit(f"{unit}_{n}")
                for k in range(2):
                    for t in range(TT):
                        for j in range(2):
                            if n == k == 0:
                                claim(pe, (stage, t, j))
                            c = slice(SEQ * j, SEQ * j + SEQ)
                            f = 2 * n + k
                            last = n == n_units - 1 and k == 1
                            mm = three(bank((stage, t, j))[:], (hi_in[:, f, tok(t)], lo_in[:, f, tok(t)]),
                                       (hi[:, k, c], lo[:, k, c]), n == k == 0, last)
                            if last:
                                mm.then_inc(full_sem((stage, t, j))[0], 1)
                if n < n_units - 1:
                    mm.then_inc(unit_used, 1)

        def columns(name):
            claim(pe, name)
            for j in range(2 * KC):
                mm = pe.matmul(bank(name)[:, j:j + 1], acc[:, P * j:P * j + P], ones[:], start=True, stop=True)
            mm.then_inc(filled[job(name)[0]], 1)

        def turn_x(stage, source=xres):
            for k in range(KC):
                claim(pe, (stage, k))
                for t in range(TT):
                    mm = pe.transpose(bank((stage, k))[:, tok(t)], source[:, t, P * k:P * k + P], ident[:])
                mm.then_inc(filled[job((stage, k))[0]], 1)

        pe.wait_ge(load["consts"], 32)
        pe.wait_ge(ada_used, KC)
        columns("cols0")
        pe.wait_ge(S["xn_ready"], TT)
        turn_x("h1")
        pe.wait_ge(S["h_lo"], KC)

        def fill(name, mm):
            mm.then_inc(filled[job(name)[0]], 1)

        def prep_pe(p):
            c = slice(P * p, P * p + P)
            claim(pe, ("z", p))
            fill(("z", p), pe.matmul(bank(("z", p))[:], wup[0:HD, c], lora[0:HD, :], start=True, stop=True))
            claim(pe, ("a", p))
            fill(("a", p), pe.matmul(bank(("a", p))[:], wup[HD:P, c], lora[HD:P, :], start=True, stop=True))
            claim(pe, ("kk", p))
            pe.wait_ge(S["kk_sq"], p + 1)
            fill(("kk", p), pe.matmul(bank(("kk", p))[:], bd64[:], sq[:], start=True, stop=True))

        for name in W_IN1:
            if name == "pu0":
                pe.wait_ge(load["masks"], 16 * 7)
                pe.wait_ge(S["acc1"], 1)
                columns("cols1")
                pe.wait_ge(S["lora_ready"], 2)
                prep_pe(0)
            if name[:2] == "pv":
                dense_token(name, 2)
            else:
                dense_feature(name, 1 if name == "lora1" else 2)

        pe.wait_ge(S["wst_ready"], 1)
        pe.wait_ge(S["pv_ready"], TT)
        for g in range(4):
            claim(pe, ("sgu", g))
            for t in range(TT):
                mm = pe.matmul(bank(("sgu", g))[:, tok(t)], pv[:, t, P * g:P * g + P], wsT[:, g, :], start=True, stop=True)
            fill(("sgu", g), mm)

        def chunk_pe(p, t, stage):
            s = sets[t % 2]
            name = (stage, p, t)
            b = bank(name)
            claim(pe, name)
            ready = lambda st, by: await_drained(pe, (st, p, t), by)
            mm = None
            if stage == "turn":
                pe.wait_ge(S["bars_ready"], p + 1)
                for i, x in enumerate((ar[:, 0, tok(t)], sig[:, tok(t)], cs[:, tok(t)], vT[:, p, tok(t)])):
                    mm = pe.transpose(b[:, i * P:i * P + P], x, ident[:])
            elif stage in ("m1", "m2"):
                rows = slice(0, HD) if stage == "m1" else slice(HD, P)
                for i, x in enumerate((bt, kt)):
                    mm = pe.matmul(b[:, 256 * i:256 * i + 256], x[rows, tok(t)], ar[rows, :, tok(t)], start=True, stop=True)
            elif stage in ("n1", "n2"):
                rows = slice(0, HD) if stage == "n1" else slice(HD, P)
                mm = pe.matmul(b[:, 0:P], ar[rows, 0, tok(t)], bt[rows, tok(t)], start=True, stop=True)
            elif stage == "mv":
                ready("turn", "act")
                ready("m2", "dve")
                for h in range(2):
                    mm = pe.matmul(b[:, HD * h:HD * h + HD], s["mm"][:, h, 2, :], s["vz"][:, HD + HD * h:2 * HD + HD * h],
                                   start=True, stop=True)
            elif stage == "q2":
                ready("n2", "dve")
                for h in range(2):
                    pe.matmul(b[:, P * h:P * h + P], s["nd"][:, h, :], s["mm"][:, h, 0, :], start=True, stop=True)
                    mm = pe.matmul(b[:, 256 + P * h:256 + P * h + P], s["mm"][:, h, 0, :], s["nd"][:, h, :],
                                   start=True, stop=True)
            elif stage == "n4":
                ready("q2", "act")
                for h in range(2):
                    mm = pe.matmul(b[:, P * h:P * h + P], s["rq"][:, h, 1, :], s["nn"][:, h, :], start=True, stop=True)
            elif stage == "q4":
                pe.wait_ge(S["r0_ready"], p * TT + t + 1)
                for h in range(2):
                    mm = pe.matmul(b[:, 256 * h:256 * h + 256], s["nn"][:, h, :], s["rq"][:, h, :, :], start=True, stop=True)
            elif stage == "r2":
                ready("n4", "act")
                ready("q4", "dve")
                ready("q4", "act")
                for h in range(2):
                    pe.matmul(b[:, P * h:P * h + P], s["nd"][:, h, :], s["rb"][:, h, :], start=True, stop=True)
                    mm = pe.matmul(b[:, 256 + P * h:256 + P * h + P], s["rq"][:, h, 1, :], s["nd"][:, h, :],
                                   start=True, stop=True)
            elif stage == "r3":
                ready("r2", "dve")
                ready("r2", "act")
                for h in range(2):
                    mm = pe.matmul(b[:, P * h:P * h + P], s["nn"][:, h, :], s["rq"][:, h, 0, :], start=True, stop=True)
            elif stage == "z1":
                ready("r3", "dve")
                ready("mv", "act")
                for h in range(2):
                    pe.matmul(b[:, P * h:P * h + P], s["ee"][:, h, :], s["rb"][:, h, :], start=True, stop=True)
                    mm = pe.matmul(b[:, 256 + P * h:256 + P * h + P], s["rb"][:, h, :], s["z0"][:, P * h:P * h + P],
                                   start=True, stop=True)
            elif stage == "z2":
                ready("z1", "act")
                ready("z1", "dve")
                for h in range(2):
                    mm = pe.matmul(b[:, P * h:P * h + P], s["nd"][:, h, :], s["z1"][:, P * h:P * h + P], start=True, stop=True)
            elif stage == "yl":
                ready("z2", "dve")
                for h in range(2):
                    c = slice(P * h, P * h + P)
                    pe.matmul(b[:, c], s["z"][:, c], s["mm"][:, h, 1, :], start=True, stop=False)
                    mm = pe.matmul(b[:, c], s["vz"][:, c], s["mm"][:, h, 3, :], start=False, stop=True)
            elif stage == "gt":
                pe.wait_ge(S["w_ready"], p * TT + t + 1)
                mm = pe.matmul(b[:], s["nn"][:, 0, :], s["bx"][:], start=True, stop=True)
            elif stage == "hh":
                for c in range(NCH):
                    o = b[:, P * c:P * c + P]
                    pe.matmul(o, s["bx"][:, c, :], s["z"][:, HD:HD + P], start=True, stop=False)
                    mm = pe.matmul(o, s["kx"][:, c, :], s["vz"][:, HD:HD + P], start=False, stop=True)
            fill(name, mm)

        for p in range(PAIRS):
            if p:
                prep_pe(p)
            claim(pe, ("bonus", p))
            pe.wait_ge(S["prep_ready"], p + 1)
            fill(("bonus", p), pe.matmul(bank(("bonus", p))[:], bd64[:], rT[:, p, :], start=True, stop=True))
            claim(pe, ("g", p))
            c = slice(P * p, P * p + P)
            pe.matmul(bank(("g", p))[:], gup[:, 0, c], gd[:, 0, :], start=True, stop=False)
            fill(("g", p), pe.matmul(bank(("g", p))[:], gup[:, 1, c], gd[:, 1, :], start=False, stop=True))
            for tiles in CHUNK_TILES:
                for stage, _ in CHUNK_STAGES:
                    for t in tiles:
                        chunk_pe(p, t, stage)
                for t in tiles:
                    s = sets[t % 2]
                    y = bank(("y", p, t))
                    claim(pe, ("y", p, t))
                    await_drained(pe, ("hh", p, t), "dve")
                    for c in range(NCH):
                        old = state[c % 2]
                        if (t, c) == (0, 0):
                            pe.wait_ge(S["state_zero"], p + 1)
                        elif c == 0:
                            await_drained(pe, ("state", p, t - 1, NCH - 1), "dve")
                        else:
                            await_drained(pe, ("state", p, t, c - 1), "dve")
                        mm = pe.matmul(y[:, CH * c:CH * c + CH], old[:], s["rp"][:, CH * c:CH * c + CH], start=True, stop=True)
                        if c == NCH - 1:
                            fill(("y", p, t), mm)
                        name = ("state", p, t, c)
                        claim(pe, name)
                        fill(name, pe.matmul(bank(name)[:, 0:P], s["gt"][:, c, :], old[:], start=True, stop=True))
            claim(pe, ("mean", p))
            pe.wait_ge(S["y_raw"], p + 1)
            fill(("mean", p), pe.matmul(bank(("mean", p))[:], bd64[:], kk[:], start=True, stop=True))
            claim(pe, ("var", p))
            pe.wait_ge(S["y_sq"], p + 1)
            fill(("var", p), pe.matmul(bank(("var", p))[:], bd64[:], sq[:], start=True, stop=True))

        pe.wait_ge(load["bias"], 16)
        pe.wait_ge(S["acc2"], 1)
        for j in range(4):
            claim(pe, ("mod_rows", j))
            b = bank(("mod_rows", j))
            pe.matmul(b[:], ones[:].to_broadcast([P, P]), acc[:, SEQ * j:SEQ * j + SEQ], start=True, stop=False)
            fill(("mod_rows", j), pe.matmul(b[:], ident[0:4, j:j + 1].to_broadcast([4, P]), bias4[:], start=False, stop=True))
        pe.wait_ge(S["y_lo"], 2)
        dense_rows("mix1", "out1", 4, act_hi, act_lo, None)
        pe.wait_ge(S["xn_ready"], 2 * TT)
        turn_x("h2")
        pe.wait_ge(S["h_lo"], 2 * KC)
        for m in range(FT):
            dense_feature(f"up1_{m}", 2)
        pe.wait_ge(S["hid_ready"], FT)
        dense_rows("ff1", "down1", FT // 2, hid_hi, hid_lo, None)
        second_pe(pe, three, next_unit, dense_feature, dense_token, dense_rows, turn_x, fill)

    ctx.close()


def lay_out(inputs):
    x = {k: np.asarray(v) for k, v in inputs.items()}
    c = lambda v: np.asarray(v).reshape(-1, P).T
    base = 2 * MIX
    mu = x["mu_shift"][0]
    lora = 3 * MIX
    ffn = x["ffn_conv_w_2"][0]
    b = x["b_ada"][0].reshape(6, DM)
    cols = {"c": c(x["c"]), "emb_g": c(x["emb_ln_g"]), "emb_b": c(x["emb_ln_b"]), "mu_l": c(mu[lora:lora + 128]),
            "mu_g0": c(mu[lora + 128:lora + 256]), "mu_g1": c(mu[lora + 160:lora + 288]),
            "mu_r": c(mu[:MIX]), "mu_k": c(mu[MIX:2 * MIX]), "mu_v": c(mu[2 * MIX:3 * MIX]),
            "ln1_g": c(x["ln1_g"]), "ln1_b": c(x["ln1_b"]), "nmp": c(x["norm_mix_pre_2"]), "nfp": c(x["norm_ffn_pre_2"]),
            "cmix": c(x["conv_mix_w_2"]), "cffn": c(ffn),
            "pe_k": np.tile(x["pe_cmp_k_2"][0].T, (2, 1)), "pe_v": np.tile(x["pe_cmp_v_2"][0].T, (2, 1)),
            "has_key": (np.arange(P)[:, None] >= L_CMP - 1).astype(np.float32),
            "b_sh1": c(b[0]), "b_sc1": c(b[1]), "b_sh2": c(b[3]), "b_sc2": c(b[4])}
    for n in ("w0", "a0", "k_k", "k_a", "r_k", "lnx_g", "lnx_b"):
        cols[n] = c(x[n])
    params = np.concatenate([cols[n] for n in COLS], 1)
    parts = []
    for _, matrix, row, tiles, ranges in UNITS:
        w = x[matrix][0]
        w = np.concatenate([w[row:row + tiles * P, a:a + n] for a, n in ranges], 1)
        parts.append(w.reshape(tiles, P, -1).transpose(1, 0, 2).reshape(P, -1))
    g_up = np.zeros((P, 2, MIX), np.float32)
    g_up[:, 0] = x["g_up"][0][:P]
    g_up[P - 32:, 1] = x["g_up"][0][P:]
    return {
        "x": x["x"], "params": params, "weights": np.concatenate(parts, 1), "consts": shape_constants(),
        "w_s_t": x["w_s"][0].transpose(2, 0, 1), "b_s": x["b_s"][0], "sg_ln_g": x["sg_ln_g"][0], "sg_ln_b": x["sg_ln_b"][0],
        "emb_ln_g": x["emb_ln_g"], "emb_ln_b": x["emb_ln_b"], "ln1_g": x["ln1_g"][0], "ln1_b": x["ln1_b"][0],
        "ln2_g": x["ln2_g"][0], "ln2_b": x["ln2_b"][0], "lora_up": np.concatenate([x["w_up"][0], x["a_up"][0]], 0),
        "w1": np.stack([x[f"w_cmp_{n}1_2"][0].reshape(L_CMP // 2, P, CMP_HID).transpose(1, 0, 2) for n in "kv"]),
        "w2k": np.tile(x["w_cmp_k2_2"][0].reshape(2, P, HD).transpose(1, 0, 2), (1, 1, 2)),
        "w2v": x["w_cmp_v2_2"][0].reshape(2, P, HD).transpose(1, 0, 2), "rel_bias_t": x["rel_bias_2"].T,
        "mix_post": x["norm_mix_post_2"][0], "ffn_post": x["norm_ffn_post_2"][0],
        "g_up_pad": g_up, "b_gates": np.concatenate([b[2], b[5]]).reshape(4, SEQ),
    }


def kernel(**inputs):
    import concourse.bacc as bacc
    from concourse.bass_utils import run_bass_kernel_spmd

    nc = bacc.Bacc("TRN2", target_bir_lowering=False, num_devices=1)
    arrays = {f"in_{n}": np.ascontiguousarray(a) for n, a in lay_out(inputs).items()}
    src = {n[3:]: nc.dram_tensor(n, a.shape, mybir.dt.from_np(a.dtype), kind="ExternalInput").ap()
           for n, a in arrays.items()}
    out = nc.dram_tensor("out", (1, SEQ, DM), F32, kind="ExternalOutput").ap()
    build(nc, src, out)
    return run_bass_kernel_spmd(nc, [arrays], core_ids=[0]).results[0]["out"]
```

```python
import math

import numpy as np

import concourse.bass as bass
from concourse import mybir

F32 = mybir.dt.float32
F32R = mybir.dt.float32r
ACT = mybir.ActivationFunctionType
ALU = mybir.AluOpType
AX_X = mybir.AxisListType.X

P = 128
SEQ = 512
TT = SEQ // P
DM = 1024
KC = DM // P
MIX = 512
PAIRS = MIX // P
HD = 64
CH = 32
NCH = P // CH
FFN = 2816
FT = FFN // P
ALPHA = 2.0 ** 0.25
LN_EPS, GN_EPS, RMS_EPS = 1e-5, 64e-5, 1e-6
DECAY = math.exp(-0.5)
N_HEADS, N_KV, REP = 8, 2, 4
L_CMP, S_CMP = 32, 16
N_CMP = (SEQ - L_CMP) // S_CMP + 1
CMP_HID = 256
N_BUCKETS, MAX_DIST = 32, 128
NEG = -1e30
GRID = SEQ + P

COLS, N_COLS = {}, 0
for _name, _n in (("c", KC), ("emb_g", KC), ("emb_b", KC), ("mu_l", 1), ("mu_g0", 1), ("mu_g1", 1),
                  ("mu_k", 4), ("mu_v", 4), ("mu_r", 4), ("w0", 4), ("a0", 4), ("k_k", 4), ("k_a", 4),
                  ("r_k", 4), ("lnx_g", 4), ("lnx_b", 4), ("ln1_g", KC), ("ln1_b", KC), ("nmp", KC),
                  ("nfp", KC), ("cmix", 12), ("cffn", 3 * 2 * FT), ("pe_k", L_CMP), ("pe_v", L_CMP),
                  ("has_key", 1), ("b_sh1", KC), ("b_sc1", KC), ("b_sh2", KC), ("b_sc2", KC)):
    COLS[_name] = N_COLS
    N_COLS += _n
N_MU = 15

CONSTS = {"ident": (0, 128), "bd64": (128, 128), "up": (256, 128), "mask_qr": (384, 256),
          "mask_mk": (640, 256), "mask_d": (896, 128), "mask_e": (1024, 128), "chunk_rows": (1152, 4),
          "onehot": (1156, GRID), "future": (1156 + GRID, SEQ)}
N_CONST = 1156 + GRID + SEQ


def shape_constants():
    c = np.zeros((P, N_CONST), np.float32)
    p, f = np.arange(P)[:, None], np.arange(P)[None, :]

    def put(name, v):
        at, n = CONSTS[name]
        c[:, at:at + n] = v

    same = lambda n: (p // n) == (f // n)
    put("ident", p == f)
    put("bd64", same(64))
    put("up", p <= f)
    put("mask_qr", np.concatenate([(p < f) & same(16), (p <= f) & same(CH)], 1))
    put("mask_mk", np.concatenate([(p < f) & same(CH), (p <= f) & same(CH)], 1))
    put("mask_d", (p > f) & same(16))
    put("mask_e", (p > f) & same(CH) & ~same(16))
    put("chunk_rows", (p // CH) == np.arange(NCH)[None, :])
    dist = (SEQ - 1) - np.arange(GRID)
    exact = N_BUCKETS // 2
    d = np.maximum(dist, 0)
    df = np.maximum(d, 1).astype(np.float32)
    scaled = np.log(df / np.float32(exact)) / np.float32(math.log(MAX_DIST / exact))
    large = exact + (scaled * np.float32(N_BUCKETS - exact)).astype(np.int32)
    bucket = np.where(d < exact, d, np.minimum(large, N_BUCKETS - 1))
    c[:N_BUCKETS, CONSTS["onehot"][0]:][:, :GRID] = bucket[None, :] == np.arange(N_BUCKETS)[:, None]
    put("future", np.where(p + 384 - np.arange(SEQ)[None, :] < 0, -NEG, 0.0))
    return c


def weight_units():
    units = [(f"ada0_{k}", "w_ada", k * P, 1, ((0, 2 * DM),)) for k in range(KC)]
    base = 2 * MIX
    lora = base + 3 * MIX
    win = [("lora0", ((lora, 256),)), ("lora1", ((lora + 160, 128),))]
    win += [(f"k{j}", ((base + MIX + 256 * j, 256),)) for j in range(2)]
    win += [(f"r{j}", ((base + 256 * j, 256),)) for j in range(2)]
    win += [(f"v{j}", ((base + 2 * MIX + 256 * j, 256),)) for j in range(2)]
    win += [(f"pv{j}", ((MIX + 256 * j, 256),)) for j in range(2)]
    win += [(f"pu{j}", ((256 * j, 256),)) for j in range(2)]
    ada = [(f"ada1_{k}", "w_ada", k * P, 1, ((3 * DM, 2 * DM),)) for k in range(KC)]
    ada += [(f"ada2_{k}", "w_ada", k * P, 1, ((2 * DM, DM), (5 * DM, DM))) for k in range(KC)]
    units += [(name, "w_in", 0, KC, ranges) for name, ranges in win] + ada
    units += [(f"out1_{n}", "w_out", 2 * n * P, 2, ((0, DM),)) for n in range(4)]
    for m in range(FT):
        units.append((f"up1_{m}", "w_ffn_in", 0, KC, ((m * P, P), (FFN + m * P, P))))
    for n in range(FT // 2):
        units.append((f"down1_{n}", "w_ffn_out", 2 * n * P, 2, ((0, DM),)))
    kv = MIX
    win2 = [("cmp", ((kv, 256),))] + [(f"q{j}", ((256 * j, 256),)) for j in range(2)]
    win2 += [("slc", ((kv + 256, 256),)), ("win", ((kv + 512, 256),)), ("gates", ((kv + 768, 24),))]
    for part, name in enumerate(("bg", "cg", "xt")):
        win2 += [(f"{name}{j}", ((kv + 792 + part * MIX + 256 * j, 256),)) for j in range(2)]
    units += [(name, "w_in_2", 0, KC, ranges) for name, ranges in win2]
    units += [(f"out2_{n}", "w_out_2", 2 * n * P, 2, ((0, DM),)) for n in range(4)]
    units += [(f"up2_{m}", "w_ffn_up_2", 0, KC, ((m * P, P), (FFN + m * P, P))) for m in range(FT)]
    units += [(f"down2_{n}", "w_ffn_down_2", 2 * n * P, 2, ((0, DM),)) for n in range(FT // 2)]
    return units


UNITS = weight_units()
UNIT_AT = {u[0]: n for n, u in enumerate(UNITS)}
UNIT_SIZE = [u[3] * sum(w for _, w in u[4]) for u in UNITS]
UNIT_START = [sum(UNIT_SIZE[:n]) for n in range(len(UNITS) + 1)]
SPLIT_UNITS = [n for n, u in enumerate(UNITS) if u[1] != "w_ada"]
SPLIT_AT = {n: i for i, n in enumerate(SPLIT_UNITS)}
RAW, SPLIT = 3, 2


class Order:

    def __init__(self, eng, own):
        self.eng, self.own, self.count, self.last = eng, own, {}, None

    def done(self, ins, sem=None):
        sem = self.own if sem is None else sem
        self.count[sem.name] = self.count.get(sem.name, 0) + 1
        ins.then_inc(sem, 1)
        self.last = (sem, self.count[sem.name])

    def settle(self):
        self.eng.wait_ge(*self.last)

    def step(self, ins, sem=None):
        self.done(ins, sem)
        self.settle()


class Banks:

    def __init__(self):
        self.fills = [0] * 8
        self.drains = {"dve": [0] * 8, "act": [0] * 8}
        self.of = {}
        self.turn = 0
        self.shared = range(4, 8)

    def add(self, name, bank=None, dve=0, act=0, unit=None):
        if bank is None:
            bank = self.shared[self.turn % len(self.shared)]
            self.turn += 1
        before = {e: self.drains[e][bank] for e in self.drains}
        if unit is None:
            self.fills[bank] += 1
        self.drains["dve"][bank] += dve
        self.drains["act"][bank] += act
        after = {e: self.drains[e][bank] for e in self.drains}
        self.of[name] = (bank, self.fills[bank] if unit is None else SPLIT_AT[UNIT_AT[unit]] + 1, before, after,
                         unit is not None)


def plan_banks():
    b = Banks()
    turn = [0]

    def dense(name, drains):
        pair = 2 * (turn[0] % 2)
        turn[0] += 1
        for j, drain in enumerate(drains):
            b.add((name, j), pair + j, unit=name if j == len(drains) - 1 else None, **drain)

    def dense_rows(name, last_unit, act=0):
        for t in range(TT):
            for j in range(2):
                b.add((name, t, j), 2 * t + j, dve=1, act=act, unit=last_unit if (t, j) == (TT - 1, 1) else None)

    for k in range(KC - 1):
        b.add(("h1", k), k, dve=1, act=1)
    b.add("cols0", KC - 1, dve=1)
    b.add(("h1", KC - 1), 0, dve=1, act=1)
    for name in ("lora0", "lora1", "k0", "k1", "r0", "r1", "v0", "v1"):
        dense(name, drains=[dict(dve=1, act=1)] * (1 if name == "lora1" else 2))
    plan_prep(b, 0, 0)
    plan_prep(b, 0, 6)
    for name in ("pv0", "pv1", "pu0", "pu1"):
        dense(name, drains=[dict(act=1)] * 2)
    for g in range(4):
        b.add(("sgu", g), dve=1)
    plan_prep(b, 0, 13)
    b.shared = range(2, 8)
    for kind, *args in CHUNK_SCHEDULE:
        if kind == "stage":
            b.add(tuple(args), **dict(CHUNK_STAGES)[args[0]])
        elif kind == "chain":
            p, t, c = args
            last = (p, t // 2) == (PAIRS - 1, 1)
            if c == 0:
                b.add(("y", p, t), 6 if last else t % 2, dve=1)
            b.add(("state", p, t, c), 7 if last else None, dve=1)
        elif kind == "prep":
            plan_prep(b, *args)
        elif kind == "cols1":
            b.add("cols1", dve=1)
        elif kind == "norm" and args[1] < 2:
            b.add((("mean", "var")[args[1]], args[0]), 7 if args[0] == PAIRS - 1 else None, dve=1)
    b.shared = range(4, 8)
    for j in range(4):
        b.add(("mod_rows", j), j, act=1)
    dense_rows("mix1", "out1_3")
    for k in range(KC):
        b.add(("h2", k), k, dve=1, act=1)
    for m in range(FT):
        dense(f"up1_{m}", drains=[dict(act=1), dict(dve=1)])
    dense_rows("ff1", f"down1_{FT // 2 - 1}")
    plan_second(b, dense, dense_rows)
    return b.of


def plan_prep(b, p, part):
    for name, at, drain in (("z", 0, dict(act=1)), ("a", 0, dict(act=1)), ("kk", 6, dict(dve=1)),
                            ("bonus", 13, dict(dve=1)), ("g", 13, dict(act=1))):
        if at == part:
            b.add((name, p), **drain)


CHUNK_STAGES = (("turn", dict(dve=2, act=2)), ("m1", dict(dve=1)), ("m2", dict(dve=1)), ("n1", dict(dve=2)),
                ("n2", dict(dve=2)), ("mv", dict(act=1)), ("q2", dict(act=2)), ("n4", dict(act=1)),
                ("q4", dict(dve=1, act=1)), ("r2", dict(dve=1, act=1)), ("r3", dict(dve=1)),
                ("z1", dict(dve=1, act=1)), ("z2", dict(dve=1)), ("yl", dict(dve=2, act=2)),
                ("gt", dict(dve=1)), ("hh", dict(dve=1)))
PREP_EVEN = {1: (0,), 3: (1,), 5: (2,), 6: (3,), 7: (4,)}
PREP_ODD = {0: (5,), 4: (6,), 5: (7,), 6: (8,), 7: (9,), 8: (10,), 9: (11,), 10: (12,)}
BONUS_AT = 5
NORM_EVEN = {9: (0,), 11: (1,), 12: (2,), 13: (3,), 14: (4,), 15: (5, 6)}
ADA_EVEN, ADA_ODD = (8, 10, 12), (11, 12)
NORM_PARTS = 7
QUARTER = SEQ // 4


def chunk_schedule():
    order, before, adas = [], [], 0
    for p in range(PAIRS):
        for first in (0, 2):
            tiles = (first, first + 1)
            for n, (stage, _) in enumerate(CHUNK_STAGES):
                order += [("stage", stage, p, t) for t in tiles]
                if n < len(before):
                    order.append(before[n])
                if p + 1 < PAIRS:
                    order += [("prep", p + 1, part) for part in (PREP_ODD if first else PREP_EVEN).get(n, ())]
                if not first and p:
                    order += [("norm", p - 1, part) for part in NORM_EVEN.get(n, ())]
                    order += [("prep", p, 13)] if n == BONUS_AT else []
                if n in (ADA_ODD if first else ADA_EVEN) and adas < 2 * KC:
                    adas += 1
                    order.append(("ada", adas))
                if (p, first, n) == (1, 2, 3):
                    order.append(("cols1",))
            before = [("chain", p, t, c) for t in tiles for c in range(NCH)]
    order.append(("mixer", 0))
    for n, step in enumerate(before):
        order.append(step)
        if n < 4:
            order.append(("mod_rows", n))
        if n == 3:
            order.append(("mixer", 1))
        if n in (6, 7):
            order.append(("out1", 0, n - 6))
    order += [("mixer", 2), ("norm", PAIRS - 1, 0), ("out1", 1, 0), ("out1", 1, 1), ("norm", PAIRS - 1, 1),
              ("out1", 2, 0), ("out1", 2, 1)]
    return order + [("norm", PAIRS - 1, part) for part in range(2, NORM_PARTS)] + [("mixer", 3)]


CHUNK_SCHEDULE = chunk_schedule()


ITEMS = [(br, h, i) for br in ("slc", "win", "cmp") for h in range(N_HEADS) for i in range(TT)]
N_SLOTS = len(ITEMS) + 3
SLOT_UNITS = ("bg0", "bg1", "cg0", "cg1", "xt0", "xt1")
PER_UNIT = -(-N_SLOTS // len(SLOT_UNITS))
FIRST_UNITS = ("cmp", "q0", "q1", "slc", "win", "gates")


def slots_of(n):
    return range(PER_UNIT * n, min(PER_UNIT * (n + 1), N_SLOTS))


def stages_of(slot):
    return [(st, slot - lag) for st, lag in (("scores", 0), ("turn2", 2), ("values", 3))
            if 0 <= slot - lag < len(ITEMS)]


def n_keys(item):
    br, _, i = ITEMS[item]
    return (P // S_CMP) * i + P // S_CMP - 1 if br == "cmp" else P * (i + 1)


def plan_second(b, dense, dense_rows):
    for k in range(KC):
        b.add(("h3", k), k, dve=1, act=1)
    for j in range(2):
        b.add(("bias", j), act=1)
    for name in FIRST_UNITS:
        dense(name, drains=[dict(act=1)] * (1 if name == "gates" else 2))
        if name in ("q1", "win"):
            kv = "k" if name == "q1" else "v"
            b.add(("hidden", kv), act=1)
            b.add(("compressed", kv), act=1)
    for n, name in enumerate(SLOT_UNITS):
        dense(name, drains=[dict(dve=1) if name[:2] == "xt" else dict(act=1)] * 2)
        for slot in slots_of(n):
            for st, item in stages_of(slot):
                b.add((st, item), **(dict(act=1) if st == "turn2" else dict(dve=1)))
    for k in range(PAIRS):
        b.add(("turn_o", k), act=1, dve=1)
    dense_rows("mix2", "out2_3", act=1)
    for k in range(KC):
        b.add(("h4", k), k, dve=1, act=1)
    for m in range(FT):
        dense(f"up2_{m}", drains=[dict(act=1, dve=1)] * 2)
    dense_rows("ff2", f"down2_{FT // 2 - 1}", act=1)


def build(nc, src, out):
    bank_of = plan_banks()
    byte = {"at": (nc.sbuf_base + 63) // 64 * 64}
    from contextlib import ExitStack
    ctx = ExitStack()

    def place(name, shape, dt=F32, at=None):
        size = (4 * int(np.prod(shape[1:])) + 31) // 32 * 32
        if at is None:
            at = byte["at"]
            byte["at"] += size
        t = nc.alloc_sbuf_tensor_at(name, list(shape), dt, offset=at)
        return t, at + size

    def sem(name):
        return ctx.enter_context(nc.semaphore(name))

    raw = [place(f"raw{i}", [P, 2048])[0] for i in range(RAW)]
    whi, wlo = zip(*((place(f"weight_hi{i}", [P, 2048], F32R)[0], place(f"weight_lo{i}", [P, 2048], F32R)[0])
                     for i in range(SPLIT)))
    act_at = byte["at"]
    slots_at = act_at - 2 * SPLIT * 8192
    act_hi, _ = place("act_hi", [P, KC, SEQ], F32R)
    act_lo, _ = place("act_lo", [P, KC, SEQ], F32R)
    xres, _ = place("xres", [P, TT, DM])
    acc, _ = place("acc", [P, 2 * DM])
    pc, _ = place("params", [P, N_COLS])
    omu, _ = place("one_minus_mu", [P, N_MU])
    oka, _ = place("one_minus_ka", [P, 4])
    affine, _ = place("affine", [P, 4, KC])
    modc, _ = place("mod_columns", [P, 2 * KC])
    ident, _ = place("ident", [P, P])
    bd64, _ = place("bd64", [P, P])
    stats, _ = place("stats", [P, 2, 6])
    mv, _ = place("mean_var", [P, TT, 2])
    rstd, _ = place("rstd", [P, TT])
    ones, _ = place("ones", [P, 1])
    bias4, _ = place("bias4", [4, SEQ])
    byte["small"] = byte["at"]
    byte["at"] += 64
    arena = byte["at"]

    nxt = arena
    def here(name, shape, dt=F32):
        nonlocal nxt
        t, nxt = place(name, shape, dt, nxt)
        return t
    kT, rT, vT = (here(f"{n}T", [P, PAIRS, SEQ]) for n in "krv")
    lora = here("lora", [P, SEQ])
    gd = here("gd", [P, 2, SEQ])
    uT = here("uT", [P, 4, SEQ])
    wup = here("wup", [P, MIX])
    gup = here("gup", [P, 2, MIX])
    chunk_rows = here("chunk_rows", [P, NCH])
    masks = here("masks", [P, 4, P])
    mask_d = here("mask_d", [P, P])
    mask_e = here("mask_e", [P, P])
    restart = here("restart", [P, SEQ])
    state = [here(f"state{i}", [P, P]) for i in range(2)]
    decayed = here("decayed", [P, P])
    pend = [here(f"chunk_decay{i}", [P, SEQ // CH]) for i in range(PAIRS)]
    gm_at = nxt
    pv = here("pv", [P, TT, MIX])
    wsT = here("wsT", [P, 4, P])
    bs = here("bs", [P, 4, P])
    sg_g = here("sg_g", [P, MIX])
    sg_b = here("sg_b", [P, MIX])
    gm_end = nxt
    pair_at = nxt
    def pair_buffers(i):
        small = ("sig", "cs", "aa", "ep", "bt", "kt")
        shapes = [(n, [P, SEQ]) for n in small] + [("ar", [P, 2, SEQ])] + [(n, [P, SEQ]) for n in ("kk", "sq")]
        return {name: here(f"{name}_{i}", shape) for name, shape in shapes}
    pairs = [pair_buffers(0)]
    pair_end = nxt
    row_a, _ = place("row_a", [P, DM], F32, pair_at)
    row_b, _ = place("row_b", [P, DM], F32, pair_at + 4096)
    up, _ = place("up", [P, P], F32, pair_at + 8192)
    assert pair_end <= nc.sbuf_usable_end, (pair_end, nc.sbuf_usable_end)

    link_shapes = (("gt", [P, NCH, P]), ("hb", [P, NCH, P]), ("rp", [P, P]), ("yl", [P, P]))
    nxt = slots_at
    pairs.append(pair_buffers(1))
    norm_buffers = [pairs[p % 2] if p < PAIRS - 1 else pairs[0] for p in range(PAIRS)]
    links = [[{name: here(f"{name}_{q}1", shape) for name, shape in link_shapes}] for q in range(2)]
    assert nxt <= act_at
    sets = []
    nxt = act_at
    gap = act_at + 2 * KC * SEQ * 4
    def chunk(name, shape):
        nonlocal nxt
        size = (4 * int(np.prod(shape[1:])) + 31) // 32 * 32
        if nxt <= gap and nxt + size > gap:
            nxt = gm_at
        t, nxt = place(name, shape, F32, nxt)
        assert nxt <= gap or gm_at < nxt <= gm_end, (name, nxt)
        return t
    for q in range(2):
        d = {}
        for name, shape in (("mm", [P, 2, 4, P]), ("nd", [P, 2, P]), ("ee", [P, 2, P]),
                            ("rq", [P, 2, 2, P]), ("nn", [P, 2, P]), ("rb", [P, 2, P]), ("z0", [P, 256]),
                            ("z1", [P, 256]), ("z", [P, 256]), ("bx", [P, NCH, P]), ("kx", [P, NCH, P]),
                            ("vz", [P, 256])):
            d[name] = chunk(f"{name}_{q}", shape)
        sets.append(d)
        links[q].insert(0, {name: chunk(f"{name}_{q}0", shape) for name, shape in link_shapes})

    hid_hi, e1 = place("hid_hi", [P, FT, SEQ], F32R, arena)
    hid_lo, e1 = place("hid_lo", [P, FT, SEQ], F32R, e1)
    assert e1 <= nc.sbuf_usable_end, (e1, nc.sbuf_usable_end)

    nxt = arena
    xn2, _ = place("xn2", [P, TT, DM], F32, nxt)
    w1 = here("w1", [P, L_CMP // 2, CMP_HID])
    qT = here("qT", [P, PAIRS, SEQ])
    kvc = here("kvc", [P, 2, SEQ])
    ksl = here("ksl", [P, 2, SEQ])
    kwn = here("kwn", [P, 2, SEQ])
    vsl = here("vsl", [P, TT, P])
    vwn = here("vwn", [P, TT, P])
    gate = here("gate", [P, TT, 24])
    bgT = here("bgT", [P, 4, SEQ])
    cgT = here("cgT", [P, 4, SEQ])
    strip = here("strip", [P, N_HEADS, SEQ])
    o_at = nxt
    o = here("o", [P, TT, MIX])
    onehot, z = place("onehot", [P, GRID], F32, o_at)
    future, z = place("future", [P, SEQ], F32, z)
    grow, z = place("grow", [N_HEADS, GRID], F32, z)
    assert z <= nxt
    blk = here("blk", [P, L_CMP // 2, 2 * N_CMP])
    w2k = here("w2k", [P, 2, P])
    w2v = here("w2v", [P, 2, HD])
    hc = here("hc", [P, 2, 2 * N_CMP])
    kc2 = here("kc2", [P, 2, N_CMP])
    vc = here("vc", [P, 2, HD])
    relb = here("relb", [P, N_HEADS])
    low = here("low", [P, 3])
    den = here("den", [P, 3])
    weights4 = here("weights4", [P, 4])
    sc4 = here("sc4", [P, SEQ])
    assert nxt <= nc.sbuf_usable_end, nxt
    scores = [acc[:, SEQ * j:SEQ * j + SEQ] for j in range(3)]
    probsT = [acc[:, 3 * SEQ:4 * SEQ], sc4[:]]
    conv_t = w1[:].rearrange("p a b -> p (a b)")[:, 0:SEQ]
    row3, z = place("row3", [P, DM], F32, arena + 4 * TT * DM)
    rms_t, z = place("rms_t", [P, DM], F32, z)
    rms_t3, _ = place("rms_t3", [P, DM], F32, z)
    row4, z = place("row4", [P, DM], F32, act_at)
    rms_t2, z = place("rms_t2", [P, DM], F32, z)
    rms_t4, _ = place("rms_t4", [P, DM], F32, z)
    squares, z = place("squares", [P, 2 * TT], F32, byte["small"])
    x_sums, _ = place("x_sums", [P, TT], F32, z)
    scratch = nc.dram_tensor("bias_rows", (N_HEADS, P, GRID), F32, kind="Internal").ap()

    banks = [ctx.enter_context(nc.psum_tensor(f"bank{i}", [P, 512], F32)) for i in range(8)]

    filled = [sem(f"filled{i}") for i in range(8)]
    drained = {"dve": [sem(f"dve_drained{i}") for i in range(8)],
               "act": [sem(f"act_drained{i}") for i in range(8)]}
    raw_landed = [sem(f"raw_landed{i}") for i in range(RAW)]
    hi_ready, lo_ready, unit_used, ada_used = sem("hi_ready"), sem("lo_ready"), sem("unit_used"), sem("ada_used")
    act_step, dve_step, pool_step = sem("act_step"), sem("dve_step"), sem("pool_step")
    load = {n: sem(f"load_{n}") for n in ("x", "params", "consts", "masks", "gmlp", "rows0", "rows1", "rows2",
                                          "bias", "out", "tabs", "w1", "strip0", "strip", "rows3", "rows4")}
    S = {n: sem(n) for n in ("silu_c", "xn_ready", "affine1", "h_hi", "h_lo", "shift_ready", "lora_ready",
                             "kk_sq", "cs_ready", "exp_ready", "ss_ready", "root_ready", "inverse_ready", "norm_root", "norm_inverse", "prep_ready",
                             "bars_ready", "wst_ready", "pv_ready", "pv_std", "pv_root", "gelu_ready", 
                             "r0_ready", "w_ready", "sets_ready", "state_zero", "y_raw", "y_sq", "var_ready", "yb_ready",
                             "y_hi", "y_lo", "y_lo_last", "gates_ready", "var1", "root1", "xn2_ready", "affine2", "hid_hi_ready",
                             "hid_ready", "var2", "root2", "x_ready", "ss3", "root3", "xn3_ready", "grow_ready", "strip_ready", "blk_ready", "hc_ready", "low_ready",
                             "exp_done", "gate_ready", "o_ready", "conv_ready", "y2_hi", "y2_lo", "squares_ready",
                             "rms_ready", "rms_root", "x_rms_ready", "x_rms_root", "x_inverse", "conv1_ready", "gelu2", "prod2", "hid2_hi", "hid2_lo", "out_ready", "keys_part", "weight_ready")}

    def job(name):
        return bank_of[name]

    def bank(name):
        return banks[job(name)[0]]

    def claim(pe, name):
        b, _, before, _, _ = job(name)
        for e in ("dve", "act"):
            if before[e]:
                pe.wait_ge(drained[e][b], before[e])

    def full_sem(name):
        b, n, _, _, by_unit = job(name)
        return (unit_used if by_unit else filled[b]), n

    def await_full(eng, name):
        eng.wait_ge(*full_sem(name))

    def await_drained(eng, name, by):
        b, _, _, after, _ = job(name)
        eng.wait_ge(drained[by][b], after[by])

    def drain(name, by):
        return drained[by][job(name)[0]]

    def raw_ready(eng, n):
        eng.wait_ge(raw_landed[n % RAW], 16 * (n // RAW + 1))

    def col(name, j=0):
        return pc[:, COLS[name] + j:COLS[name] + j + 1]

    def tok(t):
        return slice(t * P, (t + 1) * P)

    def const(name):
        at, n = CONSTS[name]
        return src["consts"][:, at:at + n]

    row2_a, a2 = place("row2_a", [P, DM], F32, act_at)
    row2_b, a2 = place("row2_b", [P, DM], F32, a2)
    mixed2, a2 = place("mixed2", [P, DM], F32, a2)
    mixed, _ = place("mixed", [P, DM], F32, arena)

    def second_act(act, a, convert, affine_hi, square_x, root_x, scaled_x):
        act.dma_start(relb[0:N_BUCKETS, :], src["rel_bias_t"]).then_inc(load["tabs"], 16)
        act.dma_start(onehot[0:N_BUCKETS, :], const("onehot")[0:N_BUCKETS]).then_inc(load["tabs"], 16)
        act.dma_start(future[:], const("future")).then_inc(load["tabs"], 16)
        act.dma_start(w2k[:], src["w2k"]).then_inc(load["tabs"], 16)
        act.dma_start(w2v[:], src["w2v"]).then_inc(load["tabs"], 16)
        affine_hi("h3", "nmp")
        act.dma_start(w1[:], src["w1"][0]).then_inc(load["w1"], 16)
        for j, n in enumerate((SEQ, GRID - SEQ)):
            await_full(act, ("bias", j))
            a.done(act.activation(grow[:, SEQ * j:SEQ * j + n], bank(("bias", j))[0:N_HEADS, 0:n], ACT.Copy, scale=-1.0),
                   drain(("bias", j), "act"))
        a.settle()
        act.wait_ge(drained["act"][job(("bias", 0))[0]], job(("bias", 0))[3]["act"])
        act.dma_start(scratch, grow[:].unsqueeze(1).to_broadcast([N_HEADS, P, GRID])).then_inc(load["strip0"], 16)
        act.wait_ge(load["strip0"], 16)
        act.dma_start(strip[:], bass.AP(scratch.tensor, P - 1, [[GRID - 1, P], [P * GRID, N_HEADS], [1, SEQ]])).then_inc(load["strip"], 16)

        def compress(kv):
            j = "kv".index(kv)
            await_full(act, ("hidden", kv))
            a.done(act.activation(hc[:].rearrange("p a b -> p (a b)"), bank(("hidden", kv))[:, 0:4 * N_CMP], ACT.Gelu_apprx_tanh),
                   drain(("hidden", kv), "act"))
            if kv == "k":
                act.dma_start(w1[:], src["w1"][1]).then_inc(load["w1"], 16)
            await_full(act, ("compressed", kv))
            b = bank(("compressed", kv))
            if kv == "k":
                a.done(act.activation(kc2[:].rearrange("p a b -> p (a b)"), b[:, 0:2 * N_CMP], ACT.Copy), drain(("compressed", kv), "act"))
            else:
                a.done(act.activation(vc[0:N_CMP].rearrange("p a b -> p (a b)"), b[0:N_CMP, 0:2 * HD], ACT.Copy),
                       drain(("compressed", kv), "act"))

        for name in FIRST_UNITS:
            if name != FIRST_UNITS[0]:
                convert()
            b0 = bank((name, 0))
            if name in ("cmp", "q0", "q1"):
                for j in range(2):
                    await_full(act, (name, j))
                    if name == "cmp":
                        ins = act.activation(kvc[:, j, :], bank((name, j))[:], ACT.Copy)
                    else:
                        ins = act.activation(qT[:, 2 * int(name[1]) + j, :], bank((name, j))[:], ACT.Copy, scale=-(HD ** -0.5))
                    a.done(ins, drain((name, j), "act"))
            elif name in ("slc", "win"):
                keys, values = (ksl, vsl) if name == "slc" else (kwn, vwn)
                await_full(act, (name, 0))
                for g in range(N_KV):
                    for half in range(2):
                        ins = act.activation(keys[HD * half:HD * half + HD, g, :], b0[HD * g:HD * g + HD, :], ACT.Copy)
                        a.done(ins, drain((name, 0), "act") if g == half == 1 else S["keys_part"])
                await_full(act, (name, 1))
                a.done(act.activation(values[:].rearrange("p t d -> p (t d)"), bank((name, 1))[:], ACT.Copy), drain((name, 1), "act"))
            else:
                await_full(act, (name, 0))
                a.done(act.activation(gate[:].rearrange("p t g -> p (t g)"), b0[:, 0:24 * TT], ACT.Sigmoid), drain((name, 0), "act"))
            if name in ("q1", "win"):
                compress("k" if name == "q1" else "v")

        for n, name in enumerate(SLOT_UNITS):
            convert()
            for slot in slots_of(n):
                if 0 <= slot < len(ITEMS):
                    x, w = slot % 3, n_keys(slot)
                    act.wait_ge(S["low_ready"], slot + 1)
                    a.step(act.activation(scores[x][:, 0:w], scores[x][:, 0:w], ACT.Exp, bias=low[:, x:x + 1], scale=-1.0,
                                          accum_out=den[:, x:x + 1]), S["exp_done"])
                if 0 <= slot - 2 < len(ITEMS):
                    item = slot - 2
                    w = n_keys(item)
                    await_full(act, ("turn2", item))
                    if item >= 2:
                        await_full(act, ("values", item - 2))
                    b = bank(("turn2", item))
                    if w < P:
                        ins = act.activation(probsT[item % 2][0:w, 0:P], b[0:w, 0:P], ACT.Copy)
                    else:
                        ins = act.activation(probsT[item % 2][:, 0:w], b[:, 0:w], ACT.Copy)
                    a.done(ins, drain(("turn2", item), "act"))
            if name[:2] != "xt":
                dest = bgT if name[0] == "b" else cgT
                for j in range(2):
                    await_full(act, (name, j))
                    a.done(act.activation(dest[:, 2 * int(name[2]) + j, :], bank((name, j))[:], ACT.Copy), drain((name, j), "act"))

        for k in range(PAIRS):
            await_full(act, ("turn_o", k))
            a.done(act.activation(act_hi[:, k, :], bank(("turn_o", k))[:], ACT.Copy), drain(("turn_o", k), "act"))
        act.wait_ge(S["conv_ready"], 4)
        a.done(act.activation(act_hi[:, 4:8, :], bgT[:], ACT.Copy), S["y2_hi"])
        act.dma_start(row3[:], src["mix_post"].partition_broadcast(P)).then_inc(load["rows3"], 16)

        def squares_of_rows(stage, e, t, temp):
            if t < TT:
                for j in range(2):
                    await_full(act, (stage, t, j))
                    a.step(act.activation(temp[:, 0:SEQ], bank((stage, t, j))[:], ACT.Square,
                                          accum_out=squares[:, 2 * t + j:2 * t + j + 1]), drain((stage, t, j), "act"))
            if t > 0 and t <= TT:
                act.wait_ge(S["rms_ready"], TT * e + t)
                a.done(act.activation(rstd[:, t - 1:t], rstd[:, t - 1:t], ACT.Sqrt), S["rms_root"])

        for n in range(3):
            convert()
        for s in range(TT + 4):
            squares_of_rows("mix2", 0, s, rms_t)
            if 0 <= s - 2 < TT:
                square_x(1, s - 2)
            if 0 <= s - 3 < TT:
                root_x(1, s - 3)
            if 0 <= s - 4 < TT:
                scaled_x(1, s - 4)
            if s in (1, TT):
                convert()
        affine_hi("h4", "nfp")

        for m in range(FT):
            if m:
                convert()
            name = f"up2_{m}"
            pair = [acc[:, SEQ * (2 * (m % 2) + j):SEQ * (2 * (m % 2) + j) + SEQ] for j in range(2)]
            for j in range(2):
                await_full(act, (name, j))
                a.done(act.activation(pair[j], bank((name, j))[:], ACT.Copy, scale=col("cffn", 2 * 2 * FT + FT * j + m)),
                       drain((name, j), "act"))
            await_drained(act, (name, 0), "dve")
            a.done(act.activation(pair[0], pair[0], ACT.Gelu_apprx_tanh), S["gelu2"])
            act.wait_ge(S["prod2"], m + 1)
            a.done(act.activation(hid_hi[:, m, :], pair[1], ACT.Copy), S["hid2_hi"])
        for n in range(FT // 2):
            convert()
            if n == 0:
                await_full(act, (f"up2_{FT - 1}", 1))
                act.dma_start(row4[:], src["ffn_post"].partition_broadcast(P)).then_inc(load["rows4"], 16)
        for s in range(TT + 1):
            squares_of_rows("ff2", 1, s, rms_t2)

    def second_dve(dve, d, ts, tt, stt, affine_lo, x_mean_square, inverse_x):
        V = dve

        temp4 = acc[:].rearrange("p (a n) -> p a n", a=4)
        affine_lo("h3", "nmp", temp4)
        dve.wait_ge(load["strip"], 16)
        dve.wait_ge(load["tabs"], 80)
        tt(strip[:], strip[:], future[:].unsqueeze(1).to_broadcast([P, N_HEADS, SEQ]), ALU.add)

        def windows(kv):
            j = "kv".index(kv)
            pe_at = COLS["pe_" + kv]
            if j:
                await_full(dve, ("hidden", "k"))
            for g in range(N_KV):
                rows = slice(HD * g, HD * g + HD)
                x = kvc[rows, j, :].rearrange("p (m l o) -> p o l m", l=8, o=2)
                for odd in range(2):
                    for half in range(2):
                        pe_c = pc[rows, pe_at + 16 * half + odd:pe_at + 16 * half + 16:2]
                        tt(blk[HD * odd:HD * odd + HD, 8 * half:8 * half + 8, N_CMP * g:N_CMP * g + N_CMP],
                           x[:, odd, :, half:half + N_CMP], pe_c.unsqueeze(2).to_broadcast([HD, 8, N_CMP]), ALU.add,
                           sem=S["blk_ready"])

        await_drained(dve, ("cmp", 1), "act")
        windows("k")
        windows("v")
        await_drained(dve, ("gates", 0), "act")
        for h in range(N_HEADS):
            ts(gate[:, 0, 3 * h:3 * h + 1], gate[:, 0, 3 * h:3 * h + 1], col("has_key"))

        for n, name in enumerate(SLOT_UNITS):
            for slot in slots_of(n):
                if 0 <= slot < len(ITEMS):
                    br, h, i = ITEMS[slot]
                    x, w = slot % 3, n_keys(slot)
                    at = 384 - P * i
                    bias = strip[:, h, at:at + w] if br != "cmp" else strip[:, h, at + L_CMP - 1:SEQ:S_CMP]
                    await_full(dve, ("scores", slot))
                    if slot >= 3:
                        await_full(dve, ("turn2", slot - 3))
                    d.step(V.tensor_tensor_reduce(out=scores[x][:, 0:w], in0=bank(("scores", slot))[:, 0:w], in1=bias,
                                                  scale=1.0, scalar=3e38, op0=ALU.add, op1=ALU.min,
                                                  accum_out=low[:, x:x + 1]), drain(("scores", slot), "dve"))
                    d.step(V.tensor_copy(low[:, x:x + 1], low[:, x:x + 1]), S["low_ready"])
                if 0 <= slot - 3 < len(ITEMS):
                    item = slot - 3
                    br, h, i = ITEMS[item]
                    part = ("cmp", "slc", "win").index(br)
                    oh = o[:, i, HD * h:HD * h + HD]
                    b = bank(("values", item))[:, 0:HD]
                    await_full(dve, ("values", item))
                    if br == "slc":
                        ts(oh, b, weights4[:, item % 4:item % 4 + 1], sem=drain(("values", item), "dve"))
                    else:
                        stt(oh, b, weights4[:, item % 4:item % 4 + 1], oh, ALU.mult, ALU.add, sem=drain(("values", item), "dve"))
                if 0 <= slot - 1 < len(ITEMS):
                    item = slot - 1
                    br, h, i = ITEMS[item]
                    part = ("cmp", "slc", "win").index(br)
                    dve.wait_ge(S["exp_done"], item + 1)
                    d.step(V.reciprocal(weights4[:, item % 4:item % 4 + 1], den[:, item % 3:item % 3 + 1]))
                    ts(weights4[:, item % 4:item % 4 + 1], weights4[:, item % 4:item % 4 + 1],
                       gate[:, i, 3 * h + part:3 * h + part + 1], sem=S["weight_ready"])
            if name[:2] == "xt":
                for j in range(2):
                    k = 2 * int(name[2]) + j
                    await_full(dve, (name, j))
                    tt(cgT[:, k, :], bank((name, j))[:], cgT[:, k, :], ALU.mult, sem=drain((name, j), "dve"))
                    ts(conv_t, cgT[:, k, :], col("cmix", 8 + k))
                    stt(conv_t[:, 1:], cgT[:, k, 0:SEQ - 1], col("cmix", 4 + k), conv_t[:, 1:], ALU.mult, ALU.add)
                    stt(conv_t[:, 2:], cgT[:, k, 0:SEQ - 2], col("cmix", k), conv_t[:, 2:], ALU.mult, ALU.add)
                    tt(bgT[:, k, :], bgT[:, k, :], conv_t, ALU.mult, sem=S["conv_ready"])
        for k in range(PAIRS):
            await_full(dve, ("turn_o", k))
            await_drained(dve, ("turn_o", k), "act")
            tt(act_lo[:, k, :], bank(("turn_o", k))[:], act_hi[:, k, :].bitcast(F32), ALU.subtract, sem=drain(("turn_o", k), "dve"))
        dve.wait_ge(S["y2_hi"], 1)
        tt(act_lo[:, 4:8, :], bgT[:], act_hi[:, 4:8, :].bitcast(F32), ALU.subtract, sem=S["y2_lo"])

        def mean_square(stage, t):
            for j in range(2):
                await_drained(dve, (stage, t, j), "act")
            tt(rstd[:, t:t + 1], squares[:, 2 * t:2 * t + 1], squares[:, 2 * t + 1:2 * t + 2], ALU.add)
            ts(rstd[:, t:t + 1], rstd[:, t:t + 1], 1.0 / DM, RMS_EPS, ALU.mult, ALU.add, sem=S["rms_ready"])

        def add_rms(stage, e, t, row, temp, sem):
            dve.wait_ge(S["rms_root"], TT * e + t + 1)
            d.step(V.reciprocal(rstd[:, t:t + 1], rstd[:, t:t + 1]))
            for j in range(2):
                h = slice(SEQ * j, SEQ * j + SEQ)
                stt(temp[:, h], bank((stage, t, j))[:], rstd[:, t:t + 1], row[:, h], ALU.mult, ALU.mult,
                    sem=drain((stage, t, j), "dve"))
            tt(xres[:, t, :], xres[:, t, :], temp[:], ALU.add, sem)

        dve.wait_ge(load["rows3"], 16)
        for s in range(TT + 4):
            if s < TT:
                mean_square("mix2", s)
            if 0 <= s - 1 < TT:
                add_rms("mix2", 0, s - 1, row3, rms_t3, S["x_ready"])
            if 0 <= s - 2 < TT:
                x_mean_square(1, s - 2)
            if 0 <= s - 3 < TT:
                inverse_x(1, s - 3)
        affine_lo("h4", "nfp", temp4)
        for m in range(FT):
            name = f"up2_{m}"
            pair = [acc[:, SEQ * (2 * (m % 2) + j):SEQ * (2 * (m % 2) + j) + SEQ] for j in range(2)]
            for j in range(2):
                await_full(dve, (name, j))
                await_drained(dve, (name, j), "act")
                c = FT * j + m
                stt(pair[j][:, 1:], bank((name, j))[:, 0:SEQ - 1], col("cffn", 2 * FT + c), pair[j][:, 1:], ALU.mult, ALU.add)
                stt(pair[j][:, 2:], bank((name, j))[:, 0:SEQ - 2], col("cffn", c), pair[j][:, 2:], ALU.mult, ALU.add,
                    sem=drain((name, j), "dve"))
            dve.wait_ge(S["gelu2"], m + 1)
            tt(pair[1], pair[1], pair[0], ALU.mult, sem=S["prod2"])
            dve.wait_ge(S["hid2_hi"], m + 1)
            tt(hid_lo[:, m, :], pair[1], hid_hi[:, m, :].bitcast(F32), ALU.subtract, sem=S["hid2_lo"])
        dve.wait_ge(load["rows4"], 16)
        for s in range(TT + 1):
            if s < TT:
                mean_square("ff2", s)
            if s:
                add_rms("ff2", 1, s - 1, row4, rms_t4, S["out_ready"])

    def second_pe(pe, three, next_unit, dense_feature, dense_token, dense_rows, turn_x, fill):
        turn_x("h3", (S["xn3_ready"], 0), xn2)
        pe.wait_ge(load["tabs"], 80)
        for j, n in enumerate((SEQ, GRID - SEQ)):
            claim(pe, ("bias", j))
            fill(("bias", j), pe.matmul(bank(("bias", j))[0:N_HEADS, 0:n], relb[0:N_BUCKETS, :],
                                        onehot[0:N_BUCKETS, SEQ * j:SEQ * j + n], start=True, stop=True))

        def compress(kv):
            j = "kv".index(kv)
            pe.wait_ge(load["w1"], 16 * (j + 1))
            pe.wait_ge(S["blk_ready"], 8 * (j + 1))
            claim(pe, ("hidden", kv))
            b = bank(("hidden", kv))
            for half in range(2):
                for l in range(L_CMP // 2):
                    mm = pe.matmul(b[:, 2 * N_CMP * half:2 * N_CMP * half + 2 * N_CMP], w1[:, l, P * half:P * half + P],
                                   blk[:, l, :], start=l == 0, stop=l == L_CMP // 2 - 1)
            fill(("hidden", kv), mm)
            claim(pe, ("compressed", kv))
            await_drained(pe, ("hidden", kv), "act")
            b = bank(("compressed", kv))
            for g in range(1 if kv == "k" else N_KV):
                for half in range(2):
                    if kv == "k":
                        mm = pe.matmul(b[:, 0:2 * N_CMP], w2k[:, half, :], hc[:, half, :], start=half == 0, stop=half == 1)
                    else:
                        mm = pe.matmul(b[0:N_CMP, HD * g:HD * g + HD], hc[:, half, N_CMP * g:N_CMP * g + N_CMP],
                                       w2v[:, half, :], start=half == 0, stop=half == 1)
            fill(("compressed", kv), mm)

        def keys_and_values(name):
            (hi, lo), w = next_unit(name)
            claim(pe, (name, 0))
            for k in range(KC):
                mm = three(bank((name, 0))[:], (hi[:, k, 0:P], lo[:, k, 0:P]), (act_hi[:, k, :], act_lo[:, k, :]),
                           k == 0, k == KC - 1)
            fill((name, 0), mm)
            claim(pe, (name, 1))
            for t in range(TT):
                for k in range(KC):
                    mm = three(bank((name, 1))[:, tok(t)], (act_hi[:, k, tok(t)], act_lo[:, k, tok(t)]),
                               (hi[:, k, P:], lo[:, k, P:]), k == 0, k == KC - 1)
            mm.then_inc(full_sem((name, 1))[0], 1)

        for name in FIRST_UNITS:
            if name in ("slc", "win"):
                keys_and_values(name)
            elif name == "gates":
                dense_token(name, TT)
            else:
                dense_feature(name, 2, stage="h3" if name == FIRST_UNITS[0] else None)
            if name in ("q1", "win"):
                compress("k" if name == "q1" else "v")

        def attention(slot):
            for st, item in stages_of(slot):
                br, h, i = ITEMS[item]
                g, rows, w = h // REP, slice(HD * (h % 2), HD * (h % 2) + HD), n_keys(item)
                b = bank((st, item))
                claim(pe, (st, item))
                if st == "scores":
                    keys = kc2[rows, g, 0:w] if br == "cmp" else (ksl if br == "slc" else kwn)[rows, g, 0:w]
                    mm = pe.matmul(b[:, 0:w], qT[rows, h // 2, tok(i)], keys, start=True, stop=True)
                elif st == "turn2":
                    pe.wait_ge(S["exp_done"], item + 1)
                    x = scores[item % 3]
                    for j in range(-(-w // P)):
                        n = min(P, w - P * j)
                        mm = pe.transpose(b[0:n, tok(j)], x[:, P * j:P * j + n], ident[:])
                else:
                    await_drained(pe, ("turn2", item), "act")
                    for j in range(-(-w // P)):
                        n = min(P, w - P * j)
                        values = vc[0:n, g, :] if br == "cmp" else (vsl if br == "slc" else vwn)[:, j, HD * g:HD * g + HD]
                        mm = pe.matmul(b[:, 0:HD], probsT[item % 2][0:n, tok(j)], values, start=j == 0, stop=j == -(-w // P) - 1)
                fill((st, item), mm)

        await_drained(pe, ("win", 1), "act")
        await_drained(pe, ("compressed", "v"), "act")
        for n, name in enumerate(SLOT_UNITS):
            slots = list(slots_of(n))
            steps = 2 * KC
            dense_feature(name, 2, lambda k: [attention(s) for s in slots[k * len(slots) // steps:(k + 1) * len(slots) // steps]])
        for k in range(PAIRS):
            claim(pe, ("turn_o", k))
            await_drained(pe, ("values", len(ITEMS) - 1), "dve")
            for t in range(TT):
                mm = pe.transpose(bank(("turn_o", k))[:, tok(t)], o[:, t, P * k:P * k + P], ident[:])
            fill(("turn_o", k), mm)
        pe.wait_ge(S["y2_lo"], 1)
        dense_rows("mix2", "out2", 4, (act_hi, act_lo))
        turn_x("h4", (S["xn3_ready"], TT), xn2)
        for m in range(FT):
            dense_feature(f"up2_{m}", 2, stage=None if m else "h4")
        pe.wait_ge(S["hid2_lo"], FT)
        dense_rows("ff2", "down2", FT // 2, (hid_hi, hid_lo))

    block = ctx.enter_context(nc.Block())
    W_IN1 = ("lora0", "lora1", "k0", "k1", "r0", "r1", "v0", "v1", "pv0", "pv1", "pu0", "pu1")
    CHUNK_TILES = ((0, 1), (2, 3))

    def finish(sp):
        for t in range(TT):
            sp.wait_ge(S["out_ready"], t + 1)
            sp.dma_start(out[0, tok(t), :], xres[:, t, :]).then_inc(load["out"], 16)
        sp.wait_ge(load["out"], 16 * TT)

    @block.sync
    def _(sp):
        sp.dma_start(pc[:], src["params"]).then_inc(load["params"], 16)
        at, n = CONSTS["ident"]
        sp.dma_start(ident[:], const("ident")).then_inc(load["consts"], 16)
        sp.dma_start(bd64[:], const("bd64")).then_inc(load["consts"], 16)
        for n in range(len(UNITS)):
            if n >= RAW:
                m = n - RAW
                if m in SPLIT_AT:
                    sp.wait_ge(lo_ready, SPLIT_AT[m] + 1)
                else:
                    sp.wait_ge(ada_used, m - sum(1 for i in SPLIT_UNITS if i < m) + 1)
            if n == RAW:
                sp.dma_start(xres[:], src["x"].rearrange("b (t p) d -> p (b t) d", p=P)).then_inc(load["x"], 16)
            sp.dma_start(raw[n % RAW][:, :UNIT_SIZE[n]],
                         src["weights"][:, UNIT_START[n]:UNIT_START[n + 1]]).then_inc(raw_landed[n % RAW], 16)
        finish(sp)

    def prep_side(o, p, part):
        pr = pairs[p % 2]
        sig, cs, aa, kk, ep, sq, ar, bt, kt = (pr[n][:] for n in ("sig", "cs", "aa", "kk", "ep", "sq", "ar", "bt", "kt"))
        chunks = lambda x: x.rearrange("p (c t) -> p c t", t=CH)
        ends = pend[p][:].unsqueeze(2).to_broadcast([P, SEQ // CH, CH])

        def times(out, a, b, sem=None):
            o.step(o.eng.tensor_tensor(out, a, b, ALU.mult), sem)

        if part == 4:
            o.eng.wait_ge(S["exp_ready"], 3 * p + 1)
            o.step(o.eng.tensor_copy(pend[p][:], ep[:, CH - 1:SEQ:CH]))
            times(ar[:, 1, :], rT[:, p, :], ep)
            await_drained(o.eng, ("a", p), "act")
            o.step(o.eng.tensor_scalar(ep, aa, col("k_a", p), oka[:, p:p + 1], ALU.mult, ALU.add))
        elif part == 5:
            o.step(o.eng.tensor_scalar(kk, kT[:, p, :], col("k_k", p), None, ALU.mult))
            times(sq, kk, kk, S["kk_sq"])
        elif part == 12:
            times(kT[:, p, :], kT[:, p, :], ep)
            o.eng.wait_ge(S["exp_ready"], 3 * p + 3)
            times(kt, kT[:, p, :], cs)
            o.step(o.eng.tensor_scalar(rT[:, p, :], rT[:, p, :], col("r_k", p), None, ALU.mult))
            times(rT[:, p, :], rT[:, p, :], kT[:, p, :], S["prep_ready"])
            o.eng.wait_ge(S["inverse_ready"], p + 1)
            times(kk, kk, sq)
            times(aa, kk, aa)
            times(bt, aa, cs)
            times(chunks(cs), chunks(kt), ends)
            times(ar[:, 0, :], kk, sig)
            o.step(o.eng.tensor_scalar(ar[:, 0, :], ar[:, 0, :], -1.0, None, ALU.mult))
            times(chunks(sig), chunks(bt), ends, S["bars_ready"])

    def norm_side(o, p, part):
        kk, sq = (norm_buffers[p][n][:] for n in ("kk", "sq"))
        if part == 6:
            o.eng.wait_ge(S["norm_inverse"], p + 1)
            o.step(o.eng.tensor_tensor(kk, kk, sq, ALU.mult))
            o.step(o.eng.tensor_scalar(kk, kk, col("lnx_g", p), col("lnx_b", p), ALU.mult, ALU.add))
            await_drained(o.eng, ("bonus", p), "dve")
            o.step(o.eng.tensor_tensor(kk, kk, rT[:, p, :], ALU.add))
            await_drained(o.eng, ("g", p), "act")
            o.step(o.eng.tensor_tensor(vT[:, p, :], kk, kT[:, p, :], ALU.mult), S["yb_ready"])

    @block.gpsimd
    def _(pool):
        o = Order(pool, pool_step)

        def split(units):
            for n in units:
                i, size = SPLIT_AT[n], UNIT_SIZE[n]
                pool.wait_ge(hi_ready, i + 1)
                pool.tensor_tensor(wlo[i % SPLIT][:, :size], raw[n % RAW][:, :size], whi[i % SPLIT][:, :size],
                                   ALU.subtract).then_inc(lo_ready, 1)

        def ada(i):
            n = UNIT_AT[f"ada{1 + (i - 1) // KC}_{(i - 1) % KC}"]
            raw_ready(pool, n)
            r, c = raw[n % RAW][:], col("c", (i - 1) % KC)
            if i == 1:
                await_full(pool, "cols0")
            elif i == KC + 1:
                await_full(pool, "cols1")
            if (i - 1) % KC == 0:
                o.step(pool.tensor_scalar(acc[:], r, c, None, ALU.mult), ada_used)
            else:
                o.step(pool.tensor_scalar(r, r, c, None, ALU.mult))
                o.step(pool.tensor_tensor(acc[:], acc[:], r, ALU.add), ada_used)

        split(SPLIT_UNITS[:len(W_IN1)])
        for kind, *args in CHUNK_SCHEDULE:
            if kind == "ada":
                ada(*args)
            elif kind == "prep":
                prep_side(o, *args)
            elif kind == "norm" and args[0] < PAIRS - 1:
                norm_side(o, *args)
            elif kind == "mixer" and args[0] < 2:
                part, at, n = ((uT, 0, 4), (vT, 4, PAIRS - 1))[args[0]]
                pool.wait_ge(S["y_hi"], args[0] + 1)
                o.step(pool.tensor_tensor(act_lo[:, at:at + n, :], part[:, 0:n, :], act_hi[:, at:at + n, :].bitcast(F32),
                                          ALU.subtract), S["y_lo"])
                if args[0] == 0:
                    split(SPLIT_UNITS[len(W_IN1):len(W_IN1) + 1])
        split(SPLIT_UNITS[len(W_IN1) + 1:])

    @block.scalar
    def _(act):
        a = Order(act, act_step)
        at = [0]

        def convert():
            i = at[0]
            at[0] += 1
            if i == len(SPLIT_UNITS):
                return
            n = SPLIT_UNITS[i]
            raw_ready(act, n)
            if i >= SPLIT:
                act.wait_ge(unit_used, i - SPLIT + 1)
            a.done(act.activation(whi[i % SPLIT][:, :UNIT_SIZE[n]], raw[n % RAW][:, :UNIT_SIZE[n]], ACT.Copy),
                   hi_ready)

        act.wait_ge(load["params"], 16)
        a.done(act.activation(pc[:, COLS["c"]:COLS["c"] + KC], pc[:, COLS["c"]:COLS["c"] + KC], ACT.Silu), S["silu_c"])
        act.wait_ge(S["var1"], 1)
        a.done(act.activation(rstd[:], rstd[:], ACT.Sqrt), S["root1"])

        def affine_hi(stage, part):
            if isinstance(part, str):
                for k in range(KC):
                    await_full(act, (stage, k))
                    a.done(act.activation(act_hi[:, k, :], bank((stage, k))[:], ACT.Copy, scale=col(part, k)),
                           drain((stage, k), "act"))
                return
            act.wait_ge(S["affine1"], part // 2 + 1)
            for k in range(KC):
                await_full(act, (stage, k))
                a.done(act.activation(act_hi[:, k, :], bank((stage, k))[:], ACT.Identity,
                                      bias=affine[:, part + 1, k:k + 1], scale=affine[:, part, k:k + 1]),
                       drain((stage, k), "act"))

        convert()
        affine_hi("h1", 0)

        act.dma_start(up[:], const("up")).then_inc(load["gmlp"], 16)
        act.dma_start(wsT[:], src["w_s_t"]).then_inc(load["gmlp"], 16)
        act.dma_start(bs[:], src["b_s"].partition_broadcast(P)).then_inc(load["gmlp"], 16)
        act.dma_start(sg_g[:], src["sg_ln_g"].partition_broadcast(P)).then_inc(load["gmlp"], 16)
        act.dma_start(sg_b[:], src["sg_ln_b"].partition_broadcast(P)).then_inc(load["gmlp"], 16)
        act.dma_start(row_a[:], src["emb_ln_g"].partition_broadcast(P)).then_inc(load["rows0"], 16)
        act.dma_start(row_b[:], src["emb_ln_b"].partition_broadcast(P)).then_inc(load["rows0"], 16)
        act.dma_start(wup[:], src["lora_up"]).then_inc(load["masks"], 16)
        act.dma_start(gup[:], src["g_up_pad"]).then_inc(load["masks"], 16)
        act.dma_start(masks[:, 0:2, :], const("mask_qr").rearrange("p (a b) -> p a b", a=2)).then_inc(load["masks"], 16)
        act.dma_start(masks[:, 2:4, :], const("mask_mk").rearrange("p (a b) -> p a b", a=2)).then_inc(load["masks"], 16)
        act.dma_start(mask_d[:], const("mask_d")).then_inc(load["masks"], 16)
        act.dma_start(mask_e[:], const("mask_e")).then_inc(load["masks"], 16)
        act.dma_start(chunk_rows[:], const("chunk_rows")).then_inc(load["masks"], 16)
        act.dma_start(bias4[:], src["b_gates"]).then_inc(load["bias"], 16)

        def unshifted(name, j, dest, mu):
            await_full(act, (name, j))
            a.done(act.activation(dest, bank((name, j))[:], ACT.Copy, scale=omu[:, mu:mu + 1]), drain((name, j), "act"))

        def prep_act(p, part):
            pr = pairs[p % 2]
            if part == 0:
                for job_name, dest, bias in (("z", pr["sig"], "w0"), ("a", pr["aa"], "a0")):
                    await_full(act, (job_name, p))
                    a.done(act.activation(dest[:], bank((job_name, p))[:], ACT.Sigmoid, bias=col(bias, p)),
                           drain((job_name, p), "act"))
            elif part == 2:
                act.wait_ge(S["cs_ready"], p + 1)
                a.done(act.activation(pr["ep"][:], pr["cs"][:], ACT.Exp, scale=-DECAY), S["exp_ready"])
            elif part == 3:
                a.step(act.activation(pr["sig"][:], pr["sig"][:], ACT.Exp, scale=-DECAY), S["exp_ready"])
            elif part == 4:
                a.done(act.activation(pr["cs"][:], pr["cs"][:], ACT.Exp, scale=DECAY), S["exp_ready"])
            elif part == 7:
                await_drained(act, ("kk", p), "dve")
                a.done(act.activation(pr["sq"][:], pr["sq"][:], ACT.Sqrt), S["root_ready"])
            elif part == 13:
                await_full(act, ("g", p))
                a.done(act.activation(kT[:, p, :], bank(("g", p))[:], ACT.Copy), drain(("g", p), "act"))

        for name in W_IN1:
            if name != W_IN1[-1]:
                convert()
            if name in ("lora0", "lora1"):
                for j in range(2 if name == "lora0" else 1):
                    m = j if name == "lora0" else 2
                    unshifted(name, j, lora[:] if m == 0 else gd[:, m - 1, :], m)
                if name == "lora1":
                    act.wait_ge(S["shift_ready"], 3)
                    a.done(act.activation(lora[0:HD, :], lora[0:HD, :], ACT.Tanh), S["lora_ready"])
                    a.done(act.activation(gd[:], gd[:], ACT.Sigmoid), S["lora_ready"])
            elif name[0] in "krv":
                dest, mu = {"k": (kT, 3), "v": (vT, 7), "r": (rT, 11)}[name[0]]
                for j in range(2):
                    n = 2 * int(name[1]) + j
                    unshifted(name, j, dest[:, n, :], mu + n)
                if name == "v1":
                    prep_act(0, 0)
            elif name[:2] == "pu":
                for j in range(2):
                    await_full(act, (name, j))
                    a.done(act.activation(uT[:, 2 * int(name[2]) + j, :], bank((name, j))[:], ACT.Gelu_apprx_tanh),
                           drain((name, j), "act"))
                if name == "pu0":
                    act.wait_ge(S["pv_std"], 1)
                    a.done(act.activation(rstd[:], rstd[:], ACT.Sqrt), S["pv_root"])
            else:
                half = slice(256 * int(name[2]), 256 * int(name[2]) + 256)
                for j in range(2):
                    await_full(act, (name, j))
                    a.done(act.activation(pv[:, 2 * j:2 * j + 2, half], bank((name, j))[:].rearrange("p (t d) -> p t d", t=2),
                                          ACT.Gelu_apprx_tanh), drain((name, j), "act"))
                if name == "pv0":
                    for part in (7, 2, 3, 4):
                        prep_act(0, part)

        def chunk_act(stage, p, t):
            d = sets[t % 2]
            link = links[t % 2][t // 2]
            if stage not in ("turn", "mv", "q2", "n4", "q4", "r2", "z1", "yl"):
                return
            b = bank((stage, p, t))
            await_full(act, (stage, p, t))
            done = lambda ins: a.done(ins, drain((stage, p, t), "act"))
            copy = lambda o, i: done(act.activation(o, i, ACT.Copy))
            if stage == "turn":
                if (p, t) == (0, 0):
                    act.wait_ge(S["sets_ready"], 1)
                copy(d["z0"][:].rearrange("p (a b) -> p a b", b=HD)[:, 0:4:3, :],
                     b[:, 0:P].rearrange("p (a b) -> p a b", b=HD))
                copy(d["vz"][:, HD:HD + P], b[:, 3 * P:4 * P])
            elif stage == "mv":
                copy(d["z0"][:, HD:HD + P], b[:, 0:P])
            elif stage == "q2":
                copy(d["rq"][:, :, 1, :], b[:, 0:256].rearrange("p (h n) -> p h n", h=2))
                copy(d["nn"][:], b[:, 256:512].rearrange("p (h n) -> p h n", h=2))
            elif stage == "n4":
                copy(d["nd"][:], b[:, 0:256].rearrange("p (h n) -> p h n", h=2))
            elif stage == "q4":
                copy(d["rq"][:, :, 1, :], b[:].rearrange("p (h a n) -> p h a n", h=2, a=2)[:, :, 1, :])
            elif stage == "r2":
                copy(d["nn"][:], b[:, 256:512].rearrange("p (h n) -> p h n", h=2))
            elif stage == "z1":
                copy(d["nd"][:], b[:, 0:256].rearrange("p (h n) -> p h n", h=2))
            elif stage == "yl":
                copy(link["yl"][0:HD, :], b[HD:P, 0:P])
                copy(link["yl"][HD:P, :], b[0:HD, P:2 * P])

        def norm_act(p, part):
            if part == 1:
                await_drained(act, ("var", p), "dve")
                a.done(act.activation(norm_buffers[p]["sq"][:], norm_buffers[p]["sq"][:], ACT.Sqrt), S["norm_root"])

        def mixer_act(n):
            if n == 0:
                await_drained(act, ("hh", PAIRS - 1, TT - 1), "dve")
                a.done(act.activation(act_hi[:, 0:4, :], uT[:], ACT.Copy), S["y_hi"])
                convert()
            elif n == 1:
                act.wait_ge(S["yb_ready"], PAIRS - 1)
                a.done(act.activation(act_hi[:, 4:7, :], vT[:, 0:PAIRS - 1, :], ACT.Copy), S["y_hi"])
            elif n == 2:
                await_drained(act, ("y", PAIRS - 1, TT - 1), "dve")
                await_drained(act, ("state", PAIRS - 1, TT - 1, NCH - 1), "dve")
                convert()
            else:
                act.wait_ge(S["yb_ready"], PAIRS)
                a.done(act.activation(act_hi[:, 7, :], vT[:, PAIRS - 1, :], ACT.Copy), S["y_hi"])

        prep_act(0, 13)
        for kind, *args in CHUNK_SCHEDULE:
            if kind == "stage":
                chunk_act(*args)
            elif kind == "prep":
                prep_act(*args)
            elif kind == "norm":
                norm_act(*args)
            elif kind == "mixer":
                mixer_act(*args)
            elif kind == "mod_rows":
                await_full(act, ("mod_rows", *args))
                a.done(act.activation(acc[:, SEQ * args[0]:SEQ * args[0] + SEQ], bank(("mod_rows", *args))[:], ACT.Copy),
                       drain(("mod_rows", *args), "act"))

        act.dma_start(row_a[:], src["ln1_g"].partition_broadcast(P)).then_inc(load["rows1"], 16)
        act.dma_start(row_b[:], src["ln1_b"].partition_broadcast(P)).then_inc(load["rows1"], 16)
        for n in range(3):
            convert()

        def root_of_variance(n):
            t = (n - 1) % TT
            act.wait_ge(S["var1"], n + 1)
            a.done(act.activation(rstd[:, t:t + 1], rstd[:, t:t + 1], ACT.Sqrt), S["root1"])

        for t in range(TT):
            root_of_variance(1 + t)
        convert()
        affine_hi("h2", 2)

        def ffn_first(m):
            if m:
                convert()
            name = f"up1_{m}"
            await_full(act, (name, 0))
            a.done(act.activation(acc[:, 0:SEQ], bank((name, 0))[:], ACT.Silu), drain((name, 0), "act"))
            await_drained(act, (name, 1), "dve")
            a.done(act.activation(hid_hi[:, m, :], acc[:, SEQ:2 * SEQ], ACT.Copy), S["hid_hi_ready"])

        for m in range(FT):
            ffn_first(m)
        for n in range(FT // 2):
            convert()
            if n == 0:
                await_full(act, (f"up1_{FT - 1}", 1))
                act.dma_start(row2_a[:], src["ln2_g"].partition_broadcast(P)).then_inc(load["rows2"], 16)
                act.dma_start(row2_b[:], src["ln2_b"].partition_broadcast(P)).then_inc(load["rows2"], 16)

        def square_x(e, t):
            act.wait_ge(S["x_ready"], TT * e + t + 1)
            a.done(act.activation(xn2[:, t, :], xres[:, t, :], ACT.Square, accum_out=x_sums[:, t:t + 1]),
                   S["squares_ready"])

        def root_x(e, t):
            act.wait_ge(S["x_rms_ready"], TT * e + t + 1)
            a.done(act.activation(x_sums[:, t:t + 1], x_sums[:, t:t + 1], ACT.Sqrt), S["x_rms_root"])

        def scaled_x(e, t):
            act.wait_ge(S["x_inverse"], TT * e + t + 1)
            a.done(act.activation(xn2[:, t, :], xres[:, t, :], ACT.Copy, scale=x_sums[:, t:t + 1]), S["xn3_ready"])

        for s in range(TT + 3):
            if s < TT:
                root_of_variance(1 + TT + s)
            if 0 <= s - 1 < TT:
                square_x(0, s - 1)
            if 0 <= s - 2 < TT:
                root_x(0, s - 2)
            if 0 <= s - 3 < TT:
                scaled_x(0, s - 3)
            if s == TT - 1:
                convert()
        second_act(act, a, convert, affine_hi, square_x, root_x, scaled_x)

    @block.vector
    def _(dve):
        d = Order(dve, dve_step)
        V = dve
        counts = {"ada": 0}

        def ts(out, in0, s1, s2=None, op0=ALU.mult, op1=None, sem=None):
            d.step(V.tensor_scalar(out, in0, s1, s2, op0, op1) if op1 is not None else
                   V.tensor_scalar(out, in0, s1, None, op0), sem)

        def tt(out, a, b, op, sem=None):
            d.step(V.tensor_tensor(out, a, b, op), sem)

        def stt(out, a, s, b, op0, op1, sem=None):
            d.step(V.scalar_tensor_tensor(out=out, in0=a, scalar=s, in1=b, op0=op0, op1=op1), sem)

        def ada(i):
            n = UNIT_AT[f"ada0_{i}"]
            raw_ready(dve, n)
            if i == 0:
                dve.wait_ge(S["silu_c"], 1)
            r, c = raw[n % RAW][:], col("c", i)
            if i == 0:
                ts(acc[:], r, c, sem=ada_used)
            else:
                stt(acc[:], r, c, acc[:], ALU.mult, ALU.add, sem=ada_used)

        def layer_stats(t, source):
            d.step(V.bn_stats(stats[:, 0, :], source[:, 0:512]))
            d.step(V.bn_stats(stats[:, 1, :], source[:, 512:1024]))
            d.step(V.bn_aggr(mv[:, t, :], stats[:]))

        def normalise():
            ts(rstd[:], mv[:, :, 1], LN_EPS, op0=ALU.add, sem=S["var1"])
            dve.wait_ge(S["root1"], 1)
            d.step(V.reciprocal(rstd[:], rstd[:]))
            for t in range(TT):
                ts(xres[:, t, :], xres[:, t, :], mv[:, t, 0:1], rstd[:, t:t + 1], ALU.subtract, ALU.mult,
                   sem=S["xn_ready"])

        def affine_rows(g, b, sem=None):
            for t in range(TT):
                tt(xres[:, t, :], xres[:, t, :], g[:], ALU.mult)
                tt(xres[:, t, :], xres[:, t, :], b[:], ALU.add, sem if t == TT - 1 else None)

        def affine_lo(stage, part, temp):
            for k in range(KC):
                full = temp[:, k % 2, :]
                await_full(dve, (stage, k))
                await_drained(dve, (stage, k), "act")
                if isinstance(part, str):
                    stt(act_lo[:, k, :], bank((stage, k))[:], col(part, k), act_hi[:, k, :].bitcast(F32), ALU.mult,
                        ALU.subtract, sem=drain((stage, k), "dve"))
                    continue
                ts(full, bank((stage, k))[:], affine[:, part, k:k + 1], affine[:, part + 1, k:k + 1],
                   ALU.mult, ALU.add, sem=drain((stage, k), "dve"))
                tt(act_lo[:, k, :], full, act_hi[:, k, :].bitcast(F32), ALU.subtract, sem=S["h_lo"])

        def mod_columns(jobname, part, g, b, sh, sc):
            await_full(dve, jobname)
            tt(modc[:], bank(jobname)[:, 0:2 * KC], pc[:, COLS[sh]:COLS[sh] + 2 * KC], ALU.add, sem=drain(jobname, "dve"))
            ts(modc[:, KC:], modc[:, KC:], 1.0, op0=ALU.add)
            tt(affine[:, part, :], pc[:, COLS[g]:COLS[g] + KC], modc[:, KC:], ALU.mult)
            tt(affine[:, part + 1, :], pc[:, COLS[b]:COLS[b] + KC], modc[:, KC:], ALU.mult)
            tt(affine[:, part + 1, :], affine[:, part + 1, :], modc[:, 0:KC], ALU.add, sem=S["affine1"])

        d.step(V.memset(ones[:], 1.0))
        d.step(V.memset(restart[:], 1.0))
        d.step(V.memset(restart[:].rearrange("p (c t) -> p c t", t=CH)[:, :, 0:1], 0.0))
        dve.wait_ge(load["params"], 16)
        ts(omu[:], pc[:, COLS["mu_l"]:COLS["mu_l"] + N_MU], -1.0, 1.0, ALU.mult, ALU.add)
        ts(oka[:], pc[:, COLS["k_a"]:COLS["k_a"] + 4], -1.0, 1.0, ALU.mult, ALU.add)
        for i in range(RAW):
            ada(i)
        dve.wait_ge(load["x"], 16)
        for t in range(TT):
            layer_stats(t, xres[:, t, :])
        normalise()
        for i in range(RAW, KC):
            ada(i)
        mod_columns("cols0", 0, "emb_g", "emb_b", "b_sh1", "b_sc1")
        affine_lo("h1", 0, pairs[0]["ar"])
        dve.wait_ge(load["rows0"], 32)
        affine_rows(row_a, row_b)

        def shifted(name, j, dest, mu, sem=None):
            await_drained(dve, (name, j), "act")
            stt(dest[:, 1:SEQ], bank((name, j))[:, 0:SEQ - 1], pc[:, COLS["mu_l"] + mu:COLS["mu_l"] + mu + 1],
                dest[:, 1:SEQ], ALU.mult, ALU.add, sem=drain((name, j), "dve"))

        def prep_dve(p, part):
            pr = pairs[p % 2]
            if part == 1:
                await_drained(dve, ("z", p), "act")
                d.step(V.tensor_tensor_scan(pr["cs"][:], restart[:], pr["sig"][:], 0.0, ALU.mult, ALU.add))
                tt(pr["sig"][:], pr["cs"][:], pr["sig"][:], ALU.subtract, sem=S["cs_ready"])
            elif part == 6:
                await_full(dve, ("kk", p))
                ts(pr["sq"][:], bank(("kk", p))[:], 1e-24, op0=ALU.max, sem=drain(("kk", p), "dve"))
            elif part in (8, 9, 10, 11):
                dve.wait_ge(S["root_ready"], p + 1)
                c = slice((part - 8) * QUARTER, (part - 7) * QUARTER)
                d.step(V.reciprocal(pr["sq"][:, c], pr["sq"][:, c]), S["inverse_ready"] if part == 11 else None)
            elif part == 13 and p:
                bonus_dve(p)

        def bonus_dve(p):
            await_full(dve, ("bonus", p))
            tt(rT[:, p, :], bank(("bonus", p))[:], vT[:, p, :], ALU.mult, sem=drain(("bonus", p), "dve"))

        for n, name in enumerate(W_IN1):
            if name in ("lora0", "lora1"):
                for j in range(2 if name == "lora0" else 1):
                    m = j if name == "lora0" else 2
                    shifted(name, j, lora[:] if m == 0 else gd[:, m - 1, :], m)
                    d.step(V.tensor_copy(stats[:, 0, 0:1], stats[:, 0, 0:1]), S["shift_ready"])
            elif name[0] in "krv":
                dest, mu = {"k": (kT, 3), "v": (vT, 7), "r": (rT, 11)}[name[0]]
                for j in range(2):
                    m = 2 * int(name[1]) + j
                    shifted(name, j, dest[:, m, :], mu + m)
            if n == KC - 1:
                dve.wait_ge(load["gmlp"], 80)
                tt(wsT[:], wsT[:], up[:].unsqueeze(1).to_broadcast([P, 4, P]), ALU.mult, sem=S["wst_ready"])
                for part in (1, 5, 6):
                    prep_dve(0, part)
                    prep_side(d, 0, part)
            if name == "pv0":
                for part in (4, 8, 9, 10, 11, 12):
                    prep_dve(0, part)
                    prep_side(d, 0, part)

        for t in range(TT):
            await_drained(dve, ("pv1", t // 2), "act")
            d.step(V.bn_stats(stats[:, 0, :], pv[:, t, :]))
            d.step(V.bn_aggr(mv[:, t, :], stats[:, 0:1, :]))
        ts(rstd[:], mv[:, :, 1], LN_EPS, op0=ALU.add, sem=S["pv_std"])
        dve.wait_ge(S["pv_root"], 1)
        d.step(V.reciprocal(rstd[:], rstd[:]))
        for t in range(TT):
            ts(pv[:, t, :], pv[:, t, :], mv[:, t, 0:1], rstd[:, t:t + 1], ALU.subtract, ALU.mult)
            tt(pv[:, t, :], pv[:, t, :], sg_g[:], ALU.mult)
            tt(pv[:, t, :], pv[:, t, :], sg_b[:], ALU.add, sem=S["pv_ready"])
        for g in range(4):
            await_full(dve, ("sgu", g))
            tt(sg_g[:].rearrange("p (t n) -> p t n", n=P), bank(("sgu", g))[:].rearrange("p (t n) -> p t n", n=P),
               bs[:, g, :].unsqueeze(1).to_broadcast([P, TT, P]), ALU.add, sem=drain(("sgu", g), "dve"))
            await_drained(dve, ("pu1", 1), "act")
            tt(uT[:, g, :], uT[:, g, :], sg_g[:], ALU.mult)
        await_full(dve, ("pu1", 1))
        await_full(dve, ("sgu", 3))
        for q in range(2):
            d.step(V.memset(sets[q]["vz"][:], 0.0))
        d.step(V.tensor_copy(stats[:, 0, 0:1], stats[:, 0, 0:1]), S["sets_ready"])

        def heads(ap):
            return ap.rearrange("p (h n) -> p h n", h=2)

        def chunk_dve(stage, p, t):
            s, link, ar = sets[t % 2], links[t % 2][t // 2], pairs[p % 2]["ar"]
            name = (stage, p, t)
            if stage in ("mv", "q2", "n4"):
                return
            b = bank(name)
            await_full(dve, name)
            if stage in ("turn", "q4", "r2", "z1", "yl"):
                await_drained(dve, name, "act")
            out_ = drain(name, "dve")
            if stage == "turn":
                rows = chunk_rows[:].unsqueeze(2).to_broadcast([P, NCH, P])
                for key, part in (("bx", 1), ("kx", 2)):
                    tt(s[key][:], b[:, part * P:part * P + P].unsqueeze(1).to_broadcast([P, NCH, P]), rows,
                       ALU.mult, sem=out_)
            elif stage in ("m1", "m2"):
                h = int(stage[1]) - 1
                tt(s["mm"][:, h], b[:].rearrange("p (a n) -> p a n", a=4), masks[:], ALU.mult, sem=out_)
            elif stage in ("n1", "n2"):
                h = int(stage[1]) - 1
                tt(s["nd"][:, h, :], b[:, 0:P], mask_d[:], ALU.mult, sem=out_)
                tt(s["ee"][:, h, :], b[:, 0:P], mask_e[:], ALU.mult, sem=out_)
                if h:
                    tt(s["rq"][:, :, 0, :], s["mm"][:, :, 0, :], ident[:].unsqueeze(1).to_broadcast([P, 2, P]),
                       ALU.add, sem=S["r0_ready"])
            elif stage == "q4":
                tt(s["rb"][:], b[:].rearrange("p (h a n) -> p h a n", h=2, a=2)[:, :, 0, :], s["rq"][:, :, 0, :],
                   ALU.add, sem=out_)
            elif stage == "r2":
                tt(s["rq"][:, :, 0, :], heads(b[:, 0:256]), s["rb"][:], ALU.add, sem=out_)
            elif stage == "r3":
                tt(s["rb"][:], heads(b[:, 0:256]), s["rq"][:, :, 0, :], ALU.add, sem=out_)
            elif stage == "z1":
                d.step(V.tensor_copy(s["z1"][:], b[:, 256:512]), out_)
            elif stage == "z2":
                tt(s["z"][:], b[:, 0:256], s["z1"][:], ALU.add, sem=out_)
                d.step(V.tensor_copy(s["nn"][:, 0, :].rearrange("p (a b) -> p a b", b=HD),
                                     s["z"][:].rearrange("p (a b) -> p a b", b=HD)[:, 0:4:3, :]), S["w_ready"])
            elif stage == "yl":
                tt(link["rp"][0:HD, :], b[0:HD, 0:P], ar[0:HD, 1, tok(t)], ALU.add, sem=out_)
                tt(link["rp"][HD:P, :], b[HD:P, P:2 * P], ar[HD:P, 1, tok(t)], ALU.add, sem=out_)
            elif stage in ("gt", "hh"):
                tt(link["gt" if stage == "gt" else "hb"][:], b[:].rearrange("p (c n) -> p c n", c=NCH),
                   bd64[:].unsqueeze(1).to_broadcast([P, NCH, P]), ALU.mult, sem=out_)

        def chain_dve(p, t, c):
            link, y = links[t % 2][t // 2], norm_buffers[p]["kk"]
            old, new = state[c % 2], state[(c + 1) % 2]
            if (t, c) == (0, 0):
                d.step(V.memset(old[:], 0.0), S["state_zero"])
            g = t * NCH + c
            stt(decayed[:], old[:], pend[p][:, g:g + 1], link["hb"][:, c, :], ALU.mult, ALU.add)
            name = ("state", p, t, c)
            await_full(dve, name)
            tt(new[:], bank(name)[:, 0:P], decayed[:], ALU.add, sem=drain(name, "dve"))
            if c == NCH - 1:
                await_full(dve, ("y", p, t))
                await_drained(dve, ("yl", p, t), "act")
                if (p, t) == (PAIRS - 1, 0):
                    dve.wait_ge(S["yb_ready"], p)
                tt(y[:, tok(t)], bank(("y", p, t))[:, 0:P], link["yl"][:], ALU.add, sem=drain(("y", p, t), "dve"))

        def norm_dve(p, part):
            kk, sq = norm_buffers[p]["kk"], norm_buffers[p]["sq"]
            if part == 0:
                await_full(dve, ("mean", p))
                stt(kk[:], bank(("mean", p))[:], -1.0 / HD, kk[:], ALU.mult, ALU.add, sem=drain(("mean", p), "dve"))
                tt(sq[:], kk[:], kk[:], ALU.mult, sem=S["y_sq"])
            elif part == 1:
                await_full(dve, ("var", p))
                ts(sq[:], bank(("var", p))[:], 1.0 / HD, GN_EPS, ALU.mult, ALU.add, sem=drain(("var", p), "dve"))
            elif part < 6:
                dve.wait_ge(S["norm_root"], p + 1)
                c = slice((part - 2) * QUARTER, (part - 1) * QUARTER)
                d.step(V.reciprocal(sq[:, c], sq[:, c]), S["norm_inverse"] if part == 5 else None)

        bonus_dve(0)
        dve.wait_ge(load["masks"], 16 * 7)
        for kind, *args in CHUNK_SCHEDULE:
            if kind == "stage":
                chunk_dve(*args)
            elif kind == "chain":
                chain_dve(*args)
            elif kind == "prep":
                prep_dve(*args)
            elif kind == "norm":
                norm_dve(*args)
                if args == [PAIRS - 1, 6]:
                    norm_side(d, *args)
            elif kind == "cols1":
                mod_columns("cols1", 2, "ln1_g", "ln1_b", "b_sh2", "b_sc2")
        dve.wait_ge(S["y_hi"], 3)
        tt(act_lo[:, 7, :], vT[:, PAIRS - 1, :], act_hi[:, 7, :].bitcast(F32), ALU.subtract, sem=S["y_lo_last"])

        def residual(stage, t, gate, temp):
            for j in range(2):
                h = slice(SEQ * j, SEQ * j + SEQ)
                await_full(dve, (stage, t, j))
                tt(temp[:, h], bank((stage, t, j))[:], gate[:, h], ALU.mult, sem=drain((stage, t, j), "dve"))
            stt(xres[:, t, :], xres[:, t, :], ALPHA, temp[:], ALU.mult, ALU.add)
            layer_stats(t, xres[:, t, :])
            ts(rstd[:, t:t + 1], mv[:, t, 1:2], LN_EPS, op0=ALU.add, sem=S["var1"])

        def inverse(n, t):
            dve.wait_ge(S["root1"], n + 1)
            d.step(V.reciprocal(rstd[:, t:t + 1], rstd[:, t:t + 1]))

        def x_mean_square(e, t):
            dve.wait_ge(S["squares_ready"], TT * e + t + 1)
            ts(x_sums[:, t:t + 1], x_sums[:, t:t + 1], 1.0 / DM, RMS_EPS, ALU.mult, ALU.add, sem=S["x_rms_ready"])

        def inverse_x(e, t):
            dve.wait_ge(S["x_rms_root"], TT * e + t + 1)
            d.step(V.reciprocal(x_sums[:, t:t + 1], x_sums[:, t:t + 1]), S["x_inverse"])

        await_drained(dve, ("mod_rows", 3), "act")
        for s in range(TT + 1):
            if s < TT:
                residual("mix1", s, acc[:, 0:DM], mixed)
            if s:
                t = s - 1
                inverse(1 + t, t)
                ts(xres[:, t, :], xres[:, t, :], mv[:, t, 0:1], rstd[:, t:t + 1], ALU.subtract, ALU.mult,
                   sem=S["xn_ready"])
        affine_lo("h2", 2, pairs[0]["ar"])
        dve.wait_ge(load["rows1"], 32)
        affine_rows(row_a, row_b)
        for m in range(FT):
            name = f"up1_{m}"
            await_full(dve, (name, 1))
            await_drained(dve, (name, 0), "act")
            tt(acc[:, SEQ:2 * SEQ], bank((name, 1))[:], acc[:, 0:SEQ], ALU.mult, sem=drain((name, 1), "dve"))
            dve.wait_ge(S["hid_hi_ready"], m + 1)
            tt(hid_lo[:, m, :], acc[:, SEQ:2 * SEQ], hid_hi[:, m, :].bitcast(F32), ALU.subtract, sem=S["hid_ready"])
        dve.wait_ge(load["rows2"], 32)
        for s in range(TT + 3):
            if s < TT:
                residual("ff1", s, acc[:, DM:2 * DM], mixed2)
                stt(xres[:, s, :], xres[:, s, :], mv[:, s, 0:1], row2_a[:], ALU.subtract, ALU.mult)
            if 0 <= s - 1 < TT:
                t = s - 1
                inverse(1 + TT + t, t)
                stt(xres[:, t, :], xres[:, t, :], rstd[:, t:t + 1], row2_b[:], ALU.mult, ALU.add, sem=S["x_ready"])
            if 0 <= s - 2 < TT:
                x_mean_square(0, s - 2)
            if 0 <= s - 3 < TT:
                inverse_x(0, s - 3)
        second_dve(dve, d, ts, tt, stt, affine_lo, x_mean_square, inverse_x)

    @block.tensor
    def _(pe):
        used = [0]

        def three(o, l, r, first, last):
            pe.matmul(o, l[0], r[0], start=first, stop=False)
            pe.matmul(o, l[0], r[1], start=False, stop=False)
            return pe.matmul(o, l[1], r[0], start=False, stop=last)

        def next_unit(name):
            i = used[0]
            used[0] += 1
            n = SPLIT_UNITS[i]
            assert UNITS[n][0] == name, (UNITS[n][0], name)
            pe.wait_ge(lo_ready, i + 1)
            kc = UNITS[n][3]
            w = UNIT_SIZE[n] // kc
            return [x[i % SPLIT][:, :kc * w].rearrange("p (k n) -> p k n", k=kc) for x in (whi, wlo)], w

        def dense_feature(name, blocks, beside=None, stage=None):
            (hi, lo), w = next_unit(name)

            def product(j, k):
                c = slice(P * j, P * j + P)
                return three(bank((name, j))[:], (hi[:, k, c], lo[:, k, c]), (act_hi[:, k, :], act_lo[:, k, :]),
                             k == 0, k == KC - 1)

            if stage is not None:
                for j in range(blocks):
                    claim(pe, (name, j))
                for k in range(KC):
                    if stage in ("h1", "h2"):
                        pe.wait_ge(S["h_lo"], KC * (int(stage[1]) - 1) + k + 1)
                    else:
                        await_drained(pe, (stage, k), "dve")
                    for j in range(blocks):
                        mm = product(j, k)
                        if k == KC - 1:
                            mm.then_inc(full_sem((name, j))[0], 1)
                return
            for j in range(blocks):
                claim(pe, (name, j))
                for k in range(KC):
                    if beside is not None:
                        beside(j * KC + k)
                    mm = product(j, k)
                mm.then_inc(full_sem((name, j))[0], 1)

        def dense_token(name, per_bank):
            (hi, lo), w = next_unit(name)
            for j in range(TT // per_bank):
                claim(pe, (name, j))
                for i in range(per_bank):
                    t = per_bank * j + i
                    for k in range(KC):
                        mm = three(bank((name, j))[:, i * w:i * w + w], (act_hi[:, k, tok(t)], act_lo[:, k, tok(t)]),
                                   (hi[:, k, :], lo[:, k, :]), k == 0, k == KC - 1)
                mm.then_inc(full_sem((name, j))[0], 1)

        def rows_product(stage, n, n_units, weights, parts, t, k):
            (hi, lo), (hi_in, lo_in) = weights, parts
            for j in range(2):
                c, f = slice(SEQ * j, SEQ * j + SEQ), 2 * n + k
                last = n == n_units - 1 and k == 1
                mm = three(bank((stage, t, j))[:], (hi_in[:, f, tok(t)], lo_in[:, f, tok(t)]),
                           (hi[:, k, c], lo[:, k, c]), n == k == 0, last)
                if last:
                    mm.then_inc(full_sem((stage, t, j))[0], 1)
            return mm

        def dense_rows(stage, unit, n_units, parts, begun=None, ready=None):
            for n in range(n_units):
                weights = begun if n == 0 and begun else next_unit(f"{unit}_{n}")[0]
                order = [(t, k) for k in range(2) for t in range(TT)]
                if n == n_units - 1:
                    order = [(t, k) for t in range(TT) for k in range(2)]
                elif n == 0:
                    tiles = (TT - 1,) if begun else range(TT)
                    order = [(t, k) for k in range(2) for t in tiles]
                    for t in tiles:
                        for j in range(2):
                            claim(pe, (stage, t, j))
                if ready is not None and n in ready:
                    pe.wait_ge(*ready[n])
                for t, k in order:
                    mm = rows_product(stage, n, n_units, weights, parts, t, k)
                if n < n_units - 1:
                    mm.then_inc(unit_used, 1)

        def columns(name):
            claim(pe, name)
            for j in range(2 * KC):
                mm = pe.matmul(bank(name)[:, j:j + 1], acc[:, P * j:P * j + P], ones[:], start=True, stop=True)
            mm.then_inc(filled[job(name)[0]], 1)

        def turn_x(stage, ready, source=xres, features=range(KC)):
            for k in features:
                claim(pe, (stage, k))
            for t in range(TT):
                pe.wait_ge(ready[0], ready[1] + t + 1)
                for k in features:
                    mm = pe.transpose(bank((stage, k))[:, tok(t)], source[:, t, P * k:P * k + P], ident[:])
                    if t == TT - 1:
                        mm.then_inc(filled[job((stage, k))[0]], 1)

        pe.wait_ge(load["consts"], 32)
        turn_x("h1", (S["xn_ready"], 0), features=range(KC - 1))
        pe.wait_ge(ada_used, KC)
        columns("cols0")
        turn_x("h1", (S["xn_ready"], 0), features=range(KC - 1, KC))

        def fill(name, mm):
            mm.then_inc(filled[job(name)[0]], 1)

        def prep_pe(p, part):
            c, sq = slice(P * p, P * p + P), pairs[p % 2]["sq"]
            if part == 0:
                claim(pe, ("z", p))
                fill(("z", p), pe.matmul(bank(("z", p))[:], wup[0:HD, c], lora[0:HD, :], start=True, stop=True))
                claim(pe, ("a", p))
                fill(("a", p), pe.matmul(bank(("a", p))[:], wup[HD:P, c], lora[HD:P, :], start=True, stop=True))
            elif part == 6:
                claim(pe, ("kk", p))
                pe.wait_ge(S["kk_sq"], p + 1)
                fill(("kk", p), pe.matmul(bank(("kk", p))[:], bd64[:], sq[:], start=True, stop=True))
            elif part == 13:
                claim(pe, ("bonus", p))
                pe.wait_ge(S["prep_ready"], p + 1)
                fill(("bonus", p), pe.matmul(bank(("bonus", p))[:], bd64[:], rT[:, p, :], start=True, stop=True))
                claim(pe, ("g", p))
                pe.matmul(bank(("g", p))[:], gup[:, 0, c], gd[:, 0, :], start=True, stop=False)
                fill(("g", p), pe.matmul(bank(("g", p))[:], gup[:, 1, c], gd[:, 1, :], start=False, stop=True))

        for name in W_IN1:
            if name == "pv0":
                pe.wait_ge(load["masks"], 16 * 7)
                pe.wait_ge(S["lora_ready"], 2)
                prep_pe(0, 0)
                prep_pe(0, 6)
            if name[:2] == "pv":
                dense_token(name, 2)
            else:
                dense_feature(name, 1 if name == "lora1" else 2, stage="h1" if name == W_IN1[0] else None)

        pe.wait_ge(S["wst_ready"], 1)
        pe.wait_ge(S["pv_ready"], TT)
        for g in range(4):
            claim(pe, ("sgu", g))
            for t in range(TT):
                mm = pe.matmul(bank(("sgu", g))[:, tok(t)], pv[:, t, P * g:P * g + P], wsT[:, g, :], start=True, stop=True)
            fill(("sgu", g), mm)

        def chunk_pe(stage, p, t):
            s, pr = sets[t % 2], pairs[p % 2]
            ar, sig, cs, bt, kt = (pr[n] for n in ("ar", "sig", "cs", "bt", "kt"))
            name = (stage, p, t)
            b = bank(name)
            claim(pe, name)
            ready = lambda st, by: await_drained(pe, (st, p, t), by)
            mm = None
            if stage == "turn":
                pe.wait_ge(S["bars_ready"], p + 1)
                for i, x in enumerate((ar[:, 0, tok(t)], sig[:, tok(t)], cs[:, tok(t)], vT[:, p, tok(t)])):
                    mm = pe.transpose(b[:, i * P:i * P + P], x, ident[:])
            elif stage in ("m1", "m2"):
                rows = slice(0, HD) if stage == "m1" else slice(HD, P)
                for i, x in enumerate((bt, kt)):
                    mm = pe.matmul(b[:, 256 * i:256 * i + 256], x[rows, tok(t)], ar[rows, :, tok(t)], start=True, stop=True)
            elif stage in ("n1", "n2"):
                rows = slice(0, HD) if stage == "n1" else slice(HD, P)
                mm = pe.matmul(b[:, 0:P], ar[rows, 0, tok(t)], bt[rows, tok(t)], start=True, stop=True)
            elif stage == "mv":
                ready("turn", "act")
                ready("m2", "dve")
                for h in range(2):
                    mm = pe.matmul(b[:, HD * h:HD * h + HD], s["mm"][:, h, 2, :], s["vz"][:, HD + HD * h:2 * HD + HD * h],
                                   start=True, stop=True)
            elif stage == "q2":
                ready("n2", "dve")
                for h in range(2):
                    pe.matmul(b[:, P * h:P * h + P], s["nd"][:, h, :], s["mm"][:, h, 0, :], start=True, stop=True)
                    mm = pe.matmul(b[:, 256 + P * h:256 + P * h + P], s["mm"][:, h, 0, :], s["nd"][:, h, :],
                                   start=True, stop=True)
            elif stage == "n4":
                ready("q2", "act")
                for h in range(2):
                    mm = pe.matmul(b[:, P * h:P * h + P], s["rq"][:, h, 1, :], s["nn"][:, h, :], start=True, stop=True)
            elif stage == "q4":
                pe.wait_ge(S["r0_ready"], p * TT + t + 1)
                for h in range(2):
                    mm = pe.matmul(b[:, 256 * h:256 * h + 256], s["nn"][:, h, :], s["rq"][:, h, :, :], start=True, stop=True)
            elif stage == "r2":
                ready("n4", "act")
                ready("q4", "dve")
                ready("q4", "act")
                for h in range(2):
                    pe.matmul(b[:, P * h:P * h + P], s["nd"][:, h, :], s["rb"][:, h, :], start=True, stop=True)
                    mm = pe.matmul(b[:, 256 + P * h:256 + P * h + P], s["rq"][:, h, 1, :], s["nd"][:, h, :],
                                   start=True, stop=True)
            elif stage == "r3":
                ready("r2", "dve")
                ready("r2", "act")
                for h in range(2):
                    mm = pe.matmul(b[:, P * h:P * h + P], s["nn"][:, h, :], s["rq"][:, h, 0, :], start=True, stop=True)
            elif stage == "z1":
                ready("r3", "dve")
                ready("mv", "act")
                for h in range(2):
                    pe.matmul(b[:, P * h:P * h + P], s["ee"][:, h, :], s["rb"][:, h, :], start=True, stop=True)
                    mm = pe.matmul(b[:, 256 + P * h:256 + P * h + P], s["rb"][:, h, :], s["z0"][:, P * h:P * h + P],
                                   start=True, stop=True)
            elif stage == "z2":
                ready("z1", "act")
                ready("z1", "dve")
                for h in range(2):
                    mm = pe.matmul(b[:, P * h:P * h + P], s["nd"][:, h, :], s["z1"][:, P * h:P * h + P], start=True, stop=True)
            elif stage == "yl":
                ready("z2", "dve")
                for h in range(2):
                    c = slice(P * h, P * h + P)
                    pe.matmul(b[:, c], s["z"][:, c], s["mm"][:, h, 1, :], start=True, stop=False)
                    mm = pe.matmul(b[:, c], s["vz"][:, c], s["mm"][:, h, 3, :], start=False, stop=True)
            elif stage == "gt":
                pe.wait_ge(S["w_ready"], p * TT + t + 1)
                mm = pe.matmul(b[:], s["nn"][:, 0, :], s["bx"][:], start=True, stop=True)
            elif stage == "hh":
                for c in range(NCH):
                    o = b[:, P * c:P * c + P]
                    pe.matmul(o, s["bx"][:, c, :], s["z"][:, HD:HD + P], start=True, stop=False)
                    mm = pe.matmul(o, s["kx"][:, c, :], s["vz"][:, HD:HD + P], start=False, stop=True)
            fill(name, mm)

        def chain_pe(p, t, c):
            link, old = links[t % 2][t // 2], state[c % 2]
            if c == 0:
                claim(pe, ("y", p, t))
                await_drained(pe, ("hh", p, t), "dve")
            if (t, c) == (0, 0):
                pe.wait_ge(S["state_zero"], p + 1)
            else:
                await_drained(pe, ("state", p, t if c else t - 1, c - 1 if c else NCH - 1), "dve")
            mm = pe.matmul(bank(("y", p, t))[:, CH * c:CH * c + CH], old[:], link["rp"][:, CH * c:CH * c + CH],
                           start=True, stop=True)
            if c == NCH - 1:
                fill(("y", p, t), mm)
            name = ("state", p, t, c)
            claim(pe, name)
            fill(name, pe.matmul(bank(name)[:, 0:P], link["gt"][:, c, :], old[:], start=True, stop=True))

        def norm_pe(p, part):
            if part == 0:
                claim(pe, ("mean", p))
                await_drained(pe, ("y", p, TT - 1), "dve")
                fill(("mean", p), pe.matmul(bank(("mean", p))[:], bd64[:], norm_buffers[p]["kk"][:], start=True, stop=True))
            elif part == 1:
                claim(pe, ("var", p))
                pe.wait_ge(S["y_sq"], p + 1)
                fill(("var", p), pe.matmul(bank(("var", p))[:], bd64[:], norm_buffers[p]["sq"][:], start=True, stop=True))

        def mod_rows(j):
            if j == 0:
                pe.wait_ge(load["bias"], 16)
                pe.wait_ge(ada_used, 3 * KC)
            claim(pe, ("mod_rows", j))
            b = bank(("mod_rows", j))
            pe.matmul(b[:], ones[:].to_broadcast([P, P]), acc[:, SEQ * j:SEQ * j + SEQ], start=True, stop=False)
            fill(("mod_rows", j), pe.matmul(b[:], ident[0:4, j:j + 1].to_broadcast([4, P]), bias4[:], start=False, stop=True))

        begun = []

        def out1(t, k):
            if (t, k) == (0, 0):
                begun.append(next_unit("out1_0")[0])
                pe.wait_ge(S["y_lo"], 1)
            if k == 0:
                for j in range(2):
                    claim(pe, ("mix1", t, j))
            rows_product("mix1", 0, 4, begun[0], (act_hi, act_lo), t, k)

        prep_pe(0, 13)
        for kind, *args in CHUNK_SCHEDULE:
            if kind == "stage":
                chunk_pe(*args)
            elif kind == "chain":
                chain_pe(*args)
            elif kind == "prep":
                prep_pe(*args)
            elif kind == "norm":
                norm_pe(*args)
            elif kind == "cols1":
                pe.wait_ge(ada_used, 2 * KC)
                columns("cols1")
            elif kind == "mod_rows":
                mod_rows(*args)
            elif kind == "out1":
                out1(*args)

        dense_rows("mix1", "out1", 4, (act_hi, act_lo), begun[0], {2: (S["y_lo"], 2), 3: (S["y_lo_last"], 1)})
        turn_x("h2", (S["xn_ready"], TT))
        for m in range(FT):
            dense_feature(f"up1_{m}", 2, stage=None if m else "h2")
        pe.wait_ge(S["hid_ready"], FT)
        dense_rows("ff1", "down1", FT // 2, (hid_hi, hid_lo))
        second_pe(pe, three, next_unit, dense_feature, dense_token, dense_rows, turn_x, fill)

    ctx.close()


def lay_out(inputs):
    x = {k: np.asarray(v) for k, v in inputs.items()}
    c = lambda v: np.asarray(v).reshape(-1, P).T
    base = 2 * MIX
    mu = x["mu_shift"][0]
    lora = 3 * MIX
    ffn = x["ffn_conv_w_2"][0]
    b = x["b_ada"][0].reshape(6, DM)
    cols = {"c": c(x["c"]), "emb_g": c(x["emb_ln_g"]), "emb_b": c(x["emb_ln_b"]), "mu_l": c(mu[lora:lora + 128]),
            "mu_g0": c(mu[lora + 128:lora + 256]), "mu_g1": c(mu[lora + 160:lora + 288]),
            "mu_r": c(mu[:MIX]), "mu_k": c(mu[MIX:2 * MIX]), "mu_v": c(mu[2 * MIX:3 * MIX]),
            "ln1_g": c(x["ln1_g"]), "ln1_b": c(x["ln1_b"]), "nmp": c(x["norm_mix_pre_2"]), "nfp": c(x["norm_ffn_pre_2"]),
            "cmix": c(x["conv_mix_w_2"]), "cffn": c(ffn),
            "pe_k": np.tile(x["pe_cmp_k_2"][0].T, (2, 1)), "pe_v": np.tile(x["pe_cmp_v_2"][0].T, (2, 1)),
            "has_key": (np.arange(P)[:, None] >= L_CMP - 1).astype(np.float32),
            "b_sh1": c(b[0]), "b_sc1": c(b[1]), "b_sh2": c(b[3]), "b_sc2": c(b[4])}
    for n in ("w0", "a0", "k_k", "k_a", "r_k", "lnx_g", "lnx_b"):
        cols[n] = c(x[n])
    params = np.concatenate([cols[n] for n in COLS], 1)
    parts = []
    for _, matrix, row, tiles, ranges in UNITS:
        w = x[matrix][0]
        w = np.concatenate([w[row:row + tiles * P, a:a + n] for a, n in ranges], 1)
        parts.append(w.reshape(tiles, P, -1).transpose(1, 0, 2).reshape(P, -1))
    g_up = np.zeros((P, 2, MIX), np.float32)
    g_up[:, 0] = x["g_up"][0][:P]
    g_up[P - 32:, 1] = x["g_up"][0][P:]
    return {
        "x": x["x"], "params": params, "weights": np.concatenate(parts, 1), "consts": shape_constants(),
        "w_s_t": x["w_s"][0].transpose(2, 0, 1), "b_s": x["b_s"][0], "sg_ln_g": x["sg_ln_g"][0], "sg_ln_b": x["sg_ln_b"][0],
        "emb_ln_g": x["emb_ln_g"], "emb_ln_b": x["emb_ln_b"], "ln1_g": x["ln1_g"][0], "ln1_b": x["ln1_b"][0],
        "ln2_g": x["ln2_g"][0], "ln2_b": x["ln2_b"][0], "lora_up": np.concatenate([x["w_up"][0], x["a_up"][0]], 0),
        "w1": np.stack([x[f"w_cmp_{n}1_2"][0].reshape(L_CMP // 2, P, CMP_HID).transpose(1, 0, 2) for n in "kv"]),
        "w2k": np.tile(x["w_cmp_k2_2"][0].reshape(2, P, HD).transpose(1, 0, 2), (1, 1, 2)),
        "w2v": x["w_cmp_v2_2"][0].reshape(2, P, HD).transpose(1, 0, 2), "rel_bias_t": x["rel_bias_2"].T,
        "mix_post": x["norm_mix_post_2"][0], "ffn_post": x["norm_ffn_post_2"][0],
        "g_up_pad": g_up, "b_gates": np.concatenate([b[2], b[5]]).reshape(4, SEQ),
    }


def kernel(**inputs):
    import concourse.bacc as bacc
    from concourse.bass_utils import run_bass_kernel_spmd

    nc = bacc.Bacc("TRN2", target_bir_lowering=False, num_devices=1)
    arrays = {f"in_{n}": np.ascontiguousarray(a) for n, a in lay_out(inputs).items()}
    src = {n[3:]: nc.dram_tensor(n, a.shape, mybir.dt.from_np(a.dtype), kind="ExternalInput").ap()
           for n, a in arrays.items()}
    out = nc.dram_tensor("out", (1, SEQ, DM), F32, kind="ExternalOutput").ap()
    build(nc, src, out)
    return run_bass_kernel_spmd(nc, [arrays], core_ids=[0]).results[0]["out"]
```

```python
import math

import numpy as np

import concourse.bass as bass
from concourse import mybir

F32 = mybir.dt.float32
F32R = mybir.dt.float32r
ACT = mybir.ActivationFunctionType
ALU = mybir.AluOpType
AX_X = mybir.AxisListType.X

P = 128
SEQ = 512
TT = SEQ // P
DM = 1024
KC = DM // P
MIX = 512
PAIRS = MIX // P
HD = 64
CH = 32
NCH = P // CH
FFN = 2816
FT = FFN // P
ALPHA = 2.0 ** 0.25
LN_EPS, GN_EPS, RMS_EPS = 1e-5, 64e-5, 1e-6
DECAY = math.exp(-0.5)
N_HEADS, N_KV, REP = 8, 2, 4
L_CMP, S_CMP = 32, 16
N_CMP = (SEQ - L_CMP) // S_CMP + 1
CMP_HID = 256
N_BUCKETS, MAX_DIST = 32, 128
NEG = -1e30
GRID = SEQ + P

COLS, N_COLS = {}, 0
for _name, _n in (("c", KC), ("emb_g", KC), ("emb_b", KC), ("mu_l", 1), ("mu_g0", 1), ("mu_g1", 1),
                  ("mu_k", 4), ("mu_v", 4), ("mu_r", 4), ("w0", 4), ("a0", 4), ("k_k", 4), ("k_a", 4),
                  ("r_k", 4), ("lnx_g", 4), ("lnx_b", 4), ("ln1_g", KC), ("ln1_b", KC), ("nmp", KC),
                  ("nfp", KC), ("cmix", 12), ("cffn", 3 * 2 * FT), ("pe_k", L_CMP), ("pe_v", L_CMP),
                  ("has_key", 1), ("b_sh1", KC), ("b_sc1", KC), ("b_sh2", KC), ("b_sc2", KC)):
    COLS[_name] = N_COLS
    N_COLS += _n
N_MU = 15

CONSTS = {"ident": (0, 128), "bd64": (128, 128), "up": (256, 128), "mask_qr": (384, 256),
          "mask_mk": (640, 256), "mask_d": (896, 128), "mask_e": (1024, 128), "chunk_rows": (1152, 4),
          "onehot": (1156, GRID), "future": (1156 + GRID, SEQ)}
N_CONST = 1156 + GRID + SEQ


def shape_constants():
    c = np.zeros((P, N_CONST), np.float32)
    p, f = np.arange(P)[:, None], np.arange(P)[None, :]

    def put(name, v):
        at, n = CONSTS[name]
        c[:, at:at + n] = v

    same = lambda n: (p // n) == (f // n)
    put("ident", p == f)
    put("bd64", same(64))
    put("up", p <= f)
    put("mask_qr", np.concatenate([(p < f) & same(16), (p <= f) & same(CH)], 1))
    put("mask_mk", np.concatenate([(p < f) & same(CH), (p <= f) & same(CH)], 1))
    put("mask_d", (p > f) & same(16))
    put("mask_e", (p > f) & same(CH) & ~same(16))
    put("chunk_rows", (p // CH) == np.arange(NCH)[None, :])
    dist = (SEQ - 1) - np.arange(GRID)
    exact = N_BUCKETS // 2
    d = np.maximum(dist, 0)
    df = np.maximum(d, 1).astype(np.float32)
    scaled = np.log(df / np.float32(exact)) / np.float32(math.log(MAX_DIST / exact))
    large = exact + (scaled * np.float32(N_BUCKETS - exact)).astype(np.int32)
    bucket = np.where(d < exact, d, np.minimum(large, N_BUCKETS - 1))
    c[:N_BUCKETS, CONSTS["onehot"][0]:][:, :GRID] = bucket[None, :] == np.arange(N_BUCKETS)[:, None]
    put("future", np.where(p + 384 - np.arange(SEQ)[None, :] < 0, -NEG, 0.0))
    return c


def weight_units():
    units = [(f"ada0_{k}", "w_ada", k * P, 1, ((0, 2 * DM),)) for k in range(KC)]
    base = 2 * MIX
    lora = base + 3 * MIX
    win = [("lora0", ((lora, 256),)), ("lora1", ((lora + 160, 128),))]
    win += [(f"k{j}", ((base + MIX + 256 * j, 256),)) for j in range(2)]
    win += [(f"r{j}", ((base + 256 * j, 256),)) for j in range(2)]
    win += [(f"v{j}", ((base + 2 * MIX + 256 * j, 256),)) for j in range(2)]
    win += [(f"pv{j}", ((MIX + 256 * j, 256),)) for j in range(2)]
    win += [(f"pu{j}", ((256 * j, 256),)) for j in range(2)]
    ada = [(f"ada1_{k}", "w_ada", k * P, 1, ((3 * DM, 2 * DM),)) for k in range(KC)]
    ada += [(f"ada2_{k}", "w_ada", k * P, 1, ((2 * DM, DM), (5 * DM, DM))) for k in range(KC)]
    units += [(name, "w_in", 0, KC, ranges) for name, ranges in win] + ada
    units += [(f"out1_{n}", "w_out", 2 * n * P, 2, ((0, DM),)) for n in range(4)]
    for m in range(FT):
        units.append((f"up1_{m}", "w_ffn_in", 0, KC, ((m * P, P), (FFN + m * P, P))))
    for n in range(FT // 2):
        units.append((f"down1_{n}", "w_ffn_out", 2 * n * P, 2, ((0, DM),)))
    kv = MIX
    win2 = [("cmp", ((kv, 256),))] + [(f"q{j}", ((256 * j, 256),)) for j in range(2)]
    win2 += [("slc", ((kv + 256, 256),)), ("win", ((kv + 512, 256),)), ("gates", ((kv + 768, 24),))]
    for part, name in ((1, "cg"), (2, "xt"), (0, "bg")):
        win2 += [(f"{name}{j}", ((kv + 792 + part * MIX + 256 * j, 256),)) for j in range(2)]
    units += [(name, "w_in_2", 0, KC, ranges) for name, ranges in win2]
    units += [(f"out2_{n}", "w_out_2", 2 * ((n + 2) % 4) * P, 2, ((0, DM),)) for n in range(4)]
    units += [(f"up2_{m}", "w_ffn_up_2", 0, KC, ((m * P, P), (FFN + m * P, P))) for m in range(FT)]
    units += [(f"down2_{n}", "w_ffn_down_2", 2 * n * P, 2, ((0, DM),)) for n in range(FT // 2)]
    return units


UNITS = weight_units()
UNIT_AT = {u[0]: n for n, u in enumerate(UNITS)}
UNIT_SIZE = [u[3] * sum(w for _, w in u[4]) for u in UNITS]
UNIT_START = [sum(UNIT_SIZE[:n]) for n in range(len(UNITS) + 1)]
SPLIT_UNITS = [n for n, u in enumerate(UNITS) if u[1] != "w_ada"]
SPLIT_AT = {n: i for i, n in enumerate(SPLIT_UNITS)}
ADA_PE = (1, 4)
RAW, SPLIT = 3, 2


TILE_ORDER = ((0, 1, 3, 2), (0, 1, 2, 3))


class Order:

    def __init__(self, eng, own):
        self.eng, self.own, self.count, self.last = eng, own, {}, None

    def done(self, ins, sem=None):
        sem = self.own if sem is None else sem
        self.count[sem.name] = self.count.get(sem.name, 0) + 1
        ins.then_inc(sem, 1)
        self.last = (sem, self.count[sem.name])

    def settle(self):
        self.eng.wait_ge(*self.last)

    def step(self, ins, sem=None):
        self.done(ins, sem)
        self.settle()


class Banks:

    def __init__(self):
        self.fills = [0] * 8
        self.drains = {"dve": [0] * 8, "act": [0] * 8}
        self.of = {}
        self.turn = 0
        self.shared = range(4, 8)

    def add(self, name, bank=None, dve=0, act=0, unit=None):
        if bank is None:
            bank = self.shared[self.turn % len(self.shared)]
            self.turn += 1
        before = {e: self.drains[e][bank] for e in self.drains}
        if unit is None:
            self.fills[bank] += 1
        self.drains["dve"][bank] += dve
        self.drains["act"][bank] += act
        after = {e: self.drains[e][bank] for e in self.drains}
        self.of[name] = (bank, self.fills[bank] if unit is None else SPLIT_AT[UNIT_AT[unit]] + 1, before, after,
                         unit is not None)


def plan_banks():
    b = Banks()
    turn = [0]

    def dense(name, drains):
        pair = 2 * (turn[0] % 2)
        turn[0] += 1
        for j, drain in enumerate(drains):
            b.add((name, j), pair + j, unit=name if j == len(drains) - 1 else None, **drain)

    def dense_rows(name, last_unit, act=0):
        for t in range(TT):
            for j in range(2):
                b.add((name, t, j), 2 * t + j, dve=1, act=act, unit=last_unit if (t, j) == (TT - 1, 1) else None)

    for k in range(KC - 1):
        b.add(("h1", k), k, dve=1, act=1)
    b.add("cols0", KC - 1, dve=1)
    b.add(("h1", KC - 1), KC - 1, dve=1, act=1)
    for name in ("lora0", "lora1", "k0", "k1", "r0", "r1", "v0", "v1"):
        dense(name, drains=[dict(dve=1, act=1)] * (1 if name == "lora1" else 2))
    plan_prep(b, 0, 0)
    plan_prep(b, 0, 6)
    for name in ("pv0", "pv1", "pu0", "pu1"):
        dense(name, drains=[dict(act=1)] * 2)
    for g in range(4):
        b.add(("sgu", g), dve=1)
    plan_prep(b, 0, 13)
    b.shared = range(2, 8)
    for kind, *args in CHUNK_SCHEDULE:
        if kind == "stage":
            stage, p, t = args
            drains = dict(CHUNK_STAGES)[stage]
            if stage in TWO_BANKS:
                b.add((stage, p, t), dve=drains["dve"])
                b.add((stage + "_act", p, t), act=drains["act"])
            else:
                b.add((stage, p, t), **drains)
        elif kind == "chain":
            p, t, c = args
            last = (p, t // 2) == (PAIRS - 1, 1)
            if c == 0:
                b.add(("y", p, t), 6 if last else t % 2, dve=1)
            b.add(("state", p, t, c), 7 if last else None, dve=1)
        elif kind == "prep":
            plan_prep(b, *args)
        elif kind == "cols1":
            b.add(("cols1", args[0]), dve=1)
        elif kind == "norm" and args[1] < 2:
            b.add((("mean", "var")[args[1]], args[0]), 7 if args[0] == PAIRS - 1 else None, dve=1)
    b.shared = range(4, 8)
    for j in range(4):
        b.add(("mod_rows", j), j, act=1)
    dense_rows("mix1", "out1_3")
    for k in range(KC):
        b.add(("h2", k), k, dve=1, act=1)
    for m in range(FT):
        dense(f"up1_{m}", drains=[dict(act=1), dict(dve=1)])
    dense_rows("ff1", f"down1_{FT // 2 - 1}")
    plan_second(b, dense, dense_rows)
    return b.of


def plan_prep(b, p, part):
    for name, at, drain in (("z", 0, dict(act=1)), ("a", 0, dict(act=1)), ("kk", 6, dict(dve=1)),
                            ("bonus", 13, dict(dve=1)), ("g", 13, dict(act=1))):
        if at == part:
            b.add((name, p), **drain)


TWO_BANKS = ("turn", "q4", "r2", "z1")
CHUNK_STAGES = (("turn", dict(dve=2, act=2)), ("m1", dict(dve=1)), ("m2", dict(dve=1)), ("n1", dict(dve=2)),
                ("n2", dict(dve=2)), ("mv", dict(act=1)), ("q2", dict(act=2)), ("n4", dict(act=1)),
                ("q4", dict(dve=1, act=1)), ("r2", dict(dve=1, act=1)), ("r3", dict(dve=1)),
                ("z1", dict(dve=1, act=1)), ("z2", dict(dve=1)), ("yl", dict(dve=2, act=2)),
                ("gt", dict(dve=1)), ("hh", dict(dve=1)))
PREP_EVEN = {2: (0,), 4: (1,), 5: (2, 3,), 8: (4,)}
PREP_ODD = {0: (5,), 4: (6,), 5: (7,), 6: (8,), 7: (9,), 8: (10,), 9: (11,), 11: (12,)}
BONUS_AT = 5
NORM_EVEN = {11: (0,), 12: (1, 2, 3,), 14: (4, 5,), 15: (6,)}
ADA_EVEN, ADA_ODD = (0, 2, 4), (12, 14)
NORM_PARTS = 7
COLS1_AT = (7, 9, 11, 13)
QUARTER = SEQ // 4


def chunk_schedule():
    order, before, adas = [], [], 0
    for p in range(PAIRS):
        for first in (0, 2):
            tiles = (first, first + 1)
            for n, (stage, _) in enumerate(CHUNK_STAGES):
                order += [("stage", stage, p, t) for t in tiles]
                if 3 <= n < len(before) + 3:
                    order.append(before[n - 3])
                if p + 1 < PAIRS:
                    order += [("prep", p + 1, part) for part in (PREP_ODD if first else PREP_EVEN).get(n, ())]
                if not first and p:
                    order += [("norm", p - 1, part) for part in NORM_EVEN.get(n, ())]
                    order += [("prep", p, 13)] if n == BONUS_AT else []
                if n in (ADA_ODD if first else ADA_EVEN) and adas < 2 * KC:
                    adas += 1
                    order.append(("ada", adas))
                if (p, first) == (1, 2) and n in COLS1_AT:
                    order.append(("cols1", COLS1_AT.index(n)))
            before = [("chain", p, t, c) for t in tiles for c in range(NCH)]
    order.append(("mixer", 0))
    for n, step in enumerate(before):
        order.append(step)
        if n < 4:
            order.append(("mod_rows", n))
        if n == 3:
            order.append(("mixer", 1))
        if n in (6, 7):
            order.append(("out1", 0, n - 6))
    order += [("mixer", 2), ("norm", PAIRS - 1, 0), ("out1", 1, 0), ("out1", 1, 1), ("norm", PAIRS - 1, 1),
              ("out1", 2, 0), ("out1", 2, 1)]
    return order + [("norm", PAIRS - 1, part) for part in range(2, NORM_PARTS)] + [("mixer", 3)]


CHUNK_SCHEDULE = chunk_schedule()


ITEMS = [(br, h, i) for br in ("slc", "win", "cmp") for h in range(N_HEADS) for i in range(TT)]
N_SLOTS = len(ITEMS) + 3
SLOT_UNITS = ("cg0", "cg1", "xt0", "xt1", "bg0", "bg1")
PER_UNIT = -(-N_SLOTS // len(SLOT_UNITS))
FIRST_UNITS = ("cmp", "q0", "q1", "slc", "win", "gates")


def slots_of(n):
    return range(PER_UNIT * n, min(PER_UNIT * (n + 1), N_SLOTS))


def stages_of(slot):
    return [(st, slot - lag) for st, lag in (("scores", 0), ("turn2", 2), ("values", 3))
            if 0 <= slot - lag < len(ITEMS)]


def n_keys(item):
    br, _, i = ITEMS[item]
    return (P // S_CMP) * i + P // S_CMP - 1 if br == "cmp" else P * (i + 1)


def plan_second(b, dense, dense_rows):
    for k in range(KC):
        b.add(("h3", k), k, dve=1, act=1)
    for name in FIRST_UNITS:
        dense(name, drains=[dict(act=1)] * (1 if name == "gates" else 2))
        if name == "cmp":
            for j in range(2):
                b.add(("bias", j), act=1)
        if name in ("q1", "win"):
            kv = "k" if name == "q1" else "v"
            if name == "win":
                b.add(("turn_v", "slc"), act=1)
            b.add(("hidden", kv), act=1)
            b.add(("compressed", kv), act=1)
    for name in ("win", "gates"):
        b.add(("turn_v", name), act=1)
    for n, name in enumerate(SLOT_UNITS):
        dense(name, drains=[dict(act=1) if name[:2] == "cg" else dict(dve=1)] * 2)
        for slot in slots_of(n):
            for st, item in stages_of(slot):
                b.add((st, item), **(dict(act=1) if st == "turn2" else dict(dve=1)))
    for k in range(PAIRS):
        b.add(("turn_o", k), act=1, dve=1)
    dense_rows("mix2", "out2_3", act=1)
    for k in range(KC):
        b.add(("h4", k), k, dve=1, act=1)
    for m in range(FT):
        dense(f"up2_{m}", drains=[dict(act=1, dve=1)] * 2)
    dense_rows("ff2", f"down2_{FT // 2 - 1}", act=1)


def build(nc, src, out):
    bank_of = plan_banks()
    byte = {"at": (nc.sbuf_base + 63) // 64 * 64}
    from contextlib import ExitStack
    ctx = ExitStack()

    def place(name, shape, dt=F32, at=None):
        size = (4 * int(np.prod(shape[1:])) + 31) // 32 * 32
        if at is None:
            at = byte["at"]
            byte["at"] += size
        t = nc.alloc_sbuf_tensor_at(name, list(shape), dt, offset=at)
        return t, at + size

    def sem(name):
        return ctx.enter_context(nc.semaphore(name))

    raw = [place(f"raw{i}", [P, 2048])[0] for i in range(RAW)]
    whi, wlo = zip(*((place(f"weight_hi{i}", [P, 2048], F32R)[0], place(f"weight_lo{i}", [P, 2048], F32R)[0])
                     for i in range(SPLIT)))
    act_at = byte["at"]
    slots_at = act_at - 2 * SPLIT * 8192
    act_hi, _ = place("act_hi", [P, KC, SEQ], F32R)
    act_lo, _ = place("act_lo", [P, KC, SEQ], F32R)
    xres, _ = place("xres", [P, TT, DM])
    acc, _ = place("acc", [P, 2 * DM])
    pc, _ = place("params", [P, N_COLS])
    omu, _ = place("one_minus_mu", [P, N_MU])
    oka, _ = place("one_minus_ka", [P, 4])
    affine, _ = place("affine", [P, 4, KC])
    modc, _ = place("mod_columns", [P, 2 * KC])
    ident, _ = place("ident", [P, P])
    bd64, _ = place("bd64", [P, P])
    stats, _ = place("stats", [P, 2, 6])
    mv, _ = place("mean_var", [P, TT, 2])
    rstd, _ = place("rstd", [P, TT])
    ones, _ = place("ones", [P, 1])
    bias4, _ = place("bias4", [4, SEQ])
    byte["small"] = byte["at"]
    byte["at"] += 64
    arena = byte["at"]

    nxt = arena
    def here(name, shape, dt=F32):
        nonlocal nxt
        t, nxt = place(name, shape, dt, nxt)
        return t
    kT, rT, vT = (here(f"{n}T", [P, PAIRS, SEQ]) for n in "krv")
    lora = here("lora", [P, SEQ])
    gd = here("gd", [P, 2, SEQ])
    uT = here("uT", [P, 4, SEQ])
    wup = here("wup", [P, MIX])
    gup = here("gup", [P, 2, MIX])
    chunk_rows = here("chunk_rows", [P, NCH])
    masks = here("masks", [P, 4, P])
    mask_d = here("mask_d", [P, P])
    mask_e = here("mask_e", [P, P])
    restart = here("restart", [P, SEQ])
    state = [here(f"state{i}", [P, P]) for i in range(2)]
    decayed = here("decayed", [P, P])
    pend = [here(f"chunk_decay{i}", [P, SEQ // CH]) for i in range(PAIRS)]
    gm_at = nxt
    pv = here("pv", [P, TT, MIX])
    wsT = here("wsT", [P, 4, P])
    bs = here("bs", [P, 4, P])
    sg_g = here("sg_g", [P, MIX])
    sg_b = here("sg_b", [P, MIX])
    gm_end = nxt
    pair_at = nxt
    def pair_buffers(i):
        small = ("sig", "cs", "aa", "ep", "bt", "kt")
        shapes = [(n, [P, SEQ]) for n in small] + [("ar", [P, 2, SEQ])] + [(n, [P, SEQ]) for n in ("kk", "sq")]
        return {name: here(f"{name}_{i}", shape) for name, shape in shapes}
    pairs = [pair_buffers(0)]
    pair_end = nxt
    row_a, _ = place("row_a", [P, DM], F32, pair_at)
    row_b, _ = place("row_b", [P, DM], F32, pair_at + 4096)
    up, _ = place("up", [P, P], F32, pair_at + 8192)
    assert pair_end <= nc.sbuf_usable_end, (pair_end, nc.sbuf_usable_end)

    link_shapes = (("gt", [P, NCH, P]), ("hb", [P, NCH, P]), ("rp", [P, P]), ("yl", [P, P]))
    nxt = slots_at
    pairs.append(pair_buffers(1))
    norm_buffers = [pairs[p % 2] if p < PAIRS - 1 else pairs[0] for p in range(PAIRS)]
    links = [[{name: here(f"{name}_{q}1", shape) for name, shape in link_shapes}] for q in range(2)]
    assert nxt <= act_at
    sets = []
    nxt = act_at
    gap = act_at + 2 * KC * SEQ * 4
    def chunk(name, shape):
        nonlocal nxt
        size = (4 * int(np.prod(shape[1:])) + 31) // 32 * 32
        if nxt <= gap and nxt + size > gap:
            nxt = gm_at
        t, nxt = place(name, shape, F32, nxt)
        assert nxt <= gap or gm_at < nxt <= gm_end, (name, nxt)
        return t
    for q in range(2):
        d = {}
        for name, shape in (("mm", [P, 2, 4, P]), ("nd", [P, 2, P]), ("ee", [P, 2, P]),
                            ("rq", [P, 2, 2, P]), ("nn", [P, 2, P]), ("rb", [P, 2, P]), ("z0", [P, 256]),
                            ("z1", [P, 256]), ("z", [P, 256]), ("bx", [P, NCH, P]), ("kx", [P, NCH, P]),
                            ("vz", [P, 256])):
            d[name] = chunk(f"{name}_{q}", shape)
        sets.append(d)
        links[q].insert(0, {name: chunk(f"{name}_{q}0", shape) for name, shape in link_shapes})

    hid_hi, e1 = place("hid_hi", [P, FT, SEQ], F32R, arena)
    hid_lo, e1 = place("hid_lo", [P, FT, SEQ], F32R, e1)
    assert e1 <= nc.sbuf_usable_end, (e1, nc.sbuf_usable_end)

    nxt = arena
    xn2, _ = place("xn2", [P, TT, DM], F32, nxt)
    w1 = here("w1", [P, L_CMP // 2, CMP_HID])
    qT = here("qT", [P, PAIRS, SEQ])
    kvc = here("kvc", [P, 2, SEQ])
    ksl = here("ksl", [P, 2, SEQ])
    kwn = here("kwn", [P, 2, SEQ])
    vsl = here("vsl", [P, TT, P])
    vwn = here("vwn", [P, TT, P])
    gate = here("gate", [P, TT, 24])
    bgT = here("bgT", [P, 4, SEQ])
    cgT = here("cgT", [P, 4, SEQ])
    strip = here("strip", [P, N_HEADS, SEQ])
    o_at = nxt
    o = here("o", [P, TT, MIX])
    onehot, z = place("onehot", [P, GRID], F32, o_at)
    future, z = place("future", [P, SEQ], F32, z)
    grow, z = place("grow", [N_HEADS, GRID], F32, z)
    assert z <= nxt
    blk = here("blk", [P, L_CMP // 2, 2 * N_CMP])
    w2k = here("w2k", [P, 2, P])
    w2v = here("w2v", [P, 2, HD])
    hc = here("hc", [P, 2, 2 * N_CMP])
    kc2 = here("kc2", [P, 2, N_CMP])
    vc = here("vc", [P, 2, HD])
    relb = here("relb", [P, N_HEADS])
    low = here("low", [P, 3])
    den = here("den", [P, 3])
    weights4 = here("weights4", [P, 4])
    sc4 = here("sc4", [P, SEQ])
    assert nxt <= nc.sbuf_usable_end, nxt
    scores = [acc[:, SEQ * j:SEQ * j + SEQ] for j in range(3)]
    probsT = [acc[:, 3 * SEQ:4 * SEQ], sc4[:]]
    before_turn = {n: acc[:, SEQ * j:SEQ * j + SEQ] for j, n in enumerate(("slc", "win", "gates"))}
    row3, z = place("row3", [P, DM], F32, arena + 4 * TT * DM)
    rms_t, z = place("rms_t", [P, DM], F32, z)
    rms_t3, _ = place("rms_t3", [P, DM], F32, z)
    row4, z = place("row4", [P, DM], F32, act_at)
    rms_t2, z = place("rms_t2", [P, DM], F32, z)
    rms_t4, _ = place("rms_t4", [P, DM], F32, z)
    squares, z = place("squares", [P, 2 * TT], F32, byte["small"])
    x_sums, _ = place("x_sums", [P, TT], F32, z)
    scratch = nc.dram_tensor("bias_rows", (N_HEADS, P, GRID), F32, kind="Internal").ap()

    banks = [ctx.enter_context(nc.psum_tensor(f"bank{i}", [P, 512], F32)) for i in range(8)]

    filled = [sem(f"filled{i}") for i in range(8)]
    drained = {"dve": [sem(f"dve_drained{i}") for i in range(8)],
               "act": [sem(f"act_drained{i}") for i in range(8)]}
    raw_landed = [sem(f"raw_landed{i}") for i in range(RAW)]
    hi_ready, lo_ready, unit_used, ada_used = sem("hi_ready"), sem("lo_ready"), sem("unit_used"), sem("ada_used")
    act_step, dve_step, pool_step = sem("act_step"), sem("dve_step"), sem("pool_step")
    load = {n: sem(f"load_{n}") for n in ("x", "params", "consts", "masks", "gmlp", "rows0", "rows1", "rows2",
                                          "bias", "out", "tabs", "w1", "strip0", "strip", "rows3", "rows4")}
    S = {n: sem(n) for n in (
        "silu_c", "ada_used_pe", "ada_scaled", "xn_ready", "affine1", "h_lo", "shift_ready", "lora_ready",
        "kk_sq", "cs_ready", "exp_ready", "root_ready", "inverse_ready", "norm_root", "norm_inverse",
        "prep_ready", "bars_ready", "wst_ready", "pv_ready", "pv_std", "pv_root", "r0_ready", "w_ready",
        "sets_ready", "state_zero", "y_sq", "yb_ready", "y_hi", "y_lo", "y_lo_last", "var1", "root1",
        "hid_hi_ready", "hid_ready", "x_ready", "x_ready_last", "x_ready2", "offset_ready", "normal_ready",
        "xn3_ready", "xn3_first", "blk_ready", "low_ready", "exp_done", "upper_free", "y2_hi", "y2_lo",
        "squares_ready", "rms_ready", "rms_root", "x_rms_ready", "x_rms_root", "x_inverse", "gelu2",
        "prod2", "hid2_hi", "hid2_lo", "out_ready", "keys_part", "weight_ready")}

    def job(name):
        return bank_of[name]

    def bank(name):
        return banks[job(name)[0]]

    def claim(pe, name):
        b, _, before, _, _ = job(name)
        for e in ("dve", "act"):
            if before[e]:
                pe.wait_ge(drained[e][b], before[e])

    def full_sem(name):
        b, n, _, _, by_unit = job(name)
        return (unit_used if by_unit else filled[b]), n

    def await_full(eng, name):
        eng.wait_ge(*full_sem(name))

    def await_drained(eng, name, by):
        b, _, _, after, _ = job(name)
        eng.wait_ge(drained[by][b], after[by])

    def drained_at(name, by):
        b, _, _, after, _ = job(name)
        return drained[by][b], after[by]

    def drain(name, by):
        return drained[by][job(name)[0]]

    def raw_ready(eng, n):
        eng.wait_ge(raw_landed[n % RAW], 16 * (n // RAW + 1))

    def col(name, j=0):
        return pc[:, COLS[name] + j:COLS[name] + j + 1]

    def ada_unit(i):
        return f"ada{1 + (i - 1) // KC}_{(i - 1) % KC}"

    def tok(t):
        return slice(t * P, (t + 1) * P)

    def const(name):
        at, n = CONSTS[name]
        return src["consts"][:, at:at + n]

    row2_a, a2 = place("row2_a", [P, DM], F32, act_at)
    row2_b, a2 = place("row2_b", [P, DM], F32, a2)
    mixed2, a2 = place("mixed2", [P, DM], F32, a2)
    mixed, _ = place("mixed", [P, DM], F32, arena)

    def second_act(act, a, convert, affine_hi, square_x, root_x, scaled_x):
        act.dma_start(relb[0:N_BUCKETS, :], src["rel_bias_t"]).then_inc(load["tabs"], 16)
        act.dma_start(onehot[0:N_BUCKETS, :], const("onehot")[0:N_BUCKETS]).then_inc(load["tabs"], 16)
        act.dma_start(future[:], const("future")).then_inc(load["tabs"], 16)
        act.dma_start(w2k[:], src["w2k"]).then_inc(load["tabs"], 16)
        act.dma_start(w2v[:], src["w2v"]).then_inc(load["tabs"], 16)
        affine_hi("h3", "nmp")
        act.dma_start(w1[:], src["w1"][0]).then_inc(load["w1"], 16)
        def bias_rows():
            for j, n in enumerate((SEQ, GRID - SEQ)):
                await_full(act, ("bias", j))
                a.done(act.activation(grow[:, SEQ * j:SEQ * j + n], bank(("bias", j))[0:N_HEADS, 0:n], ACT.Copy, scale=-1.0),
                       drain(("bias", j), "act"))
            a.settle()
            act.wait_ge(drained["act"][job(("bias", 0))[0]], job(("bias", 0))[3]["act"])
            act.dma_start(scratch, grow[:].unsqueeze(1).to_broadcast([N_HEADS, P, GRID])).then_inc(load["strip0"], 16)

        def bias_strips():
            act.wait_ge(load["strip0"], 16)
            act.dma_start(strip[:], bass.AP(scratch.tensor, P - 1, [[GRID - 1, P], [P * GRID, N_HEADS], [1, SEQ]])).then_inc(load["strip"], 16)

        def turned(name, values):
            await_full(act, ("turn_v", name))
            a.done(act.activation(values[:].rearrange("p t d -> p (t d)"), bank(("turn_v", name))[:], ACT.Copy),
                   drain(("turn_v", name), "act"))

        def compress(kv):
            j = "kv".index(kv)
            await_full(act, ("hidden", kv))
            a.done(act.activation(hc[:].rearrange("p a b -> p (a b)"), bank(("hidden", kv))[:, 0:4 * N_CMP], ACT.Gelu_apprx_tanh),
                   drain(("hidden", kv), "act"))
            if kv == "k":
                act.dma_start(w1[:], src["w1"][1]).then_inc(load["w1"], 16)
            await_full(act, ("compressed", kv))
            b = bank(("compressed", kv))
            if kv == "k":
                a.done(act.activation(kc2[:].rearrange("p a b -> p (a b)"), b[:, 0:2 * N_CMP], ACT.Copy), drain(("compressed", kv), "act"))
            else:
                a.done(act.activation(vc[0:N_CMP].rearrange("p a b -> p (a b)"), b[0:N_CMP, 0:2 * HD], ACT.Copy),
                       drain(("compressed", kv), "act"))

        for name in FIRST_UNITS:
            if name != FIRST_UNITS[0]:
                convert()
            b0 = bank((name, 0))
            if name in ("cmp", "q0", "q1"):
                for j in range(2):
                    await_full(act, (name, j))
                    if name == "cmp":
                        ins = act.activation(kvc[:, j, :], bank((name, j))[:], ACT.Copy)
                    else:
                        ins = act.activation(qT[:, 2 * int(name[1]) + j, :], bank((name, j))[:], ACT.Copy, scale=-(HD ** -0.5))
                    a.done(ins, drain((name, j), "act"))
            elif name in ("slc", "win"):
                keys = ksl if name == "slc" else kwn
                await_full(act, (name, 0))
                for g in range(N_KV):
                    for half in range(2):
                        ins = act.activation(keys[HD * half:HD * half + HD, g, :], b0[HD * g:HD * g + HD, :], ACT.Copy)
                        a.done(ins, drain((name, 0), "act") if g == half == 1 else S["keys_part"])
                await_full(act, (name, 1))
                a.done(act.activation(before_turn[name], bank((name, 1))[:], ACT.Copy), drain((name, 1), "act"))
            else:
                await_full(act, (name, 0))
                a.done(act.activation(before_turn[name][0:24], b0[0:24, :], ACT.Sigmoid), drain((name, 0), "act"))
            if name == "cmp":
                bias_rows()
            elif name == "q1":
                bias_strips()
            if name == "win":
                turned("slc", vsl)
            if name in ("q1", "win"):
                compress("k" if name == "q1" else "v")
        turned("win", vwn)
        await_full(act, ("turn_v", "gates"))
        a.done(act.activation(gate[:].rearrange("p t g -> p (t g)"), bank(("turn_v", "gates"))[:, 0:24 * TT], ACT.Copy),
               drain(("turn_v", "gates"), "act"))

        for n, name in enumerate(SLOT_UNITS):
            convert()
            for slot in slots_of(n):
                if 0 <= slot - 2 < len(ITEMS):
                    item = slot - 2
                    w = n_keys(item)
                    await_full(act, ("turn2", item))
                    if item >= 2:
                        await_full(act, ("values", item - 2))
                    b = bank(("turn2", item))
                    if w < P:
                        ins = act.activation(probsT[item % 2][0:w, 0:P], b[0:w, 0:P], ACT.Copy)
                    else:
                        ins = act.activation(probsT[item % 2][:, 0:w], b[:, 0:w], ACT.Copy)
                    a.done(ins, drain(("turn2", item), "act"))
                if 0 <= slot < len(ITEMS):
                    x, w = slot % 3, n_keys(slot)
                    act.wait_ge(S["low_ready"], slot + 1)
                    a.step(act.activation(scores[x][:, 0:w], scores[x][:, 0:w], ACT.Exp, bias=low[:, x:x + 1], scale=-1.0,
                                          accum_out=den[:, x:x + 1]), S["exp_done"])
            if name[:2] == "cg":
                for j in range(2):
                    await_full(act, (name, j))
                    a.done(act.activation(cgT[:, 2 * int(name[2]) + j, :], bank((name, j))[:], ACT.Copy), drain((name, j), "act"))

        act.wait_ge(S["upper_free"], 1)
        for k in range(4):
            await_drained(act, (f"bg{k // 2}", k % 2), "dve")
            a.done(act.activation(act_hi[:, 4 + k, :], bgT[:, k, :], ACT.Copy), S["y2_hi"])
        for k in range(PAIRS):
            await_full(act, ("turn_o", k))
            a.done(act.activation(act_hi[:, k, :], bank(("turn_o", k))[:], ACT.Copy), drain(("turn_o", k), "act"))
        act.dma_start(row3[:], src["mix_post"].partition_broadcast(P)).then_inc(load["rows3"], 16)

        def squares_of_rows(stage, e, t, temp):
            if t < TT:
                for j in range(2):
                    await_full(act, (stage, t, j))
                    a.step(act.activation(temp[:, 0:SEQ], bank((stage, t, j))[:], ACT.Square,
                                          accum_out=squares[:, 2 * t + j:2 * t + j + 1]), drain((stage, t, j), "act"))
            if t > 0 and t <= TT:
                act.wait_ge(S["rms_ready"], TT * e + t)
                a.done(act.activation(rstd[:, t - 1:t], rstd[:, t - 1:t], ACT.Sqrt), S["rms_root"])

        for n in range(3):
            convert()
        for s in range(TT + 4):
            squares_of_rows("mix2", 0, s, rms_t)
            if 0 <= s - 2 < TT:
                square_x(1, s - 2)
            if 0 <= s - 3 < TT:
                root_x(1, s - 3)
            if 0 <= s - 4 < TT:
                scaled_x(1, s - 4)
            if s in (1, TT):
                convert()
        affine_hi("h4", "nfp")

        for m in range(FT):
            if m:
                convert()
            name = f"up2_{m}"
            pair = [acc[:, SEQ * (2 * (m % 2) + j):SEQ * (2 * (m % 2) + j) + SEQ] for j in range(2)]
            for j in range(2):
                await_full(act, (name, j))
                a.done(act.activation(pair[j], bank((name, j))[:], ACT.Copy, scale=col("cffn", 2 * 2 * FT + FT * j + m)),
                       drain((name, j), "act"))
            await_drained(act, (name, 0), "dve")
            a.done(act.activation(pair[0], pair[0], ACT.Gelu_apprx_tanh), S["gelu2"])
            act.wait_ge(S["prod2"], m + 1)
            a.done(act.activation(hid_hi[:, m, :], pair[1], ACT.Copy), S["hid2_hi"])
        for n in range(FT // 2):
            convert()
            if n == 0:
                await_full(act, (f"up2_{FT - 1}", 1))
                act.dma_start(row4[:], src["ffn_post"].partition_broadcast(P)).then_inc(load["rows4"], 16)
        for s in range(TT + 1):
            squares_of_rows("ff2", 1, s, rms_t2)

    def second_dve(dve, d, ts, tt, stt, affine_lo, x_mean_square, inverse_x):
        V = dve

        temp4 = acc[:].rearrange("p (a n) -> p a n", a=4)
        affine_lo("h3", "nmp", temp4)

        def windows(kv):
            j = "kv".index(kv)
            pe_at = COLS["pe_" + kv]
            if j:
                await_full(dve, ("hidden", "k"))
            for g in range(N_KV):
                rows = slice(HD * g, HD * g + HD)
                x = kvc[rows, j, :].rearrange("p (m l o) -> p o l m", l=8, o=2)
                for odd in range(2):
                    for half in range(2):
                        pe_c = pc[rows, pe_at + 16 * half + odd:pe_at + 16 * half + 16:2]
                        tt(blk[HD * odd:HD * odd + HD, 8 * half:8 * half + 8, N_CMP * g:N_CMP * g + N_CMP],
                           x[:, odd, :, half:half + N_CMP], pe_c.unsqueeze(2).to_broadcast([HD, 8, N_CMP]), ALU.add,
                           sem=S["blk_ready"])

        await_drained(dve, ("cmp", 1), "act")
        windows("k")
        windows("v")
        dve.wait_ge(load["strip"], 16)
        dve.wait_ge(load["tabs"], 80)
        tt(strip[:], strip[:], future[:].unsqueeze(1).to_broadcast([P, N_HEADS, SEQ]), ALU.add)
        await_drained(dve, ("turn_v", "gates"), "act")
        for h in range(N_HEADS):
            ts(gate[:, 0, 3 * h:3 * h + 1], gate[:, 0, 3 * h:3 * h + 1], col("has_key"))

        def lo_of_convolution(k):
            dve.wait_ge(S["y2_hi"], k + 1)
            tt(act_lo[:, 4 + k, :], bgT[:, k, :], act_hi[:, 4 + k, :].bitcast(F32), ALU.subtract, sem=S["y2_lo"])

        def convolve(k, tap):
            if tap == 0:
                ts(bgT[:, k, :], cgT[:, k, :], col("cmix", 8 + k))
            else:
                stt(bgT[:, k, tap:], cgT[:, k, 0:SEQ - tap], col("cmix", 8 - 4 * tap + k), bgT[:, k, tap:], ALU.mult, ALU.add)

        for n, name in enumerate(SLOT_UNITS):
            for slot in slots_of(n):
                step = 2 * (slot - slots_of(n)[0])
                if name in ("xt1", "bg0") and step % 4 == 0 and step < 24:
                    convolve((0 if name == "xt1" else 2) + step // 12, step // 4 % 3)
                if 0 <= slot < len(ITEMS):
                    br, h, i = ITEMS[slot]
                    x, w = slot % 3, n_keys(slot)
                    at = 384 - P * i
                    bias = strip[:, h, at:at + w] if br != "cmp" else strip[:, h, at + L_CMP - 1:SEQ:S_CMP]
                    await_full(dve, ("scores", slot))
                    if slot >= 3:
                        await_full(dve, ("turn2", slot - 3))
                    d.step(V.tensor_tensor_reduce(out=scores[x][:, 0:w], in0=bank(("scores", slot))[:, 0:w], in1=bias,
                                                  scale=1.0, scalar=3e38, op0=ALU.add, op1=ALU.min,
                                                  accum_out=low[:, x:x + 1]), drain(("scores", slot), "dve"))
                    d.step(V.tensor_copy(low[:, x:x + 1], low[:, x:x + 1]), S["low_ready"])
                if 0 <= slot - 3 < len(ITEMS):
                    item = slot - 3
                    br, h, i = ITEMS[item]
                    part = ("cmp", "slc", "win").index(br)
                    oh = o[:, i, HD * h:HD * h + HD]
                    b = bank(("values", item))[:, 0:HD]
                    await_full(dve, ("values", item))
                    if br == "slc":
                        ts(oh, b, weights4[:, item % 4:item % 4 + 1], sem=drain(("values", item), "dve"))
                    else:
                        stt(oh, b, weights4[:, item % 4:item % 4 + 1], oh, ALU.mult, ALU.add, sem=drain(("values", item), "dve"))
                if 0 <= slot - 1 < len(ITEMS):
                    item = slot - 1
                    br, h, i = ITEMS[item]
                    part = ("cmp", "slc", "win").index(br)
                    dve.wait_ge(S["exp_done"], item + 1)
                    d.step(V.reciprocal(weights4[:, item % 4:item % 4 + 1], den[:, item % 3:item % 3 + 1]))
                    ts(weights4[:, item % 4:item % 4 + 1], weights4[:, item % 4:item % 4 + 1],
                       gate[:, i, 3 * h + part:3 * h + part + 1], sem=S["weight_ready"])
            if name[:2] == "xt":
                for j in range(2):
                    k = 2 * int(name[2]) + j
                    await_full(dve, (name, j))
                    tt(cgT[:, k, :], bank((name, j))[:], cgT[:, k, :], ALU.mult, sem=drain((name, j), "dve"))
            elif name[:2] == "bg":
                if name == "bg1":
                    for k in range(2):
                        lo_of_convolution(k)
                for j in range(2):
                    k = 2 * int(name[2]) + j
                    await_full(dve, (name, j))
                    tt(bgT[:, k, :], bank((name, j))[:], bgT[:, k, :], ALU.mult, sem=drain((name, j), "dve"))
        for k in (2, 3):
            lo_of_convolution(k)
        for k in range(PAIRS):
            await_full(dve, ("turn_o", k))
            await_drained(dve, ("turn_o", k), "act")
            tt(act_lo[:, k, :], bank(("turn_o", k))[:], act_hi[:, k, :].bitcast(F32), ALU.subtract, sem=drain(("turn_o", k), "dve"))

        def mean_square(stage, t):
            for j in range(2):
                await_drained(dve, (stage, t, j), "act")
            tt(rstd[:, t:t + 1], squares[:, 2 * t:2 * t + 1], squares[:, 2 * t + 1:2 * t + 2], ALU.add)
            ts(rstd[:, t:t + 1], rstd[:, t:t + 1], 1.0 / DM, RMS_EPS, ALU.mult, ALU.add, sem=S["rms_ready"])

        def add_rms(stage, e, t, row, temp, sem):
            dve.wait_ge(S["rms_root"], TT * e + t + 1)
            d.step(V.reciprocal(rstd[:, t:t + 1], rstd[:, t:t + 1]))
            for j in range(2):
                h = slice(SEQ * j, SEQ * j + SEQ)
                stt(temp[:, h], bank((stage, t, j))[:], rstd[:, t:t + 1], row[:, h], ALU.mult, ALU.mult,
                    sem=drain((stage, t, j), "dve"))
            tt(xres[:, t, :], xres[:, t, :], temp[:], ALU.add, sem)

        dve.wait_ge(load["rows3"], 16)
        for s in range(TT + 4):
            if s < TT:
                mean_square("mix2", s)
            if 0 <= s - 1 < TT:
                add_rms("mix2", 0, s - 1, row3, rms_t3, S["x_ready2"])
            if 0 <= s - 2 < TT:
                x_mean_square(1, s - 2)
            if 0 <= s - 3 < TT:
                inverse_x(1, s - 3)
        affine_lo("h4", "nfp", temp4)
        for m in range(FT):
            name = f"up2_{m}"
            pair = [acc[:, SEQ * (2 * (m % 2) + j):SEQ * (2 * (m % 2) + j) + SEQ] for j in range(2)]
            for j in range(2):
                await_full(dve, (name, j))
                await_drained(dve, (name, j), "act")
                c = FT * j + m
                stt(pair[j][:, 1:], bank((name, j))[:, 0:SEQ - 1], col("cffn", 2 * FT + c), pair[j][:, 1:], ALU.mult, ALU.add)
                stt(pair[j][:, 2:], bank((name, j))[:, 0:SEQ - 2], col("cffn", c), pair[j][:, 2:], ALU.mult, ALU.add,
                    sem=drain((name, j), "dve"))
            dve.wait_ge(S["gelu2"], m + 1)
            tt(pair[1], pair[1], pair[0], ALU.mult, sem=S["prod2"])
            dve.wait_ge(S["hid2_hi"], m + 1)
            tt(hid_lo[:, m, :], pair[1], hid_hi[:, m, :].bitcast(F32), ALU.subtract, sem=S["hid2_lo"])
        dve.wait_ge(load["rows4"], 16)
        for s in range(TT + 1):
            if s < TT:
                mean_square("ff2", s)
            if s:
                add_rms("ff2", 1, s - 1, row4, rms_t4, S["out_ready"])

    def second_pe(pe, three, next_unit, dense_feature, dense_rows, turn_x, fill):
        turn_x("h3", (S["xn3_first"], 0), xn2, tiles=TILE_ORDER[0])
        def bias_rows():
            pe.wait_ge(load["tabs"], 80)
            for j, n in enumerate((SEQ, GRID - SEQ)):
                claim(pe, ("bias", j))
                fill(("bias", j), pe.matmul(bank(("bias", j))[0:N_HEADS, 0:n], relb[0:N_BUCKETS, :],
                                            onehot[0:N_BUCKETS, SEQ * j:SEQ * j + n], start=True, stop=True))

        def compress(kv):
            j = "kv".index(kv)
            pe.wait_ge(load["w1"], 16 * (j + 1))
            pe.wait_ge(S["blk_ready"], 8 * (j + 1))
            claim(pe, ("hidden", kv))
            b = bank(("hidden", kv))
            for half in range(2):
                for l in range(L_CMP // 2):
                    mm = pe.matmul(b[:, 2 * N_CMP * half:2 * N_CMP * half + 2 * N_CMP], w1[:, l, P * half:P * half + P],
                                   blk[:, l, :], start=l == 0, stop=l == L_CMP // 2 - 1)
            fill(("hidden", kv), mm)
            claim(pe, ("compressed", kv))
            await_drained(pe, ("hidden", kv), "act")
            b = bank(("compressed", kv))
            for g in range(1 if kv == "k" else N_KV):
                for half in range(2):
                    if kv == "k":
                        mm = pe.matmul(b[:, 0:2 * N_CMP], w2k[:, half, :], hc[:, half, :], start=half == 0, stop=half == 1)
                    else:
                        mm = pe.matmul(b[0:N_CMP, HD * g:HD * g + HD], hc[:, half, N_CMP * g:N_CMP * g + N_CMP],
                                       w2v[:, half, :], start=half == 0, stop=half == 1)
            fill(("compressed", kv), mm)

        def gates_features():
            (hi, lo), w = next_unit("gates")
            claim(pe, ("gates", 0))
            for k in range(KC):
                mm = three(bank(("gates", 0))[0:24, :], (hi[:, k, :], lo[:, k, :]), (act_hi[:, k, :], act_lo[:, k, :]),
                           k == 0, k == KC - 1)
            mm.then_inc(full_sem(("gates", 0))[0], 1)

        def turn_v(name):
            last = 1 if name != "gates" else 0
            await_drained(pe, (name, last), "act")
            claim(pe, ("turn_v", name))
            n = 24 if name == "gates" else P
            for t in range(TT):
                mm = pe.transpose(bank(("turn_v", name))[:, n * t:n * t + n], before_turn[name][0:n, tok(t)], ident[0:n, 0:n])
            fill(("turn_v", name), mm)

        for name in FIRST_UNITS:
            if name in ("slc", "win"):
                dense_feature(name, 2)
            elif name == "gates":
                gates_features()
            else:
                dense_feature(name, 2, stage="h3" if name == FIRST_UNITS[0] else None)
            if name == "cmp":
                bias_rows()
            if name == "win":
                turn_v("slc")
            if name in ("q1", "win"):
                compress("k" if name == "q1" else "v")
        turn_v("win")
        turn_v("gates")

        def attention(slot):
            for st, item in stages_of(slot):
                br, h, i = ITEMS[item]
                g, rows, w = h // REP, slice(HD * (h % 2), HD * (h % 2) + HD), n_keys(item)
                b = bank((st, item))
                claim(pe, (st, item))
                if st == "scores":
                    keys = kc2[rows, g, 0:w] if br == "cmp" else (ksl if br == "slc" else kwn)[rows, g, 0:w]
                    mm = pe.matmul(b[:, 0:w], qT[rows, h // 2, tok(i)], keys, start=True, stop=True)
                elif st == "turn2":
                    pe.wait_ge(S["exp_done"], item + 1)
                    x = scores[item % 3]
                    for j in range(-(-w // P)):
                        n = min(P, w - P * j)
                        mm = pe.transpose(b[0:n, tok(j)], x[:, P * j:P * j + n], ident[:])
                else:
                    await_drained(pe, ("turn2", item), "act")
                    for j in range(-(-w // P)):
                        n = min(P, w - P * j)
                        values = vc[0:n, g, :] if br == "cmp" else (vsl if br == "slc" else vwn)[:, j, HD * g:HD * g + HD]
                        mm = pe.matmul(b[:, 0:HD], probsT[item % 2][0:n, tok(j)], values, start=j == 0, stop=j == -(-w // P) - 1)
                fill((st, item), mm)

        await_drained(pe, ("win", 0), "act")
        for name in ("win", "gates"):
            await_drained(pe, ("turn_v", name), "act")
        for n, name in enumerate(SLOT_UNITS):
            slots = list(slots_of(n))
            steps = 2 * KC
            dense_feature(name, 2, lambda k: [attention(s) for s in slots[k * len(slots) // steps:(k + 1) * len(slots) // steps]],
                          upper_first=name == "bg1")
        for k in range(PAIRS):
            claim(pe, ("turn_o", k))
            await_drained(pe, ("values", len(ITEMS) - 1), "dve")
            for t in range(TT):
                mm = pe.transpose(bank(("turn_o", k))[:, tok(t)], o[:, t, P * k:P * k + P], ident[:])
            fill(("turn_o", k), mm)
        dense_rows("mix2", "out2", 4, (act_hi, act_lo),
                   ready={0: (S["y2_lo"], 2), 1: (S["y2_lo"], 4), 2: drained_at(("turn_o", 1), "dve"),
                          3: drained_at(("turn_o", 3), "dve")}, turned=True)
        turn_x("h4", (S["xn3_ready"], 0), xn2)
        for m in range(FT):
            dense_feature(f"up2_{m}", 2, stage=None if m else "h4")
        dense_rows("ff2", "down2", FT // 2, (hid_hi, hid_lo),
                   ready={n: (S["hid2_lo"], 2 * n + 2) for n in range(FT // 2)})

    block = ctx.enter_context(nc.Block())
    W_IN1 = ("lora0", "lora1", "k0", "k1", "r0", "r1", "v0", "v1", "pv0", "pv1", "pu0", "pu1")

    def finish(sp):
        for t in range(TT):
            sp.wait_ge(S["out_ready"], t + 1)
            sp.dma_start(out[0, tok(t), :], xres[:, t, :]).then_inc(load["out"], 16)
        sp.wait_ge(load["out"], 16 * TT)

    @block.sync
    def _(sp):
        sp.dma_start(pc[:], src["params"]).then_inc(load["params"], 16)
        at, n = CONSTS["ident"]
        sp.dma_start(ident[:], const("ident")).then_inc(load["consts"], 16)
        sp.dma_start(bd64[:], const("bd64")).then_inc(load["consts"], 16)
        for n in range(len(UNITS)):
            if n >= RAW:
                m = n - RAW
                if m in SPLIT_AT:
                    sp.wait_ge(lo_ready, SPLIT_AT[m] + 1)
                else:
                    at = m - sum(1 for i in SPLIT_UNITS if i < m)
                    by_pe = sum(1 for i in ADA_PE if i <= at)
                    if at in ADA_PE:
                        sp.wait_ge(S["ada_used_pe"], by_pe)
                    else:
                        sp.wait_ge(ada_used, at + 1 - by_pe)
            if n == RAW:
                sp.dma_start(xres[:], src["x"].rearrange("b (t p) d -> p (b t) d", p=P)).then_inc(load["x"], 16)
            sp.dma_start(raw[n % RAW][:, :UNIT_SIZE[n]],
                         src["weights"][:, UNIT_START[n]:UNIT_START[n + 1]]).then_inc(raw_landed[n % RAW], 16)
        finish(sp)

    def prep_side(o, p, part):
        pr = pairs[p % 2]
        sig, cs, aa, kk, ep, sq, ar, bt, kt = (pr[n][:] for n in ("sig", "cs", "aa", "kk", "ep", "sq", "ar", "bt", "kt"))
        chunks = lambda x: x.rearrange("p (c t) -> p c t", t=CH)
        ends = pend[p][:].unsqueeze(2).to_broadcast([P, SEQ // CH, CH])

        def times(out, a, b, sem=None):
            o.step(o.eng.tensor_tensor(out, a, b, ALU.mult), sem)

        if part == 4:
            o.eng.wait_ge(S["exp_ready"], 3 * p + 1)
            o.step(o.eng.tensor_copy(pend[p][:], ep[:, CH - 1:SEQ:CH]))
            times(ar[:, 1, :], rT[:, p, :], ep)
            await_drained(o.eng, ("a", p), "act")
            o.step(o.eng.tensor_scalar(ep, aa, col("k_a", p), oka[:, p:p + 1], ALU.mult, ALU.add))
        elif part == 5:
            o.step(o.eng.tensor_scalar(kk, kT[:, p, :], col("k_k", p), None, ALU.mult))
            times(sq, kk, kk, S["kk_sq"])
        elif part == 12:
            times(kT[:, p, :], kT[:, p, :], ep)
            o.eng.wait_ge(S["exp_ready"], 3 * p + 3)
            times(kt, kT[:, p, :], cs)
            o.step(o.eng.tensor_scalar(rT[:, p, :], rT[:, p, :], col("r_k", p), None, ALU.mult))
            times(rT[:, p, :], rT[:, p, :], kT[:, p, :], S["prep_ready"])
            o.eng.wait_ge(S["inverse_ready"], p + 1)
            times(kk, kk, sq)
            times(aa, kk, aa)
            times(bt, aa, cs)
            times(chunks(cs), chunks(kt), ends)
            times(ar[:, 0, :], kk, sig)
            o.step(o.eng.tensor_scalar(ar[:, 0, :], ar[:, 0, :], -1.0, None, ALU.mult))
            times(chunks(sig), chunks(bt), ends, S["bars_ready"])

    def norm_side(o, p, part):
        kk, sq = (norm_buffers[p][n][:] for n in ("kk", "sq"))
        if part == 6:
            o.eng.wait_ge(S["norm_inverse"], p + 1)
            o.step(o.eng.tensor_tensor(kk, kk, sq, ALU.mult))
            o.step(o.eng.tensor_scalar(kk, kk, col("lnx_g", p), col("lnx_b", p), ALU.mult, ALU.add))
            await_drained(o.eng, ("bonus", p), "dve")
            o.step(o.eng.tensor_tensor(kk, kk, rT[:, p, :], ALU.add))
            await_drained(o.eng, ("g", p), "act")
            o.step(o.eng.tensor_tensor(vT[:, p, :], kk, kT[:, p, :], ALU.mult), S["yb_ready"])

    @block.gpsimd
    def _(pool):
        o = Order(pool, pool_step)

        def split(units):
            for n in units:
                i, size = SPLIT_AT[n], UNIT_SIZE[n]
                pool.wait_ge(hi_ready, i + 1)
                pool.tensor_tensor(wlo[i % SPLIT][:, :size], raw[n % RAW][:, :size], whi[i % SPLIT][:, :size],
                                   ALU.subtract).then_inc(lo_ready, 1)

        def ada(i):
            r = raw[UNIT_AT[ada_unit(i)] % RAW][:]
            pool.wait_ge(S["ada_scaled"], i)
            if i == 1:
                await_full(pool, "cols0")
            elif i == KC + 1:
                await_full(pool, ("cols1", 3))
            if (i - 1) % KC == 0:
                o.done(pool.tensor_copy(acc[:], r), ada_used)
            else:
                o.done(pool.tensor_tensor(acc[:], acc[:], r, ALU.add), ada_used)
            pool.wait_ge(ada_used, KC - len(ADA_PE) + i)

        split(SPLIT_UNITS[:len(W_IN1)])
        for kind, *args in CHUNK_SCHEDULE:
            if kind == "ada":
                ada(*args)
            elif kind == "prep":
                prep_side(o, *args)
            elif kind == "norm" and args[0] < PAIRS - 1:
                norm_side(o, *args)
            elif kind == "mixer" and args[0] < 2:
                part, at, n = ((uT, 0, 4), (vT, 4, PAIRS - 1))[args[0]]
                pool.wait_ge(S["y_hi"], args[0] + 1)
                o.step(pool.tensor_tensor(act_lo[:, at:at + n, :], part[:, 0:n, :], act_hi[:, at:at + n, :].bitcast(F32),
                                          ALU.subtract), S["y_lo"])
                if args[0] == 0:
                    split(SPLIT_UNITS[len(W_IN1):len(W_IN1) + 1])
        second = SPLIT_AT[UNIT_AT["cmp"]]
        split(SPLIT_UNITS[len(W_IN1) + 1:second])
        for t in range(TT - 1):
            pool.wait_ge(load["rows2"], 32)
            pool.wait_ge(S["normal_ready"], t + 1)
            o.step(pool.tensor_tensor(xres[:, t, :], xres[:, t, :], row2_a[:], ALU.mult))
            o.step(pool.tensor_tensor(xres[:, t, :], xres[:, t, :], row2_b[:], ALU.add), S["x_ready"])
        split(SPLIT_UNITS[second:])

    @block.scalar
    def _(act):
        a = Order(act, act_step)
        at = [0]

        def convert():
            i = at[0]
            at[0] += 1
            if i == len(SPLIT_UNITS):
                return
            n = SPLIT_UNITS[i]
            raw_ready(act, n)
            if i >= SPLIT:
                act.wait_ge(unit_used, i - SPLIT + 1)
            a.done(act.activation(whi[i % SPLIT][:, :UNIT_SIZE[n]], raw[n % RAW][:, :UNIT_SIZE[n]], ACT.Copy),
                   hi_ready)

        act.wait_ge(load["params"], 16)
        a.done(act.activation(pc[:, COLS["c"]:COLS["c"] + KC], pc[:, COLS["c"]:COLS["c"] + KC], ACT.Silu), S["silu_c"])
        act.wait_ge(S["var1"], 1)
        a.done(act.activation(rstd[:], rstd[:], ACT.Sqrt), S["root1"])

        def normalise(n, t, sem):
            act.wait_ge(S["offset_ready"], TT * n + t + 1)
            a.done(act.activation(xres[:, t, :], xres[:, t, :], ACT.Identity, bias=mv[:, t, 0:1], scale=rstd[:, t:t + 1]), sem)

        for t in range(TT):
            normalise(0, t, S["xn_ready"])

        def affine_hi(stage, part):
            if isinstance(part, str):
                for k in range(KC):
                    await_full(act, (stage, k))
                    a.done(act.activation(act_hi[:, k, :], bank((stage, k))[:], ACT.Copy, scale=col(part, k)),
                           drain((stage, k), "act"))
                return
            act.wait_ge(S["affine1"], part // 2 + 1)
            for k in range(KC):
                await_full(act, (stage, k))
                a.done(act.activation(act_hi[:, k, :], bank((stage, k))[:], ACT.Identity,
                                      bias=affine[:, part + 1, k:k + 1], scale=affine[:, part, k:k + 1]),
                       drain((stage, k), "act"))

        convert()
        affine_hi("h1", 0)

        act.dma_start(up[:], const("up")).then_inc(load["gmlp"], 16)
        act.dma_start(wsT[:], src["w_s_t"]).then_inc(load["gmlp"], 16)
        act.dma_start(bs[:], src["b_s"].partition_broadcast(P)).then_inc(load["gmlp"], 16)
        act.dma_start(sg_g[:], src["sg_ln_g"].partition_broadcast(P)).then_inc(load["gmlp"], 16)
        act.dma_start(sg_b[:], src["sg_ln_b"].partition_broadcast(P)).then_inc(load["gmlp"], 16)
        act.dma_start(row_a[:], src["emb_ln_g"].partition_broadcast(P)).then_inc(load["rows0"], 16)
        act.dma_start(row_b[:], src["emb_ln_b"].partition_broadcast(P)).then_inc(load["rows0"], 16)
        act.dma_start(wup[:], src["lora_up"]).then_inc(load["masks"], 16)
        act.dma_start(gup[:], src["g_up_pad"]).then_inc(load["masks"], 16)
        act.dma_start(masks[:, 0:2, :], const("mask_qr").rearrange("p (a b) -> p a b", a=2)).then_inc(load["masks"], 16)
        act.dma_start(masks[:, 2:4, :], const("mask_mk").rearrange("p (a b) -> p a b", a=2)).then_inc(load["masks"], 16)
        act.dma_start(mask_d[:], const("mask_d")).then_inc(load["masks"], 16)
        act.dma_start(mask_e[:], const("mask_e")).then_inc(load["masks"], 16)
        act.dma_start(chunk_rows[:], const("chunk_rows")).then_inc(load["masks"], 16)
        act.dma_start(bias4[:], src["b_gates"]).then_inc(load["bias"], 16)

        def unshifted(name, j, dest, mu):
            await_full(act, (name, j))
            a.done(act.activation(dest, bank((name, j))[:], ACT.Copy, scale=omu[:, mu:mu + 1]), drain((name, j), "act"))

        def prep_act(p, part):
            pr = pairs[p % 2]
            if part == 0:
                for job_name, dest, bias in (("z", pr["sig"], "w0"), ("a", pr["aa"], "a0")):
                    await_full(act, (job_name, p))
                    a.done(act.activation(dest[:], bank((job_name, p))[:], ACT.Sigmoid, bias=col(bias, p)),
                           drain((job_name, p), "act"))
            elif part == 2:
                act.wait_ge(S["cs_ready"], p + 1)
                a.done(act.activation(pr["ep"][:], pr["cs"][:], ACT.Exp, scale=-DECAY), S["exp_ready"])
            elif part == 3:
                a.step(act.activation(pr["sig"][:], pr["sig"][:], ACT.Exp, scale=-DECAY), S["exp_ready"])
            elif part == 4:
                a.done(act.activation(pr["cs"][:], pr["cs"][:], ACT.Exp, scale=DECAY), S["exp_ready"])
            elif part == 7:
                await_drained(act, ("kk", p), "dve")
                a.done(act.activation(pr["sq"][:], pr["sq"][:], ACT.Sqrt), S["root_ready"])
            elif part == 13:
                await_full(act, ("g", p))
                a.done(act.activation(kT[:, p, :], bank(("g", p))[:], ACT.Copy), drain(("g", p), "act"))

        for name in W_IN1:
            if name != W_IN1[-1]:
                convert()
            if name in ("lora0", "lora1"):
                for j in range(2 if name == "lora0" else 1):
                    m = j if name == "lora0" else 2
                    unshifted(name, j, lora[:] if m == 0 else gd[:, m - 1, :], m)
                if name == "lora1":
                    act.wait_ge(S["shift_ready"], 3)
                    a.done(act.activation(lora[0:HD, :], lora[0:HD, :], ACT.Tanh), S["lora_ready"])
                    a.done(act.activation(gd[:], gd[:], ACT.Sigmoid), S["lora_ready"])
            elif name[0] in "krv":
                dest, mu = {"k": (kT, 3), "v": (vT, 7), "r": (rT, 11)}[name[0]]
                for j in range(2):
                    n = 2 * int(name[1]) + j
                    unshifted(name, j, dest[:, n, :], mu + n)
                if name == "v1":
                    prep_act(0, 0)
            elif name[:2] == "pu":
                for j in range(2):
                    await_full(act, (name, j))
                    a.done(act.activation(uT[:, 2 * int(name[2]) + j, :], bank((name, j))[:], ACT.Gelu_apprx_tanh),
                           drain((name, j), "act"))
                if name == "pu0":
                    act.wait_ge(S["pv_std"], 1)
                    a.done(act.activation(rstd[:], rstd[:], ACT.Sqrt), S["pv_root"])
            else:
                half = slice(256 * int(name[2]), 256 * int(name[2]) + 256)
                for j in range(2):
                    await_full(act, (name, j))
                    a.done(act.activation(pv[:, 2 * j:2 * j + 2, half], bank((name, j))[:].rearrange("p (t d) -> p t d", t=2),
                                          ACT.Gelu_apprx_tanh), drain((name, j), "act"))
                if name == "pv0":
                    for part in (7, 2, 3, 4):
                        prep_act(0, part)

        def chunk_act(stage, p, t):
            d = sets[t % 2]
            link = links[t % 2][t // 2]
            if stage not in ("turn", "mv", "q2", "n4", "q4", "r2", "z1", "yl"):
                return
            name = (stage + "_act" if stage in TWO_BANKS else stage, p, t)
            b = bank(name)
            await_full(act, name)
            done = lambda ins: a.done(ins, drain(name, "act"))
            copy = lambda o, i: done(act.activation(o, i, ACT.Copy))
            if stage == "turn":
                if (p, t) == (0, 0):
                    act.wait_ge(S["sets_ready"], 1)
                copy(d["z0"][:].rearrange("p (a b) -> p a b", b=HD)[:, 0:4:3, :],
                     b[:, 0:P].rearrange("p (a b) -> p a b", b=HD))
                copy(d["vz"][:, HD:HD + P], b[:, P:2 * P])
            elif stage == "mv":
                copy(d["z0"][:, HD:HD + P], b[:, 0:P])
            elif stage == "q2":
                copy(d["rq"][:, :, 1, :], b[:, 0:256].rearrange("p (h n) -> p h n", h=2))
                copy(d["nn"][:], b[:, 256:512].rearrange("p (h n) -> p h n", h=2))
            elif stage == "n4":
                copy(d["nd"][:], b[:, 0:256].rearrange("p (h n) -> p h n", h=2))
            elif stage == "q4":
                copy(d["rq"][:, :, 1, :], b[:, 0:256].rearrange("p (h n) -> p h n", h=2))
            elif stage == "r2":
                copy(d["nn"][:], b[:, 0:256].rearrange("p (h n) -> p h n", h=2))
            elif stage == "z1":
                copy(d["nd"][:], b[:, 0:256].rearrange("p (h n) -> p h n", h=2))
            elif stage == "yl":
                copy(link["yl"][0:HD, :], b[HD:P, 0:P])
                copy(link["yl"][HD:P, :], b[0:HD, P:2 * P])

        def norm_act(p, part):
            if part == 1:
                await_drained(act, ("var", p), "dve")
                a.done(act.activation(norm_buffers[p]["sq"][:], norm_buffers[p]["sq"][:], ACT.Sqrt), S["norm_root"])

        def mixer_act(n):
            if n == 0:
                await_drained(act, ("hh", PAIRS - 1, TT - 1), "dve")
                a.done(act.activation(act_hi[:, 0:4, :], uT[:], ACT.Copy), S["y_hi"])
                convert()
            elif n == 1:
                act.wait_ge(S["yb_ready"], PAIRS - 1)
                a.done(act.activation(act_hi[:, 4:7, :], vT[:, 0:PAIRS - 1, :], ACT.Copy), S["y_hi"])
            elif n == 2:
                await_drained(act, ("y", PAIRS - 1, TT - 1), "dve")
                await_drained(act, ("state", PAIRS - 1, TT - 1, NCH - 1), "dve")
                convert()
            else:
                act.wait_ge(S["yb_ready"], PAIRS)
                a.done(act.activation(act_hi[:, 7, :], vT[:, PAIRS - 1, :], ACT.Copy), S["y_hi"])

        def ada_act(i):
            n = UNIT_AT[ada_unit(i)]
            raw_ready(act, n)
            a.done(act.activation(raw[n % RAW][:], raw[n % RAW][:], ACT.Copy, scale=col("c", (i - 1) % KC)), S["ada_scaled"])

        prep_act(0, 13)
        for kind, *args in CHUNK_SCHEDULE:
            if kind == "ada":
                ada_act(*args)
            if kind == "stage":
                chunk_act(*args)
            elif kind == "prep":
                prep_act(*args)
            elif kind == "norm":
                norm_act(*args)
            elif kind == "mixer":
                mixer_act(*args)
            elif kind == "mod_rows":
                await_full(act, ("mod_rows", *args))
                a.done(act.activation(acc[:, SEQ * args[0]:SEQ * args[0] + SEQ], bank(("mod_rows", *args))[:], ACT.Copy),
                       drain(("mod_rows", *args), "act"))

        act.dma_start(row_a[:], src["ln1_g"].partition_broadcast(P)).then_inc(load["rows1"], 16)
        act.dma_start(row_b[:], src["ln1_b"].partition_broadcast(P)).then_inc(load["rows1"], 16)
        for n in range(3):
            convert()

        def root_of_variance(n):
            t = (n - 1) % TT
            act.wait_ge(S["var1"], n + 1)
            a.done(act.activation(rstd[:, t:t + 1], rstd[:, t:t + 1], ACT.Sqrt), S["root1"])

        for s in range(TT + 1):
            if s < TT:
                root_of_variance(1 + s)
            if s:
                normalise(1, s - 1, S["xn_ready"])
        convert()
        affine_hi("h2", 2)

        def ffn_first(m):
            if m:
                convert()
            name = f"up1_{m}"
            await_full(act, (name, 0))
            a.done(act.activation(acc[:, 0:SEQ], bank((name, 0))[:], ACT.Silu), drain((name, 0), "act"))
            await_drained(act, (name, 1), "dve")
            a.done(act.activation(hid_hi[:, m, :], acc[:, SEQ:2 * SEQ], ACT.Copy), S["hid_hi_ready"])

        for m in range(FT):
            ffn_first(m)
        for n in range(FT // 2):
            convert()
            if n == 0:
                await_full(act, (f"up1_{FT - 1}", 1))
                act.dma_start(row2_a[:], src["ln2_g"].partition_broadcast(P)).then_inc(load["rows2"], 16)
                act.dma_start(row2_b[:], src["ln2_b"].partition_broadcast(P)).then_inc(load["rows2"], 16)

        def square_x(e, t):
            if e:
                act.wait_ge(S["x_ready2"], t + 1)
            elif t < TT - 1:
                act.wait_ge(S["x_ready"], t + 1)
            else:
                act.wait_ge(S["x_ready_last"], 1)
            a.done(act.activation(xn2[:, t, :], xres[:, t, :], ACT.Square, accum_out=x_sums[:, t:t + 1]),
                   S["squares_ready"])

        def root_x(e, t):
            act.wait_ge(S["x_rms_ready"], TT * e + TILE_ORDER[e].index(t) + 1)
            a.done(act.activation(x_sums[:, t:t + 1], x_sums[:, t:t + 1], ACT.Sqrt), S["x_rms_root"])

        def scaled_x(e, t):
            act.wait_ge(S["x_inverse"], t + 1)
            a.done(act.activation(xn2[:, t, :], xres[:, t, :], ACT.Copy, scale=x_sums[:, t:t + 1]), S["xn3_ready"])

        for t in range(TT - 1):
            root_of_variance(1 + TT + t)
            if t:
                normalise(2, t - 1, S["normal_ready"])
        normalise(2, TT - 2, S["normal_ready"])
        square_x(0, 0)
        root_of_variance(1 + TT + TT - 1)
        for t in TILE_ORDER[0][1:]:
            square_x(0, t)
            if t == 1:
                root_x(0, 0)
            root_x(0, t)
            if t == 3:
                convert()
        second_act(act, a, convert, affine_hi, square_x, root_x, scaled_x)

    @block.vector
    def _(dve):
        d = Order(dve, dve_step)
        V = dve
        counts = {"ada": 0}

        def ts(out, in0, s1, s2=None, op0=ALU.mult, op1=None, sem=None):
            d.step(V.tensor_scalar(out, in0, s1, s2, op0, op1) if op1 is not None else
                   V.tensor_scalar(out, in0, s1, None, op0), sem)

        def tt(out, a, b, op, sem=None):
            d.step(V.tensor_tensor(out, a, b, op), sem)

        def stt(out, a, s, b, op0, op1, sem=None):
            d.step(V.scalar_tensor_tensor(out=out, in0=a, scalar=s, in1=b, op0=op0, op1=op1), sem)

        def ada(i):
            n = UNIT_AT[f"ada0_{i}"]
            raw_ready(dve, n)
            if i == 0:
                dve.wait_ge(S["silu_c"], 1)
            r, c = raw[n % RAW][:], col("c", i)
            if i == 0:
                ts(acc[:], r, c, sem=ada_used)
            else:
                stt(acc[:], r, c, acc[:], ALU.mult, ALU.add, sem=ada_used)

        def layer_stats(t, source):
            d.step(V.bn_stats(stats[:, 0, :], source[:, 0:512]))
            d.step(V.bn_stats(stats[:, 1, :], source[:, 512:1024]))
            d.step(V.bn_aggr(mv[:, t, :], stats[:]))

        def offset(t):
            stt(mv[:, t, 0:1], mv[:, t, 0:1], -1.0, rstd[:, t:t + 1], ALU.mult, ALU.mult, sem=S["offset_ready"])

        def normalise():
            ts(rstd[:], mv[:, :, 1], LN_EPS, op0=ALU.add, sem=S["var1"])
            dve.wait_ge(S["root1"], 1)
            d.step(V.reciprocal(rstd[:], rstd[:]))
            for t in range(TT):
                offset(t)

        def affine_row(t, g, b):
            tt(xres[:, t, :], xres[:, t, :], g[:], ALU.mult)
            tt(xres[:, t, :], xres[:, t, :], b[:], ALU.add)

        def affine_lo(stage, part, temp):
            for k in range(KC):
                full = temp[:, k % 2, :]
                await_full(dve, (stage, k))
                await_drained(dve, (stage, k), "act")
                if isinstance(part, str):
                    stt(act_lo[:, k, :], bank((stage, k))[:], col(part, k), act_hi[:, k, :].bitcast(F32), ALU.mult,
                        ALU.subtract, sem=drain((stage, k), "dve"))
                    continue
                ts(full, bank((stage, k))[:], affine[:, part, k:k + 1], affine[:, part + 1, k:k + 1],
                   ALU.mult, ALU.add, sem=drain((stage, k), "dve"))
                tt(act_lo[:, k, :], full, act_hi[:, k, :].bitcast(F32), ALU.subtract, sem=S["h_lo"])

        def mod_columns(sums, part, g, b, sh, sc, sem=None):
            tt(modc[:], sums, pc[:, COLS[sh]:COLS[sh] + 2 * KC], ALU.add, sem=sem)
            ts(modc[:, KC:], modc[:, KC:], 1.0, op0=ALU.add)
            tt(affine[:, part, :], pc[:, COLS[g]:COLS[g] + KC], modc[:, KC:], ALU.mult)
            tt(affine[:, part + 1, :], pc[:, COLS[b]:COLS[b] + KC], modc[:, KC:], ALU.mult)
            tt(affine[:, part + 1, :], affine[:, part + 1, :], modc[:, 0:KC], ALU.add, sem=S["affine1"])

        d.step(V.memset(ones[:], 1.0))
        d.step(V.memset(restart[:], 1.0))
        d.step(V.memset(restart[:].rearrange("p (c t) -> p c t", t=CH)[:, :, 0:1], 0.0))
        dve.wait_ge(load["params"], 16)
        ts(omu[:], pc[:, COLS["mu_l"]:COLS["mu_l"] + N_MU], -1.0, 1.0, ALU.mult, ALU.add)
        ts(oka[:], pc[:, COLS["k_a"]:COLS["k_a"] + 4], -1.0, 1.0, ALU.mult, ALU.add)
        for i in (0, 2):
            ada(i)
        dve.wait_ge(load["x"], 16)
        for t in range(TT):
            layer_stats(t, xres[:, t, :])
        normalise()
        for i in range(RAW, KC):
            if i not in ADA_PE:
                ada(i)
        await_full(dve, "cols0")
        mod_columns(bank("cols0")[:, 0:2 * KC], 0, "emb_g", "emb_b", "b_sh1", "b_sc1", sem=drain("cols0", "dve"))
        affine_lo("h1", 0, pairs[0]["ar"])

        def shifted(name, j, dest, mu, sem=None):
            await_drained(dve, (name, j), "act")
            stt(dest[:, 1:SEQ], bank((name, j))[:, 0:SEQ - 1], pc[:, COLS["mu_l"] + mu:COLS["mu_l"] + mu + 1],
                dest[:, 1:SEQ], ALU.mult, ALU.add, sem=drain((name, j), "dve"))

        def prep_dve(p, part):
            pr = pairs[p % 2]
            if part == 1:
                await_drained(dve, ("z", p), "act")
                d.step(V.tensor_tensor_scan(pr["cs"][:], restart[:], pr["sig"][:], 0.0, ALU.mult, ALU.add))
                tt(pr["sig"][:], pr["cs"][:], pr["sig"][:], ALU.subtract, sem=S["cs_ready"])
            elif part == 6:
                await_full(dve, ("kk", p))
                ts(pr["sq"][:], bank(("kk", p))[:], 1e-24, op0=ALU.max, sem=drain(("kk", p), "dve"))
            elif part in (8, 9, 10, 11):
                dve.wait_ge(S["root_ready"], p + 1)
                c = slice((part - 8) * QUARTER, (part - 7) * QUARTER)
                d.step(V.reciprocal(pr["sq"][:, c], pr["sq"][:, c]), S["inverse_ready"] if part == 11 else None)
            elif part == 13 and p:
                bonus_dve(p)

        def bonus_dve(p):
            await_full(dve, ("bonus", p))
            tt(rT[:, p, :], bank(("bonus", p))[:], vT[:, p, :], ALU.mult, sem=drain(("bonus", p), "dve"))

        for n, name in enumerate(W_IN1):
            if name in ("lora0", "lora1"):
                for j in range(2 if name == "lora0" else 1):
                    m = j if name == "lora0" else 2
                    shifted(name, j, lora[:] if m == 0 else gd[:, m - 1, :], m)
                    d.step(V.tensor_copy(stats[:, 0, 0:1], stats[:, 0, 0:1]), S["shift_ready"])
            elif name[0] in "krv":
                dest, mu = {"k": (kT, 3), "v": (vT, 7), "r": (rT, 11)}[name[0]]
                for j in range(2):
                    m = 2 * int(name[1]) + j
                    shifted(name, j, dest[:, m, :], mu + m)
            if n < TT:
                dve.wait_ge(load["rows0"], 32)
                affine_row(n, row_a, row_b)
            if n == KC - 1:
                dve.wait_ge(load["gmlp"], 80)
                tt(wsT[:], wsT[:], up[:].unsqueeze(1).to_broadcast([P, 4, P]), ALU.mult, sem=S["wst_ready"])
                for part in (1, 5, 6):
                    prep_dve(0, part)
                    prep_side(d, 0, part)
            if name == "pv0":
                for part in (4, 8, 9, 10, 11, 12):
                    prep_dve(0, part)
                    prep_side(d, 0, part)

        for t in range(TT):
            await_drained(dve, ("pv1", t // 2), "act")
            d.step(V.bn_stats(stats[:, 0, :], pv[:, t, :]))
            d.step(V.bn_aggr(mv[:, t, :], stats[:, 0:1, :]))
        ts(rstd[:], mv[:, :, 1], LN_EPS, op0=ALU.add, sem=S["pv_std"])
        dve.wait_ge(S["pv_root"], 1)
        d.step(V.reciprocal(rstd[:], rstd[:]))
        for t in range(TT):
            ts(pv[:, t, :], pv[:, t, :], mv[:, t, 0:1], rstd[:, t:t + 1], ALU.subtract, ALU.mult)
            tt(pv[:, t, :], pv[:, t, :], sg_g[:], ALU.mult)
            tt(pv[:, t, :], pv[:, t, :], sg_b[:], ALU.add, sem=S["pv_ready"])
        for g in range(4):
            await_full(dve, ("sgu", g))
            tt(sg_g[:].rearrange("p (t n) -> p t n", n=P), bank(("sgu", g))[:].rearrange("p (t n) -> p t n", n=P),
               bs[:, g, :].unsqueeze(1).to_broadcast([P, TT, P]), ALU.add, sem=drain(("sgu", g), "dve"))
            await_drained(dve, ("pu1", 1), "act")
            tt(uT[:, g, :], uT[:, g, :], sg_g[:], ALU.mult)
        await_full(dve, ("pu1", 1))
        await_full(dve, ("sgu", 3))
        for q in range(2):
            d.step(V.memset(sets[q]["vz"][:], 0.0))
        d.step(V.tensor_copy(stats[:, 0, 0:1], stats[:, 0, 0:1]), S["sets_ready"])

        def heads(ap):
            return ap.rearrange("p (h n) -> p h n", h=2)

        def chunk_dve(stage, p, t):
            s, link, ar = sets[t % 2], links[t % 2][t // 2], pairs[p % 2]["ar"]
            name = (stage, p, t)
            if stage in ("mv", "q2", "n4"):
                return
            b = bank(name)
            await_full(dve, name)
            if stage == "yl":
                await_drained(dve, name, "act")
            out_ = drain(name, "dve")
            if stage == "turn":
                rows = chunk_rows[:].unsqueeze(2).to_broadcast([P, NCH, P])
                for key, part in (("bx", 0), ("kx", 1)):
                    tt(s[key][:], b[:, part * P:part * P + P].unsqueeze(1).to_broadcast([P, NCH, P]), rows,
                       ALU.mult, sem=out_)
            elif stage in ("m1", "m2"):
                h = int(stage[1]) - 1
                tt(s["mm"][:, h], b[:].rearrange("p (a n) -> p a n", a=4), masks[:], ALU.mult, sem=out_)
            elif stage in ("n1", "n2"):
                h = int(stage[1]) - 1
                tt(s["nd"][:, h, :], b[:, 0:P], mask_d[:], ALU.mult, sem=out_)
                tt(s["ee"][:, h, :], b[:, 0:P], mask_e[:], ALU.mult, sem=out_)
                if h:
                    tt(s["rq"][:, :, 0, :], s["mm"][:, :, 0, :], ident[:].unsqueeze(1).to_broadcast([P, 2, P]),
                       ALU.add, sem=S["r0_ready"])
            elif stage == "q4":
                tt(s["rb"][:], heads(b[:, 0:256]), s["rq"][:, :, 0, :], ALU.add, sem=out_)
            elif stage == "r2":
                tt(s["rq"][:, :, 0, :], heads(b[:, 0:256]), s["rb"][:], ALU.add, sem=out_)
            elif stage == "r3":
                tt(s["rb"][:], heads(b[:, 0:256]), s["rq"][:, :, 0, :], ALU.add, sem=out_)
            elif stage == "z1":
                d.step(V.tensor_copy(s["z1"][:], b[:, 0:256]), out_)
            elif stage == "z2":
                tt(s["z"][:], b[:, 0:256], s["z1"][:], ALU.add, sem=out_)
                d.step(V.tensor_copy(s["nn"][:, 0, :].rearrange("p (a b) -> p a b", b=HD),
                                     s["z"][:].rearrange("p (a b) -> p a b", b=HD)[:, 0:4:3, :]), S["w_ready"])
            elif stage == "yl":
                tt(link["rp"][0:HD, :], b[0:HD, 0:P], ar[0:HD, 1, tok(t)], ALU.add, sem=out_)
                tt(link["rp"][HD:P, :], b[HD:P, P:2 * P], ar[HD:P, 1, tok(t)], ALU.add, sem=out_)
            elif stage in ("gt", "hh"):
                tt(link["gt" if stage == "gt" else "hb"][:], b[:].rearrange("p (c n) -> p c n", c=NCH),
                   bd64[:].unsqueeze(1).to_broadcast([P, NCH, P]), ALU.mult, sem=out_)

        def chain_dve(p, t, c):
            link, y = links[t % 2][t // 2], norm_buffers[p]["kk"]
            old, new = state[c % 2], state[(c + 1) % 2]
            if (t, c) == (0, 0):
                d.step(V.memset(old[:], 0.0), S["state_zero"])
            g = t * NCH + c
            stt(decayed[:], old[:], pend[p][:, g:g + 1], link["hb"][:, c, :], ALU.mult, ALU.add)
            name = ("state", p, t, c)
            await_full(dve, name)
            tt(new[:], bank(name)[:, 0:P], decayed[:], ALU.add, sem=drain(name, "dve"))
            if c == NCH - 1:
                await_full(dve, ("y", p, t))
                await_drained(dve, ("yl", p, t), "act")
                if (p, t) == (PAIRS - 1, 0):
                    dve.wait_ge(S["yb_ready"], p)
                tt(y[:, tok(t)], bank(("y", p, t))[:, 0:P], link["yl"][:], ALU.add, sem=drain(("y", p, t), "dve"))

        def norm_dve(p, part):
            kk, sq = norm_buffers[p]["kk"], norm_buffers[p]["sq"]
            if part == 0:
                await_full(dve, ("mean", p))
                stt(kk[:], bank(("mean", p))[:], -1.0 / HD, kk[:], ALU.mult, ALU.add, sem=drain(("mean", p), "dve"))
                tt(sq[:], kk[:], kk[:], ALU.mult, sem=S["y_sq"])
            elif part == 1:
                await_full(dve, ("var", p))
                ts(sq[:], bank(("var", p))[:], 1.0 / HD, GN_EPS, ALU.mult, ALU.add, sem=drain(("var", p), "dve"))
            elif part < 6:
                dve.wait_ge(S["norm_root"], p + 1)
                c = slice((part - 2) * QUARTER, (part - 1) * QUARTER)
                d.step(V.reciprocal(sq[:, c], sq[:, c]), S["norm_inverse"] if part == 5 else None)

        bonus_dve(0)
        dve.wait_ge(load["masks"], 16 * 7)
        for kind, *args in CHUNK_SCHEDULE:
            if kind == "stage":
                chunk_dve(*args)
            elif kind == "chain":
                chain_dve(*args)
            elif kind == "prep":
                prep_dve(*args)
            elif kind == "norm":
                norm_dve(*args)
                if args == [PAIRS - 1, 6]:
                    norm_side(d, *args)
            elif kind == "cols1":
                q, rows = args[0], pairs[1]["ep"][:].rearrange("p (a n) -> p a n", a=4)
                await_full(dve, ("cols1", q))
                tt(rows, bank(("cols1", q))[:].rearrange("p (a n) -> p a n", a=4),
                   ident[:].unsqueeze(1).to_broadcast([P, 4, P]), ALU.mult, sem=drain(("cols1", q), "dve"))
                d.step(V.tensor_reduce(out=modc[:, 4 * q:4 * q + 4], in_=rows, op=ALU.add, axis=AX_X))
                if q == 3:
                    mod_columns(modc[:], 2, "ln1_g", "ln1_b", "b_sh2", "b_sc2")
        dve.wait_ge(S["y_hi"], 3)
        tt(act_lo[:, 7, :], vT[:, PAIRS - 1, :], act_hi[:, 7, :].bitcast(F32), ALU.subtract, sem=S["y_lo_last"])

        def residual(stage, t, gate, temp):
            for j in range(2):
                h = slice(SEQ * j, SEQ * j + SEQ)
                await_full(dve, (stage, t, j))
                tt(temp[:, h], bank((stage, t, j))[:], gate[:, h], ALU.mult, sem=drain((stage, t, j), "dve"))
            stt(xres[:, t, :], xres[:, t, :], ALPHA, temp[:], ALU.mult, ALU.add)
            layer_stats(t, xres[:, t, :])
            ts(rstd[:, t:t + 1], mv[:, t, 1:2], LN_EPS, op0=ALU.add, sem=S["var1"])

        def inverse(n, t):
            dve.wait_ge(S["root1"], n + 1)
            d.step(V.reciprocal(rstd[:, t:t + 1], rstd[:, t:t + 1]))

        def x_mean_square(e, t):
            dve.wait_ge(S["squares_ready"], TT * e + TILE_ORDER[e].index(t) + 1)
            ts(x_sums[:, t:t + 1], x_sums[:, t:t + 1], 1.0 / DM, RMS_EPS, ALU.mult, ALU.add, sem=S["x_rms_ready"])

        def inverse_x(e, t):
            dve.wait_ge(S["x_rms_root"], TT * e + TILE_ORDER[e].index(t) + 1)
            d.step(V.reciprocal(x_sums[:, t:t + 1], x_sums[:, t:t + 1]), S["x_inverse"] if e else None)
            if not e:
                ts(xn2[:, t, :], xres[:, t, :], x_sums[:, t:t + 1], sem=S["xn3_first"])

        await_drained(dve, ("mod_rows", 3), "act")
        for s in range(TT + 1):
            if s < TT:
                residual("mix1", s, acc[:, 0:DM], mixed)
            if s:
                t = s - 1
                inverse(1 + t, t)
                offset(t)
        affine_lo("h2", 2, pairs[0]["ar"])
        for m in range(FT):
            name = f"up1_{m}"
            await_full(dve, (name, 1))
            await_drained(dve, (name, 0), "act")
            tt(acc[:, SEQ:2 * SEQ], bank((name, 1))[:], acc[:, 0:SEQ], ALU.mult, sem=drain((name, 1), "dve"))
            dve.wait_ge(S["hid_hi_ready"], m + 1)
            tt(hid_lo[:, m, :], acc[:, SEQ:2 * SEQ], hid_hi[:, m, :].bitcast(F32), ALU.subtract, sem=S["hid_ready"])
            if m < TT:
                dve.wait_ge(load["rows1"], 32)
                affine_row(m, row_a, row_b)
        dve.wait_ge(load["rows2"], 32)
        gate, last = acc[:, DM:2 * DM], TT - 1
        for t in range(last):
            residual("ff1", t, gate, mixed2)
            for n in ((), (0,), (1, 2))[t]:
                inverse(1 + TT + n, n)
                offset(n)
        residual("ff1", last, gate, mixed2)
        stt(xres[:, last, :], xres[:, last, :], mv[:, last, 0:1], row2_a[:], ALU.subtract, ALU.mult)
        inverse(1 + TT + last, last)
        stt(xres[:, last, :], xres[:, last, :], rstd[:, last:last + 1], row2_b[:], ALU.mult, ALU.add, sem=S["x_ready_last"])
        x_mean_square(0, 0)
        x_mean_square(0, 1)
        inverse_x(0, 0)
        inverse_x(0, 1)
        for t in TILE_ORDER[0][2:]:
            x_mean_square(0, t)
            inverse_x(0, t)
        second_dve(dve, d, ts, tt, stt, affine_lo, x_mean_square, inverse_x)

    @block.tensor
    def _(pe):
        used = [0]

        def three(o, l, r, first, last):
            pe.matmul(o, l[0], r[0], start=first, stop=False)
            pe.matmul(o, l[0], r[1], start=False, stop=False)
            return pe.matmul(o, l[1], r[0], start=False, stop=last)

        def next_unit(name):
            i = used[0]
            used[0] += 1
            n = SPLIT_UNITS[i]
            assert UNITS[n][0] == name, (UNITS[n][0], name)
            pe.wait_ge(lo_ready, i + 1)
            kc = UNITS[n][3]
            w = UNIT_SIZE[n] // kc
            return [x[i % SPLIT][:, :kc * w].rearrange("p (k n) -> p k n", k=kc) for x in (whi, wlo)], w

        def dense_feature(name, blocks, beside=None, stage=None, upper_first=False):
            (hi, lo), w = next_unit(name)

            def product(j, k, step=None):
                step = k if step is None else step
                c = slice(P * j, P * j + P)
                return three(bank((name, j))[:], (hi[:, k, c], lo[:, k, c]), (act_hi[:, k, :], act_lo[:, k, :]),
                             step == 0, step == KC - 1)

            if stage is not None:
                for j in range(blocks):
                    claim(pe, (name, j))
                for k in range(KC):
                    if stage in ("h1", "h2"):
                        pe.wait_ge(S["h_lo"], KC * (int(stage[1]) - 1) + k + 1)
                    else:
                        await_drained(pe, (stage, k), "dve")
                    for j in range(blocks):
                        mm = product(j, k)
                        if k == KC - 1:
                            mm.then_inc(full_sem((name, j))[0], 1)
                return
            for j in range(blocks):
                claim(pe, (name, j))
                for k in range(KC):
                    if beside is not None:
                        beside(j * KC + k)
                    if upper_first and j == blocks - 1:
                        mm = product(j, (k + KC // 2) % KC, k)
                        if k == KC // 2 - 1:
                            mm.then_inc(S["upper_free"], 1)
                    else:
                        mm = product(j, k)
                mm.then_inc(full_sem((name, j))[0], 1)

        def dense_token(name, per_bank):
            (hi, lo), w = next_unit(name)
            for j in range(TT // per_bank):
                claim(pe, (name, j))
                for i in range(per_bank):
                    t = per_bank * j + i
                    for k in range(KC):
                        mm = three(bank((name, j))[:, i * w:i * w + w], (act_hi[:, k, tok(t)], act_lo[:, k, tok(t)]),
                                   (hi[:, k, :], lo[:, k, :]), k == 0, k == KC - 1)
                mm.then_inc(full_sem((name, j))[0], 1)

        def rows_product(stage, n, n_units, weights, parts, t, k, turned=False):
            (hi, lo), (hi_in, lo_in) = weights, parts
            for j in range(2):
                c, f = slice(SEQ * j, SEQ * j + SEQ), 2 * ((n + 2) % 4 if turned else n) + k
                last = n == n_units - 1 and k == 1
                mm = three(bank((stage, t, j))[:], (hi_in[:, f, tok(t)], lo_in[:, f, tok(t)]),
                           (hi[:, k, c], lo[:, k, c]), n == k == 0, last)
                if last:
                    mm.then_inc(full_sem((stage, t, j))[0], 1)
            return mm

        def dense_rows(stage, unit, n_units, parts, begun=None, ready=None, turned=False):
            for n in range(n_units):
                weights = begun if n == 0 and begun else next_unit(f"{unit}_{n}")[0]
                order = [(t, k) for k in range(2) for t in range(TT)]
                if n == n_units - 1:
                    order = [(t, k) for t in range(TT) for k in range(2)]
                elif n == 0:
                    tiles = (TT - 1,) if begun else range(TT)
                    order = [(t, k) for k in range(2) for t in tiles]
                if ready is not None and n in ready:
                    pe.wait_ge(*ready[n])
                for t, k in order:
                    if n == k == 0:
                        for j in range(2):
                            claim(pe, (stage, t, j))
                    mm = rows_product(stage, n, n_units, weights, parts, t, k, turned)
                if n < n_units - 1:
                    mm.then_inc(unit_used, 1)

        def columns(name):
            for j in range(2 * KC):
                mm = pe.matmul(bank(name)[:, j:j + 1], acc[:, P * j:P * j + P], ones[:], start=False, stop=j == 2 * KC - 1)
            mm.then_inc(filled[job(name)[0]], 1)

        def turn_x(stage, ready, source=xres, features=range(KC), tiles=range(TT)):
            for k in features:
                claim(pe, (stage, k))
            for n, t in enumerate(tiles):
                pe.wait_ge(ready[0], ready[1] + n + 1)
                for k in features:
                    mm = pe.transpose(bank((stage, k))[:, tok(t)], source[:, t, P * k:P * k + P], ident[:])
                    if n == TT - 1:
                        mm.then_inc(filled[job((stage, k))[0]], 1)

        pe.wait_ge(S["silu_c"], 1)
        claim(pe, "cols0")
        for i in ADA_PE:
            raw_ready(pe, i)
            for j in range(2 * KC):
                mm = pe.matmul(bank("cols0")[:, j:j + 1], raw[i % RAW][:, P * j:P * j + P], col("c", i),
                               start=(i, j) == (ADA_PE[0], 0), stop=False)
            mm.then_inc(S["ada_used_pe"], 1)
        pe.wait_ge(load["consts"], 32)
        turn_x("h1", (S["xn_ready"], 0), features=range(KC - 1))
        pe.wait_ge(ada_used, KC - len(ADA_PE))
        columns("cols0")
        turn_x("h1", (S["xn_ready"], 0), features=range(KC - 1, KC))

        def fill(name, mm):
            mm.then_inc(filled[job(name)[0]], 1)

        def prep_pe(p, part):
            c, sq = slice(P * p, P * p + P), pairs[p % 2]["sq"]
            if part == 0:
                claim(pe, ("z", p))
                fill(("z", p), pe.matmul(bank(("z", p))[:], wup[0:HD, c], lora[0:HD, :], start=True, stop=True))
                claim(pe, ("a", p))
                fill(("a", p), pe.matmul(bank(("a", p))[:], wup[HD:P, c], lora[HD:P, :], start=True, stop=True))
            elif part == 6:
                claim(pe, ("kk", p))
                pe.wait_ge(S["kk_sq"], p + 1)
                fill(("kk", p), pe.matmul(bank(("kk", p))[:], bd64[:], sq[:], start=True, stop=True))
            elif part == 13:
                claim(pe, ("bonus", p))
                pe.wait_ge(S["prep_ready"], p + 1)
                fill(("bonus", p), pe.matmul(bank(("bonus", p))[:], bd64[:], rT[:, p, :], start=True, stop=True))
                claim(pe, ("g", p))
                pe.matmul(bank(("g", p))[:], gup[:, 0, c], gd[:, 0, :], start=True, stop=False)
                fill(("g", p), pe.matmul(bank(("g", p))[:], gup[:, 1, c], gd[:, 1, :], start=False, stop=True))

        for name in W_IN1:
            if name == "pv0":
                pe.wait_ge(load["masks"], 16 * 7)
                pe.wait_ge(S["lora_ready"], 2)
                prep_pe(0, 0)
                prep_pe(0, 6)
            if name[:2] == "pv":
                dense_token(name, 2)
            else:
                dense_feature(name, 1 if name == "lora1" else 2, stage="h1" if name == W_IN1[0] else None)

        pe.wait_ge(S["wst_ready"], 1)
        pe.wait_ge(S["pv_ready"], TT)
        for g in range(4):
            claim(pe, ("sgu", g))
            for t in range(TT):
                mm = pe.matmul(bank(("sgu", g))[:, tok(t)], pv[:, t, P * g:P * g + P], wsT[:, g, :], start=True, stop=True)
            fill(("sgu", g), mm)

        def chunk_pe(stage, p, t):
            s, pr = sets[t % 2], pairs[p % 2]
            ar, sig, cs, bt, kt = (pr[n] for n in ("ar", "sig", "cs", "bt", "kt"))
            name = (stage, p, t)
            b = bank(name)
            claim(pe, name)
            ready = lambda st, by: await_drained(pe, (st + "_act" if by == "act" and st in TWO_BANKS else st, p, t), by)
            mm = None
            if stage in TWO_BANKS:
                name_act = (stage + "_act", p, t)
                b_act = bank(name_act)
                claim(pe, name_act)
            if stage == "turn":
                pe.wait_ge(S["bars_ready"], p + 1)
                for i, x in enumerate((sig[:, tok(t)], cs[:, tok(t)])):
                    mm = pe.transpose(b[:, i * P:i * P + P], x, ident[:])
                for i, x in enumerate((ar[:, 0, tok(t)], vT[:, p, tok(t)])):
                    mm_act = pe.transpose(b_act[:, i * P:i * P + P], x, ident[:])
            elif stage in ("m1", "m2"):
                rows = slice(0, HD) if stage == "m1" else slice(HD, P)
                for i, x in enumerate((bt, kt)):
                    mm = pe.matmul(b[:, 256 * i:256 * i + 256], x[rows, tok(t)], ar[rows, :, tok(t)], start=True, stop=True)
            elif stage in ("n1", "n2"):
                rows = slice(0, HD) if stage == "n1" else slice(HD, P)
                mm = pe.matmul(b[:, 0:P], ar[rows, 0, tok(t)], bt[rows, tok(t)], start=True, stop=True)
            elif stage == "mv":
                ready("turn", "act")
                ready("m2", "dve")
                for h in range(2):
                    mm = pe.matmul(b[:, HD * h:HD * h + HD], s["mm"][:, h, 2, :], s["vz"][:, HD + HD * h:2 * HD + HD * h],
                                   start=True, stop=True)
            elif stage == "q2":
                ready("n2", "dve")
                for h in range(2):
                    pe.matmul(b[:, P * h:P * h + P], s["nd"][:, h, :], s["mm"][:, h, 0, :], start=True, stop=True)
                    mm = pe.matmul(b[:, 256 + P * h:256 + P * h + P], s["mm"][:, h, 0, :], s["nd"][:, h, :],
                                   start=True, stop=True)
            elif stage == "n4":
                ready("q2", "act")
                for h in range(2):
                    mm = pe.matmul(b[:, P * h:P * h + P], s["rq"][:, h, 1, :], s["nn"][:, h, :], start=True, stop=True)
            elif stage == "q4":
                pe.wait_ge(S["r0_ready"], p * TT + t + 1)
                for h in range(2):
                    mm_act = pe.matmul(b_act[:, P * h:P * h + P], s["nn"][:, h, :], s["rq"][:, h, 1, :], start=True, stop=True)
                for h in range(2):
                    mm = pe.matmul(b[:, P * h:P * h + P], s["nn"][:, h, :], s["rq"][:, h, 0, :], start=True, stop=True)
            elif stage == "r2":
                ready("n4", "act")
                ready("q4", "dve")
                ready("q4", "act")
                for h in range(2):
                    mm = pe.matmul(b[:, P * h:P * h + P], s["nd"][:, h, :], s["rb"][:, h, :], start=True, stop=True)
                for h in range(2):
                    mm_act = pe.matmul(b_act[:, P * h:P * h + P], s["rq"][:, h, 1, :], s["nd"][:, h, :],
                                       start=True, stop=True)
            elif stage == "r3":
                ready("r2", "dve")
                ready("r2", "act")
                for h in range(2):
                    mm = pe.matmul(b[:, P * h:P * h + P], s["nn"][:, h, :], s["rq"][:, h, 0, :], start=True, stop=True)
            elif stage == "z1":
                ready("r3", "dve")
                ready("mv", "act")
                for h in range(2):
                    mm_act = pe.matmul(b_act[:, P * h:P * h + P], s["ee"][:, h, :], s["rb"][:, h, :], start=True, stop=True)
                for h in range(2):
                    mm = pe.matmul(b[:, P * h:P * h + P], s["rb"][:, h, :], s["z0"][:, P * h:P * h + P],
                                   start=True, stop=True)
            elif stage == "z2":
                ready("z1", "act")
                ready("z1", "dve")
                for h in range(2):
                    mm = pe.matmul(b[:, P * h:P * h + P], s["nd"][:, h, :], s["z1"][:, P * h:P * h + P], start=True, stop=True)
            elif stage == "yl":
                ready("z2", "dve")
                for h in range(2):
                    c = slice(P * h, P * h + P)
                    pe.matmul(b[:, c], s["z"][:, c], s["mm"][:, h, 1, :], start=True, stop=False)
                    mm = pe.matmul(b[:, c], s["vz"][:, c], s["mm"][:, h, 3, :], start=False, stop=True)
            elif stage == "gt":
                pe.wait_ge(S["w_ready"], p * TT + t + 1)
                mm = pe.matmul(b[:], s["nn"][:, 0, :], s["bx"][:], start=True, stop=True)
            elif stage == "hh":
                for c in range(NCH):
                    o = b[:, P * c:P * c + P]
                    pe.matmul(o, s["bx"][:, c, :], s["z"][:, HD:HD + P], start=True, stop=False)
                    mm = pe.matmul(o, s["kx"][:, c, :], s["vz"][:, HD:HD + P], start=False, stop=True)
            fill(name, mm)
            if stage in TWO_BANKS:
                fill(name_act, mm_act)

        def chain_pe(p, t, c):
            link, old = links[t % 2][t // 2], state[c % 2]
            if c == 0:
                claim(pe, ("y", p, t))
                await_drained(pe, ("hh", p, t), "dve")
            if (t, c) == (0, 0):
                pe.wait_ge(S["state_zero"], p + 1)
            else:
                await_drained(pe, ("state", p, t if c else t - 1, c - 1 if c else NCH - 1), "dve")
            mm = pe.matmul(bank(("y", p, t))[:, CH * c:CH * c + CH], old[:], link["rp"][:, CH * c:CH * c + CH],
                           start=True, stop=True)
            if c == NCH - 1:
                fill(("y", p, t), mm)
            name = ("state", p, t, c)
            claim(pe, name)
            fill(name, pe.matmul(bank(name)[:, 0:P], link["gt"][:, c, :], old[:], start=True, stop=True))

        def norm_pe(p, part):
            if part == 0:
                claim(pe, ("mean", p))
                await_drained(pe, ("y", p, TT - 1), "dve")
                fill(("mean", p), pe.matmul(bank(("mean", p))[:], bd64[:], norm_buffers[p]["kk"][:], start=True, stop=True))
            elif part == 1:
                claim(pe, ("var", p))
                pe.wait_ge(S["y_sq"], p + 1)
                fill(("var", p), pe.matmul(bank(("var", p))[:], bd64[:], norm_buffers[p]["sq"][:], start=True, stop=True))

        def mod_rows(j):
            if j == 0:
                pe.wait_ge(load["bias"], 16)
                pe.wait_ge(ada_used, 3 * KC - len(ADA_PE))
            claim(pe, ("mod_rows", j))
            b = bank(("mod_rows", j))
            pe.matmul(b[:], ones[:].to_broadcast([P, P]), acc[:, SEQ * j:SEQ * j + SEQ], start=True, stop=False)
            fill(("mod_rows", j), pe.matmul(b[:], ident[0:4, j:j + 1].to_broadcast([4, P]), bias4[:], start=False, stop=True))

        begun = []

        def out1(t, k):
            if (t, k) == (0, 0):
                begun.append(next_unit("out1_0")[0])
                pe.wait_ge(S["y_lo"], 1)
            if k == 0:
                for j in range(2):
                    claim(pe, ("mix1", t, j))
            rows_product("mix1", 0, 4, begun[0], (act_hi, act_lo), t, k)

        prep_pe(0, 13)
        for kind, *args in CHUNK_SCHEDULE:
            if kind == "stage":
                chunk_pe(*args)
            elif kind == "chain":
                chain_pe(*args)
            elif kind == "prep":
                prep_pe(*args)
            elif kind == "norm":
                norm_pe(*args)
            elif kind == "cols1":
                q = args[0]
                pe.wait_ge(ada_used, 2 * KC - len(ADA_PE))
                claim(pe, ("cols1", q))
                fill(("cols1", q), pe.matmul(bank(("cols1", q))[:], ones[:].to_broadcast([P, P]),
                                             acc[:, SEQ * q:SEQ * q + SEQ], start=True, stop=True))
            elif kind == "mod_rows":
                mod_rows(*args)
            elif kind == "out1":
                out1(*args)

        dense_rows("mix1", "out1", 4, (act_hi, act_lo), begun[0], {2: (S["y_lo"], 2), 3: (S["y_lo_last"], 1)})
        turn_x("h2", (S["xn_ready"], TT))
        for m in range(FT):
            dense_feature(f"up1_{m}", 2, stage=None if m else "h2")
        dense_rows("ff1", "down1", FT // 2, (hid_hi, hid_lo),
                   ready={n: (S["hid_ready"], 2 * n + 2) for n in range(FT // 2)})
        second_pe(pe, three, next_unit, dense_feature, dense_rows, turn_x, fill)

    ctx.close()


def lay_out(inputs):
    x = {k: np.asarray(v) for k, v in inputs.items()}
    c = lambda v: np.asarray(v).reshape(-1, P).T
    base = 2 * MIX
    mu = x["mu_shift"][0]
    lora = 3 * MIX
    ffn = x["ffn_conv_w_2"][0]
    b = x["b_ada"][0].reshape(6, DM)
    cols = {"c": c(x["c"]), "emb_g": c(x["emb_ln_g"]), "emb_b": c(x["emb_ln_b"]), "mu_l": c(mu[lora:lora + 128]),
            "mu_g0": c(mu[lora + 128:lora + 256]), "mu_g1": c(mu[lora + 160:lora + 288]),
            "mu_r": c(mu[:MIX]), "mu_k": c(mu[MIX:2 * MIX]), "mu_v": c(mu[2 * MIX:3 * MIX]),
            "ln1_g": c(x["ln1_g"]), "ln1_b": c(x["ln1_b"]), "nmp": c(x["norm_mix_pre_2"]), "nfp": c(x["norm_ffn_pre_2"]),
            "cmix": c(x["conv_mix_w_2"]), "cffn": c(ffn),
            "pe_k": np.tile(x["pe_cmp_k_2"][0].T, (2, 1)), "pe_v": np.tile(x["pe_cmp_v_2"][0].T, (2, 1)),
            "has_key": (np.arange(P)[:, None] >= L_CMP - 1).astype(np.float32),
            "b_sh1": c(b[0]), "b_sc1": c(b[1]), "b_sh2": c(b[3]), "b_sc2": c(b[4])}
    for n in ("w0", "a0", "k_k", "k_a", "r_k", "lnx_g", "lnx_b"):
        cols[n] = c(x[n])
    params = np.concatenate([cols[n] for n in COLS], 1)
    parts = []
    for _, matrix, row, tiles, ranges in UNITS:
        w = x[matrix][0]
        w = np.concatenate([w[row:row + tiles * P, a:a + n] for a, n in ranges], 1)
        parts.append(w.reshape(tiles, P, -1).transpose(1, 0, 2).reshape(P, -1))
    g_up = np.zeros((P, 2, MIX), np.float32)
    g_up[:, 0] = x["g_up"][0][:P]
    g_up[P - 32:, 1] = x["g_up"][0][P:]
    return {
        "x": x["x"], "params": params, "weights": np.concatenate(parts, 1), "consts": shape_constants(),
        "w_s_t": x["w_s"][0].transpose(2, 0, 1), "b_s": x["b_s"][0], "sg_ln_g": x["sg_ln_g"][0], "sg_ln_b": x["sg_ln_b"][0],
        "emb_ln_g": x["emb_ln_g"], "emb_ln_b": x["emb_ln_b"], "ln1_g": x["ln1_g"][0], "ln1_b": x["ln1_b"][0],
        "ln2_g": x["ln2_g"][0], "ln2_b": x["ln2_b"][0], "lora_up": np.concatenate([x["w_up"][0], x["a_up"][0]], 0),
        "w1": np.stack([x[f"w_cmp_{n}1_2"][0].reshape(L_CMP // 2, P, CMP_HID).transpose(1, 0, 2) for n in "kv"]),
        "w2k": np.tile(x["w_cmp_k2_2"][0].reshape(2, P, HD).transpose(1, 0, 2), (1, 1, 2)),
        "w2v": x["w_cmp_v2_2"][0].reshape(2, P, HD).transpose(1, 0, 2), "rel_bias_t": x["rel_bias_2"].T,
        "mix_post": x["norm_mix_post_2"][0], "ffn_post": x["norm_ffn_post_2"][0],
        "g_up_pad": g_up, "b_gates": np.concatenate([b[2], b[5]]).reshape(4, SEQ),
    }


def kernel(**inputs):
    import concourse.bacc as bacc
    from concourse.bass_utils import run_bass_kernel_spmd

    nc = bacc.Bacc("TRN2", target_bir_lowering=False, num_devices=1)
    arrays = {f"in_{n}": np.ascontiguousarray(a) for n, a in lay_out(inputs).items()}
    src = {n[3:]: nc.dram_tensor(n, a.shape, mybir.dt.from_np(a.dtype), kind="ExternalInput").ap()
           for n, a in arrays.items()}
    out = nc.dram_tensor("out", (1, SEQ, DM), F32, kind="ExternalOutput").ap()
    build(nc, src, out)
    return run_bass_kernel_spmd(nc, [arrays], core_ids=[0]).results[0]["out"]
```
